# Optimizing a Trainium2 kernel written in Bass

```python
import math
import jax, jax.numpy as jnp
from jax import lax
import numpy as np

D_MODEL = 1024
BATCH = 1
SEQ = 1024
DEPTH = 2
DEC_BATCH = 8
DEC_SEQ = 1
PAST_LEN = 2048
PAGE_SIZE = 128

N_EVEN = (DEPTH + 1) // 2
N_ODD = DEPTH // 2
HA = 4
DA = D_MODEL // (4 * HA)
DVA = 2 * DA
HB = 4
DKB = D_MODEL // (2 * HB)
DVB = D_MODEL // (2 * HB)
C_QKV_B = 2 * HB * DKB + HB * DVB
GDN_CONV = 4
GDN_CHUNK = 64
D_CONV = D_MODEL
CONV_W = 31
D_FF = -(-8 * D_MODEL // (3 * 256)) * 256
NUM_BUCKETS = 32
MAX_DISTANCE = 128
QBLOCK = 128
RMS_EPS = 1e-6
LN_EPS = 1e-5
IN_SIZES = (HA * 2 * DA, HA * 2 * DA, HA * DVA, C_QKV_B, HB * DVB, HB, HB)
IN_COLS = sum(IN_SIZES)
IN_SPLITS = tuple(int(s) for s in np.cumsum(IN_SIZES)[:-1])
MIX_OUT = HA * DVA + HB * DVB

kernel_name = 'hybrid_diffattn_gdn_conformer_step'

def rms_norm(x, w, eps=RMS_EPS):
    xf = x.astype(jnp.float32)
    y = xf * lax.rsqrt(jnp.mean(xf * xf, axis=-1, keepdims=True) + eps)
    return (y * w.astype(jnp.float32)).astype(x.dtype)

def layer_norm(x, g, b, eps=LN_EPS):
    xf = x.astype(jnp.float32)
    mu = jnp.mean(xf, axis=-1, keepdims=True)
    xc = xf - mu
    var = jnp.mean(xc * xc, axis=-1, keepdims=True)
    y = xc * lax.rsqrt(var + eps) * g.astype(jnp.float32) + b.astype(jnp.float32)
    return y.astype(x.dtype)

def l2_norm(x):
    xf = x.astype(jnp.float32)
    return xf * lax.rsqrt(jnp.sum(xf * xf, axis=-1, keepdims=True) + 1e-6)

def swiglu(x, wg, wu, wd):
    return (jax.nn.silu(x @ wg) * (x @ wu)) @ wd

def causal_dwconv(x_ext, w):
    return lax.conv_general_dilated(
        x_ext, w[:, None, :], window_strides=(1,), padding='VALID',
        dimension_numbers=('NWC', 'WIO', 'NWC'), feature_group_count=x_ext.shape[-1])

def t5_bucket(q_pos, k_pos):
    n = jnp.maximum(q_pos[:, None] - k_pos[None, :], 0)
    max_exact = NUM_BUCKETS // 2
    nf = jnp.maximum(n, 1).astype(jnp.float32)
    large = max_exact + (jnp.log(nf / max_exact) / math.log(MAX_DISTANCE / max_exact)
                         * (NUM_BUCKETS - max_exact)).astype(jnp.int32)
    large = jnp.minimum(large, NUM_BUCKETS - 1)
    return jnp.where(n < max_exact, n, large)

def diff_attn_core(q, k, v, q_pos, k_pos, lam, rel_bias):
    bias = jnp.transpose(rel_bias[t5_bucket(q_pos, k_pos)], (2, 0, 1)).astype(jnp.float32)
    s = jnp.einsum('bqhmd,bkhmd->bhmqk', q, k, preferred_element_type=jnp.float32) * DA ** -0.5
    s = s + bias[None, :, None]
    s = jnp.where(k_pos[None, :] <= q_pos[:, None], s, -jnp.inf)
    p = jax.nn.softmax(s, axis=-1)
    a = p[:, :, 0] - lam * p[:, :, 1]
    return jnp.einsum('bhqk,bkhe->bqhe', a.astype(v.dtype), v)

def diff_attn_prompt(q, k, v, lam, rel_bias):
    B, T = q.shape[:2]
    nb = T // QBLOCK
    qb = jnp.moveaxis(q.reshape(B, nb, QBLOCK, HA, 2, DA), 1, 0)
    k_pos = jnp.arange(T)

    def block(args):
        q_blk, i = args
        q_pos = i * QBLOCK + jnp.arange(QBLOCK)
        return diff_attn_core(q_blk, k, v, q_pos, k_pos, lam, rel_bias)

    o = lax.map(block, (qb, jnp.arange(nb)))
    return jnp.moveaxis(o, 0, 1).reshape(B, T, HA, DVA)

def diff_attn_sample(q, k_new, v_new, k_pool, v_pool, page_table, lam, rel_bias):
    db, s = q.shape[:2]
    past = page_table.shape[1] * k_pool.shape[1]
    k_past = k_pool[page_table].reshape(db, past, HA, 2, DA)
    v_past = v_pool[page_table].reshape(db, past, HA, DVA)
    k = jnp.concatenate([k_past, k_new.astype(k_past.dtype)], axis=1)
    v = jnp.concatenate([v_past, v_new.astype(v_past.dtype)], axis=1)
    q_pos = past + jnp.arange(s)
    k_pos = jnp.arange(past + s)
    return diff_attn_core(q, k, v, q_pos, k_pos, lam, rel_bias)

def gated_delta_chunked(q, k, v, beta, g, s0):
    f32 = jnp.float32
    B, T, H, DK = q.shape
    DV = v.shape[-1]
    C = min(GDN_CHUNK, T)
    pad = (-T) % C
    n = (T + pad) // C

    def prep(x):
        x = jnp.pad(x.astype(f32), [(0, 0), (0, pad)] + [(0, 0)] * (x.ndim - 2))
        x = x.reshape((B, n, C) + x.shape[2:])
        return jnp.moveaxis(jnp.moveaxis(x, 3, 2), 1, 0)

    q = prep(q) * DK ** -0.5
    k, v, beta, g = prep(k), prep(v), prep(beta), prep(g)
    g = jnp.cumsum(g, axis=-1)
    idx = jnp.arange(C)
    incl = idx[:, None] >= idx[None, :]
    strict = idx[:, None] > idx[None, :]
    diff = g[..., :, None] - g[..., None, :]
    decay = jnp.where(incl, jnp.exp(jnp.where(incl, diff, 0.0)), 0.0)
    k_beta = k * beta[..., None]
    v_beta = v * beta[..., None]
    L = jnp.where(strict, jnp.einsum('...id,...jd->...ij', k_beta, k) * decay, 0.0)
    eye = jnp.eye(C, dtype=f32)
    t_inv = lax.linalg.triangular_solve(eye + L, jnp.broadcast_to(eye, L.shape),
                                        left_side=True, lower=True, unit_diagonal=True)
    u = t_inv @ v_beta
    w = t_inv @ (k_beta * jnp.exp(g)[..., None])
    attn = jnp.einsum('...id,...jd->...ij', q, k) * decay
    g_last = g[..., -1]
    k_dec = k * jnp.exp(g_last[..., None] - g)[..., None]
    q_dec = q * jnp.exp(g)[..., None]

    def step(S, xs):
        u_c, w_c, attn_c, q_c, k_c, gl = xs
        v_new = u_c - w_c @ S
        o = q_c @ S + attn_c @ v_new
        S = S * jnp.exp(gl)[..., None, None] + jnp.einsum('bhck,bhcv->bhkv', k_c, v_new)
        return S, o

    S, o = lax.scan(step, s0.astype(f32), (u, w, attn, q_dec, k_dec, g_last))
    o = jnp.moveaxis(jnp.moveaxis(o, 0, 1), 2, 3).reshape(B, n * C, H, DV)[:, :T]
    return o, S

def gated_deltanet(qkv, beta_in, a_in, z, conv_state, s0, conv_w, a_log, dt_bias, norm_w):
    B, T = qkv.shape[:2]
    x_ext = jnp.concatenate([conv_state.astype(qkv.dtype), qkv], axis=1)
    conv_new = x_ext[:, -(GDN_CONV - 1):]
    h = jax.nn.silu(causal_dwconv(x_ext, conv_w))
    q, k, v = jnp.split(h, [HB * DKB, 2 * HB * DKB], axis=-1)
    q = l2_norm(q.reshape(B, T, HB, DKB))
    k = l2_norm(k.reshape(B, T, HB, DKB))
    v = v.reshape(B, T, HB, DVB)
    beta = jax.nn.sigmoid(beta_in.astype(jnp.float32))
    g = -jnp.exp(a_log.astype(jnp.float32)) * jax.nn.softplus(
        a_in.astype(jnp.float32) + dt_bias.astype(jnp.float32))
    o, s_new = gated_delta_chunked(q, k, v, beta, g, s0)
    o = rms_norm(o, norm_w) * jax.nn.silu(z.reshape(B, T, HB, DVB).astype(jnp.float32))
    return o.reshape(B, T, HB * DVB).astype(qkv.dtype), conv_new, s_new.astype(qkv.dtype)

def conformer_conv(xn, buf, w_pw1, b_pw1, w_dw, b_dw, ln_g, ln_b, w_pw2, b_pw2):
    a, gate = jnp.split(xn @ w_pw1 + b_pw1, 2, axis=-1)
    h = a * jax.nn.sigmoid(gate)
    x_ext = jnp.concatenate([buf.astype(h.dtype), h], axis=1)
    buf_new = x_ext[:, -(CONV_W - 1):]
    h = causal_dwconv(x_ext, w_dw) + b_dw
    h = jax.nn.silu(layer_norm(h, ln_g, ln_b))
    return h @ w_pw2 + b_pw2, buf_new

def setup_inputs(seed: int = 0) -> dict:
    key = jax.random.key(seed)
    keys = iter(jax.random.split(key, 48))
    f32 = jnp.float32

    def normal(shape, scale):
        return jax.random.normal(next(keys), shape, f32) * scale

    def gain(shape):
        return 1.0 + normal(shape, 0.05)

    n_pages = PAST_LEN // PAGE_SIZE
    n_used = DEC_BATCH * n_pages
    n_pool = n_used + max(1, n_used // 4)
    page_table = jax.random.permutation(next(keys), n_pool)[:n_used].reshape(
        DEC_BATCH, n_pages).astype(jnp.int32)
    dt = jnp.exp(jax.random.uniform(next(keys), (N_EVEN, HB), f32, math.log(1e-3), math.log(1e-1)))
    a_log = jnp.log(jax.random.uniform(next(keys), (N_EVEN, HB), f32, 1.0, 16.0))
    return {
        'x_prompt': normal((BATCH, SEQ, D_MODEL), 1.0),
        'x_sample': normal((DEC_BATCH, DEC_SEQ, D_MODEL), 1.0),
        'cache_attn_k': normal((N_EVEN, n_pool, PAGE_SIZE, HA, 2 * DA), 1.0),
        'cache_attn_v': normal((N_EVEN, n_pool, PAGE_SIZE, HA, DVA), 1.0),
        'page_table': page_table,
        'state_gdn_conv': normal((N_EVEN, DEC_BATCH, GDN_CONV - 1, C_QKV_B), 1.0),
        'state_gdn_s': normal((N_EVEN, DEC_BATCH, HB, DKB, DVB), 0.3),
        'state_conv_buf': normal((N_ODD, DEC_BATCH, CONV_W - 1, D_CONV), 0.5),
        'norm_mix': gain((DEPTH, D_MODEL)),
        'norm_ffn': gain((DEPTH, D_MODEL)),
        'norm_final': gain((D_MODEL,)),
        'w_in': normal((N_EVEN, D_MODEL, IN_COLS), D_MODEL ** -0.5),
        'w_out': normal((N_EVEN, MIX_OUT, D_MODEL), MIX_OUT ** -0.5),
        'gdn_conv_w': normal((N_EVEN, GDN_CONV, C_QKV_B), GDN_CONV ** -0.5),
        'gdn_A_log': a_log,
        'gdn_dt_bias': dt + jnp.log(-jnp.expm1(-dt)),
        'gdn_norm_w': gain((N_EVEN, DVB)),
        'lam_q1': normal((N_EVEN, DA), 0.1),
        'lam_k1': normal((N_EVEN, DA), 0.1),
        'lam_q2': normal((N_EVEN, DA), 0.1),
        'lam_k2': normal((N_EVEN, DA), 0.1),
        'diff_subln_w': gain((N_EVEN, DVA)),
        'rel_bias': normal((NUM_BUCKETS, HA), 0.5),
        'conv_w_pw1': normal((N_ODD, D_MODEL, 2 * D_CONV), D_MODEL ** -0.5),
        'conv_b_pw1': normal((N_ODD, 2 * D_CONV), 0.02),
        'conv_w_dw': normal((N_ODD, CONV_W, D_CONV), CONV_W ** -0.5),
        'conv_b_dw': normal((N_ODD, D_CONV), 0.02),
        'conv_ln_g': gain((N_ODD, D_CONV)),
        'conv_ln_b': normal((N_ODD, D_CONV), 0.02),
        'conv_w_pw2': normal((N_ODD, D_CONV, D_MODEL), D_CONV ** -0.5),
        'conv_b_pw2': normal((N_ODD, D_MODEL), 0.02),
        'ffn_w_gate': normal((DEPTH, D_MODEL, D_FF), D_MODEL ** -0.5),
        'ffn_w_up': normal((DEPTH, D_MODEL, D_FF), D_MODEL ** -0.5),
        'ffn_w_down': normal((DEPTH, D_FF, D_MODEL), D_FF ** -0.5),
    }

def reference(x_prompt, x_sample, cache_attn_k, cache_attn_v, page_table,
              state_gdn_conv, state_gdn_s, state_conv_buf,
              norm_mix, norm_ffn, norm_final, w_in, w_out,
              gdn_conv_w, gdn_A_log, gdn_dt_bias, gdn_norm_w,
              lam_q1, lam_k1, lam_q2, lam_k2, diff_subln_w, rel_bias,
              conv_w_pw1, conv_b_pw1, conv_w_dw, conv_b_dw, conv_ln_g, conv_ln_b,
              conv_w_pw2, conv_b_pw2, ffn_w_gate, ffn_w_up, ffn_w_down):
    f32 = jnp.float32
    xp, xs = x_prompt, x_sample
    k_p, v_p, k_s, v_s = [], [], [], []
    gc_p, gc_s, gs_p, gs_s = [], [], [], []
    cb_p, cb_s = [], []
    for layer in range(DEPTH):
        if layer % 2 == 0:
            e = layer // 2
            lam_init = 0.8 - 0.6 * math.exp(-0.3 * layer)
            lam = (jnp.exp(jnp.sum(lam_q1[e].astype(f32) * lam_k1[e].astype(f32)))
                   - jnp.exp(jnp.sum(lam_q2[e].astype(f32) * lam_k2[e].astype(f32))) + lam_init)

            def mix_even(x, attend, conv_state, s0):
                B, T, _ = x.shape
                h = rms_norm(x, norm_mix[layer]) @ w_in[e]
                qa, ka, va, qkv_b, z_b, beta_b, a_b = jnp.split(h, IN_SPLITS, axis=-1)
                ka = ka.reshape(B, T, HA, 2, DA)
                va = va.reshape(B, T, HA, DVA)
                oa = attend(qa.reshape(B, T, HA, 2, DA), ka, va)
                oa = (rms_norm(oa, diff_subln_w[e], LN_EPS) * (1.0 - lam_init)).reshape(B, T, HA * DVA)
                ob, conv_new, s_new = gated_deltanet(qkv_b, beta_b, a_b, z_b, conv_state, s0,
                                                     gdn_conv_w[e], gdn_A_log[e], gdn_dt_bias[e],
                                                     gdn_norm_w[e])
                y = jnp.concatenate([oa.astype(x.dtype), ob], axis=-1) @ w_out[e]
                return x + y, ka.reshape(B, T, HA, 2 * DA), va, conv_new, s_new

            bp = xp.shape[0]
            xp, kr, vr, cn, sn = mix_even(
                xp, lambda q, k, v: diff_attn_prompt(q, k, v, lam, rel_bias),
                jnp.zeros((bp, GDN_CONV - 1, C_QKV_B), xp.dtype),
                jnp.zeros((bp, HB, DKB, DVB), f32))
            k_p.append(kr); v_p.append(vr); gc_p.append(cn); gs_p.append(sn)
            xs, kr, vr, cn, sn = mix_even(
                xs, lambda q, k, v: diff_attn_sample(q, k, v, cache_attn_k[e], cache_attn_v[e],
                                                     page_table, lam, rel_bias),
                state_gdn_conv[e], state_gdn_s[e])
            k_s.append(kr); v_s.append(vr); gc_s.append(cn); gs_s.append(sn)
        else:
            c = layer // 2

            def mix_odd(x, buf):
                y, buf_new = conformer_conv(rms_norm(x, norm_mix[layer]), buf,
                                            conv_w_pw1[c], conv_b_pw1[c], conv_w_dw[c], conv_b_dw[c],
                                            conv_ln_g[c], conv_ln_b[c], conv_w_pw2[c], conv_b_pw2[c])
                return x + y, buf_new

            xp, bn = mix_odd(xp, jnp.zeros((xp.shape[0], CONV_W - 1, D_CONV), xp.dtype))
            cb_p.append(bn)
            xs, bn = mix_odd(xs, state_conv_buf[c])
            cb_s.append(bn)
        xp = xp + swiglu(rms_norm(xp, norm_ffn[layer]), ffn_w_gate[layer], ffn_w_up[layer], ffn_w_down[layer])
        xs = xs + swiglu(rms_norm(xs, norm_ffn[layer]), ffn_w_gate[layer], ffn_w_up[layer], ffn_w_down[layer])
    y_prompt = rms_norm(xp, norm_final)
    y_sample = rms_norm(xs, norm_final)
    new_k_prompt = jnp.stack(k_p)
    new_v_prompt = jnp.stack(v_p)
    new_k_sample = jnp.stack(k_s)
    new_v_sample = jnp.stack(v_s)
    new_gdn_conv_prompt = jnp.stack(gc_p)
    new_gdn_conv_sample = jnp.stack(gc_s)
    new_gdn_s_prompt = jnp.stack(gs_p)
    new_gdn_s_sample = jnp.stack(gs_s)
    new_conv_buf_prompt = jnp.stack(cb_p)
    new_conv_buf_sample = jnp.stack(cb_s)
    return (y_prompt, y_sample, new_k_prompt, new_v_prompt, new_k_sample, new_v_sample,
            new_gdn_conv_prompt, new_gdn_conv_sample, new_gdn_s_prompt, new_gdn_s_sample,
            new_conv_buf_prompt, new_conv_buf_sample)


_drawn_inputs = setup_inputs


def setup_inputs(seed=0):
    import zlib

    import numpy as np

    out = dict(_drawn_inputs(seed))
    spreads = {}
    factors = {'lam_k1': 3.903,
     'lam_q2': 4.351,
     'lam_k2': 6.445,
     'conv_b_pw1': 2.677,
     'conv_b_dw': 3.207,
     'conv_ln_b': 6.053,
     'conv_b_pw2': 3.86}
    for name, (base, spread) in spreads.items():
        noise = np.random.default_rng([zlib.crc32(name.encode()), seed]).standard_normal(out[name].shape)
        drawn = base * np.exp(spread * noise) if base else spread * noise
        out[name] = __import__('jax').numpy.asarray(drawn.astype(out[name].dtype))
    for name, factor in factors.items():
        out[name] = (out[name] * factor).astype(out[name].dtype)
    return out
```

```python
import math
from contextlib import ExitStack

import numpy as np

import concourse.bass as bass
from concourse import mybir

F32, I32, U8, F32R = mybir.dt.float32, mybir.dt.int32, mybir.dt.uint8, mybir.dt.float32r
ALU = mybir.AluOpType
ACT = mybir.ActivationFunctionType
AX = mybir.AxisListType
ds = bass.ds

P = 128
D = 1024
KD = D // P
T = 1024
NB = T // P
B = 8
TT = T + B
NCH = 3
CH = TT // NCH
H = 4
DA = 64
FF = 2816
KF = FF // P
SLAB = KF // 2
CW = 31
GW = 4
CQ = 1536
PAST = 2048
PG = 16
NBUCKET, MAXD = 32, 128
NEG = -1e30
LN_EPS = 1e-5
LAM0 = 0.8 - 0.6 * math.exp(-0.3 * 0)
LEVELS = 7
GL = T + CW - 1 + B

V_MIX0, V_MIX1, V_FFN0, V_FFN1, V_FIN, V_BA, V_BG, V_BDW, V_LG, V_LB, V_BPW2, V_WDW = range(12)
NV = V_WDW + CW


def bucket(n):
    exact = NBUCKET // 2
    if n < exact:
        return n
    return min(exact + int(math.log(n / exact) / math.log(MAXD / exact) * (NBUCKET - exact) + 1e-9), NBUCKET - 1)


def shape_constants():
    i = np.arange(P)
    ident = np.eye(P, dtype=np.float32)
    triu = (i[:, None] <= i[None, :]).astype(np.float32)
    causal = np.where(i[None, :] >= i[:, None], 0.0, NEG).astype(np.float32)
    merge = np.zeros((P, 2, LEVELS, P), np.int32)
    for lv in range(LEVELS):
        s = 1 << lv
        m = (i[:, None] // (2 * s) == i[None, :] // (2 * s)) & (i[:, None] // s % 2 == 1) & (i[None, :] // s % 2 == 0)
        merge[:, 0, lv] = m
        merge[:, 1, lv] = m.T
    hot = np.zeros((NBUCKET, 384), np.float32)
    for m in range(256):
        hot[bucket(255 - m), m] = 1
    hots = np.zeros((NBUCKET, 3, P), np.float32)
    for r in range(P):
        hots[bucket(P - r), 0, r] = 1
        hots[NBUCKET - 1, 1, r] = 1
        hots[0, 2, r] = 1
    halves = np.zeros((P, 2, P), np.float32)
    halves[:DA, 0] = 1
    halves[DA:, 1] = 1
    return dict(c_ident=ident, c_triu=triu, c_causal=causal, c_merge=merge.reshape(P, -1), c_hot=hot,
                c_hots=hots.reshape(NBUCKET, -1), c_halves=halves.reshape(P, -1))


class Chain:

    def __init__(self, eng, sem):
        self.eng, self.sem, self.n, self.i, self.per = eng, sem, 0, None, 0

    def __call__(self, ins):
        ins.then_inc(self.sem, 1)
        self.n += 1
        self.eng.wait_ge(self.sem, self.n if self.i is None else self.i * self.per + self.n)

    def enter(self, i, per_round):
        self.i, self.per, self.start = i, per_round, self.n

    def leave(self, rounds):
        assert self.n - self.start == self.per, (self.n - self.start, self.per)
        self.n = self.start + rounds * self.per
        self.i = None


class Marks:

    def __init__(self, sem, **steps):
        self.sem, self.steps = sem, steps

    def wait(self, eng, name, n=1):
        before = list(self.steps)[:list(self.steps).index(name)]
        eng.wait_ge(self.sem, sum(self.steps[x] for x in before) + n)


class Gemm:

    def __init__(self, sems, rounds, last=(2, 5, 8, 11)):
        self.full, self.free = sems["full"], sems["free"]
        self.last = last
        self.per, self.rounds = last[3] + 1, rounds
        self.jobs0 = sems["jobs"]
        sems["jobs"] += self.per * rounds

    def grant(self, eng, parities):
        if self.jobs0 == 0:
            for p in parities:
                eng.sem_inc(self.free[p], 3)

    def wait_bank(self, pe, i, j):
        pe.wait_ge(self.free[j % 2], i * (self.per // 2) + (self.jobs0 // 2 + j // 2 + 1))

    def wait_full(self, eng, i, j):
        eng.wait_ge(self.full, i * self.per + (self.jobs0 + j + 1))

    def wait_read(self, eng, i, j):
        self.wait_pair(eng, i, j, j % 2)

    def wait_pair(self, eng, i, j, parity):
        eng.wait_ge(self.free[parity], i * (self.per // 2) + (self.jobs0 // 2 + j // 2 + 4))

    def wait_all_read(self, eng):
        for p in (0, 1):
            eng.wait_ge(self.free[p], 3 + (self.jobs0 + self.rounds * self.per) // 2)


def build(nc, a, o):
    with ExitStack() as ctx:
        def sb(name, shape, dt=F32):
            return ctx.enter_context(nc.sbuf_tensor(name, shape, dt))

        def sem(name):
            return ctx.enter_context(nc.semaphore(name))

        bank = ctx.enter_context(nc.psum_tensor("bank", [P, 8, 512], F32))
        place = {"res_a": -(-nc.sbuf_base // 32) * 32}
        res_a = sb("res_a", [P, KD, TT])
        res_b = sb("res_b", [P, KD, TT])
        place["big"] = -(-nc.sbuf_base // 32) * 32
        big = sb("big", [P, KF * TT])
        place["wring"] = -(-nc.sbuf_base // 32) * 32
        wring = sb("wring", [P, 4, SLAB, P])

        def rounded(name, where, off, shape):
            return nc.alloc_sbuf_tensor_at(name, shape, F32R, offset=place[where] + 4 * off)
        tmp = sb("tmp", [P, 4, CH])
        rstd = sb("rstd", [P, NCH, CH])
        ident = sb("ident", [P, P])
        ones = sb("ones", [P, P])
        triu = sb("triu", [P, P])
        causal = sb("causal", [P, P])
        merge = sb("merge", [P, 2, LEVELS, P], U8)
        halves = sb("halves", [P, 2, P])
        vec = sb("vec", [P, KD, NV])
        gcw = sb("gcw", [P, 12, GW])
        gst = sb("gst", [P, 12, B, GW - 1])
        sbias = sb("sbias", [P, 3, H])
        gate0 = sb("gate0", [P, 2, H])
        hw = sb("hw", [P, 2])
        lam = sb("lam", [P, 8])
        pages = sb("pages", [1, P], I32)
        aw = sb("aw", [P, B, PG, H])
        gnew = sb("gnew", [P, 12, GW - 1 + B])
        wba = sb("wba", [P, KD, 2 * H])
        sq = sb("sq", [P, 12, B])
        probs = sb("probs", [P, B, PG, 2 * H])
        state = sb("state", [P, H, P])
        small = sb("small", [P, 512])
        park = nc.dram_tensor("park", (P, KD * TT), F32, kind="Internal")
        brow = nc.dram_tensor("brow", (P, H, 384), F32, kind="Internal")

        def tiles(n0, n):
            return big[:, n0 * TT:(n0 + n) * TT].rearrange("p (n t) -> p n t", n=n)

        def flat(off, *shape, parts=P):
            n = int(np.prod(shape))
            v = big[0:parts, off:off + n]
            names = "abc"[:len(shape)]
            if len(shape) == 1:
                return v
            return v.rearrange(f"p ({' '.join(names)}) -> p {' '.join(names)}", **{k: s for k, s in zip(names[1:], shape[1:])})

        def vcol(v, k):
            return vec[:, k, v:v + 1]

        xrows = flat(8192, NB, D)
        vrows = flat(0, D, parts=NV)
        grows = flat(1024, CQ, parts=GW)
        srows = flat(2560, CQ, parts=B * (GW - 1))
        hot = flat(4096, 384, parts=NBUCKET)
        hots = flat(4480, 3, P, parts=NBUCKET)
        xsrows = flat(4864, D, parts=B)
        rel = flat(5888, H, parts=NBUCKET)
        merge_words = flat(16384, 2 * LEVELS * P).bitcast(I32)
        lamv = flat(5892, 4, parts=DA)
        lamp = flat(5896, 2, parts=DA)
        bsb = small[0:H, 0:384]

        x_in = [sem("x_in0"), sem("x_in1")]
        const_in = sem("const_in")
        ones_set = sem("ones_set")
        xt_full = sem("xt_full")
        xt_act = sem("xt_act")
        xt_dve = sem("xt_dve")
        set_mm = sem("set_mm")
        lam_prod = sem("lam_prod")
        set_dve = sem("set_dve")
        lam_exp = sem("lam_exp")
        bias_io = sem("bias_io")
        dve_step, act_step, pool_step = sem("dve_step"), sem("act_step"), sem("pool_step")

        w_in = [sem(f"w_in{s}") for s in range(4)]
        w_rounds = [0, 0]

        n_act, n_dve = sem("n_act"), sem("n_dve")
        n_mm = sem("n_mm")
        n_log = sem("n_log")
        n_rstd = sem("n_rstd")
        n_out = sem("n_out")

        def chunk(c):
            return slice(c * CH, (c + 1) * CH)

        def norm_pe(pe, nn):
            for c in range(NCH):
                q = 3 * nn + c
                if q >= 2:
                    pe.wait_ge(n_log, q - 1)
                for k in range(KD):
                    pe.wait_ge((n_act, n_dve)[k % 2], 4 * q + k // 2 + 1)
                    pe.matmul(bank[:, 6 + q % 2, 0:CH], ones[:, :], tmp[:, k % 4, :],
                              start=(k == 0), stop=(k == KD - 1)).then_inc(n_mm, 1)

        def norm_squares(eng, nn, c, x, par):
            for k in range(par, KD, 2):
                m = KD * (3 * nn + c) + k
                if m >= 4:
                    eng.wait_ge(n_mm, m - 3)
                if par == 0:
                    eng.activation(tmp[:, k % 4, :], x[:, k, chunk(c)], ACT.Square).then_inc(n_act, 1)
                else:
                    eng.tensor_tensor(tmp[:, k % 4, :], x[:, k, chunk(c)], x[:, k, chunk(c)], ALU.mult).then_inc(n_dve, 1)

        def norm_act(act, nn, x, eps=1e-6, copy=None):
            for c in range(NCH + (2 if copy else 1)):
                if c < NCH:
                    norm_squares(act, nn, c, x, 0)
                if 0 < c <= NCH:
                    q = 3 * nn + c - 1
                    act.wait_ge(n_mm, KD * (q + 1))
                    act.activation(rstd[:, c - 1, :], bank[:, 6 + q % 2, 0:CH], ACT.Ln, scale=1.0 / D, bias=eps).then_inc(n_log, 1)
                    act.wait_ge(n_log, q + 1)
                    act.activation(rstd[:, c - 1, :], rstd[:, c - 1, :], ACT.Exp, scale=-0.5).then_inc(n_rstd, 1)
                if copy and c >= 2:
                    copy(c - 2)

        def norm_dve(dve, nn, x, out, wv):
            for c in range(NCH + 1):
                if c < NCH:
                    norm_squares(dve, nn, c, x, 1)
                if c:
                    norm_apply(dve, nn, c - 1, x, out, wv)

        def norm_apply(dve, nn, c, x, out, wv):
            dve.wait_ge(n_rstd, 3 * nn + c + 1)
            for k in range(KD):
                dve.scalar_tensor_tensor(out[:, k, chunk(c)], x[:, k, chunk(c)], vcol(wv, k), rstd[:, c, :],
                                         ALU.mult, ALU.mult).then_inc(n_out, 1)

        def load_slab(sp, g, i, s, source, before):
            if not isinstance(i, int):
                g.wait_full(sp, i, g.last[s] - g.per)
            elif i:
                g.wait_full(sp, i - 1, g.last[s])
            elif before is not None:
                before.wait_full(sp, before.rounds - 1, before.last[s])
            w = source(i, s)
            sp.dma_start(wring[:, s, 0:w.shape[1], :], w).then_inc(w_in[s], 16)

        def stream(sp, g, source, before):
            for s in range(4):
                load_slab(sp, g, 0, s, source, before)
            with sp.Fori(1, g.rounds) as i:
                for s in range(4):
                    load_slab(sp, g, i, s, source, before)

        def job(pe, g, i, j, slots, rhs):
            g.wait_bank(pe, i, j)
            total, k = sum(n for _, n in slots), 0
            for s, n in slots:
                for kk in range(n):
                    mm = pe.matmul(bank[:, j % 6, 0:CH], wring[:, s, kk, :], rhs(k, j), start=(k == 0), stop=(k == total - 1))
                    k += 1
            mm.then_inc(g.full, 1)
            return mm

        def wait_slab(pe, i, s):
            pe.wait_ge(w_in[s], 16 * (i + w_rounds[1] + 1))

        def project_pe(pe, g, x):
            with pe.Fori(0, g.rounds) as i:
                for s in range(4):
                    wait_slab(pe, i, s)
                    for c in range(NCH):
                        job(pe, g, i, NCH * s + c, [(s, KD)], lambda k, j: x[:, k, chunk(j % NCH)])
            w_rounds[1] += g.rounds

        def cols(w, n):
            return w.rearrange("(k p) n -> p k n", p=P)[:, :, ds(n * P, P)]

        g_sems = {"full": sem("job_full"), "free": [sem("bank_free_even"), sem("bank_free_odd")], "jobs": 0}
        g_att = Gemm(g_sems, 3)

        w_in0 = a["w_in"].rearrange("e k n -> (e k) n")
        blk = ctx.enter_context(nc.Block())

        def setup_sp(sp):
            xp = a["x_prompt"].rearrange("o (n p) d -> p (o n) d", p=P)
            sp.dma_start(ident[:], a["c_ident"]).then_inc(const_in, 16)
            for n in range(NB):
                sp.dma_start(xrows[:, n, :], xp[:, n, :]).then_inc(x_in[n // 4], 16)
            rows = [(a["norm_mix"], V_MIX0, 2), (a["norm_ffn"], V_FFN0, 2), (a["norm_final"].rearrange("(o d) -> o d", o=1), V_FIN, 1),
                    (a["conv_b_pw1"].rearrange("o (g d) -> (o g) d", g=2), V_BA, 2), (a["conv_b_dw"], V_BDW, 1),
                    (a["conv_ln_g"], V_LG, 1), (a["conv_ln_b"], V_LB, 1), (a["conv_b_pw2"], V_BPW2, 1),
                    (a["conv_w_dw"].rearrange("o w d -> (o w) d"), V_WDW, CW)]
            n = 1
            for src, r, m in rows:
                sp.dma_start(vrows[r:r + m, :], src).then_inc(const_in, 16)
                n += 1
            lams = [a[k].rearrange("o (d u) -> (o d) u", u=1) for k in ("lam_q1", "lam_q2", "lam_k1", "lam_k2")]
            rest = [(xsrows, a["x_sample"].rearrange("b o d -> (b o) d")), (grows, a["gdn_conv_w"].rearrange("o w d -> (o w) d")),
                    (srows, a["state_gdn_conv"].rearrange("o b w d -> (o b w) d")), (triu[:], a["c_triu"]), (causal[:], a["c_causal"]),
                    (merge_words, a["c_merge"]), (halves[:].rearrange("p a m -> p (a m)"), a["c_halves"]),
                    (hot, a["c_hot"]), (hots.rearrange("p a m -> p (a m)"), a["c_hots"]), (rel, a["rel_bias"]),
                    (pages[:], a["page_table"].rearrange("(o b) g -> o (b g)", o=1)),
                    (gate0[:, 0, :], a["gdn_A_log"].broadcast_to([P, H])), (gate0[:, 1, :], a["gdn_dt_bias"].broadcast_to([P, H])),
                    (hw[:, 0:1], a["diff_subln_w"].rearrange("o (d u) -> (o d) u", u=1)),
                    (hw[:, 1:2], a["gdn_norm_w"].rearrange("o (d u) -> (o d) u", u=1))]
            rest += [(lamv[:, q:q + 1], lams[q]) for q in range(4)]
            for dst, src in rest:
                sp.dma_start(dst, src).then_inc(const_in, 16)
                n += 1
            return 16 * n
        CONSTS = 16 * (1 + 9 + 19)

        def setup_pe(pe):
            pe.wait_ge(const_in, CONSTS)
            for n in range(NB):
                pe.wait_ge(x_in[n // 4], 64)
                if n >= 2:
                    pe.wait_ge(xt_act, n - 1)
                    pe.wait_ge(xt_dve, n - 1)
                for k in range(KD):
                    mm = pe.transpose(bank[:, 2 * (n % 2) + k // 4, k % 4 * P:(k % 4 + 1) * P], xrows[:, n, k * P:(k + 1) * P], ident[:, :])
                mm.then_inc(xt_full, 1)
            for k in range(KD):
                pe.transpose(bank[:, 4, k * NV:(k + 1) * NV], vrows[:, k * P:(k + 1) * P], ident[0:NV, 0:NV])
            for k in range(12):
                pe.transpose(bank[:, 5, k * GW:(k + 1) * GW], grows[:, k * P:(k + 1) * P], ident[0:GW, 0:GW])
            for k in range(KD):
                pe.transpose(bank[:, 5, 96 + k * B:96 + (k + 1) * B], xsrows[:, k * P:(k + 1) * P], ident[0:B, 0:B])
            R = B * (GW - 1)
            for k in range(12):
                mm = pe.transpose(bank[:, 6, k * R:(k + 1) * R], srows[:, k * P:(k + 1) * P], ident[0:R, 0:R])
            mm.then_inc(set_mm, 1)
            pe.wait_ge(xt_act, NB)
            for r in range(3):
                pe.matmul(bank[:, 0, 192 + r * H:192 + (r + 1) * H], hots[:, r, :], rel, start=True, stop=True)
            pe.wait_ge(lam_prod, 1)
            pe.wait_ge(ones_set, 1)
            pe.matmul(bank[:, 0, 256:258], ones[0:DA, :], lamp, start=True, stop=True)
            pe.matmul(bank[0:H, 7, 0:384], rel, hot, start=True, stop=True).then_inc(set_mm, 1)

        def setup_act(act):
            for n in range(NB):
                act.wait_ge(xt_full, n + 1)
                act.activation(res_a[:, 0:4, n * P:(n + 1) * P], bank[:, 2 * (n % 2), :].rearrange("p (k t) -> p k t", k=4), ACT.Copy).then_inc(xt_act, 1)
            act.wait_ge(set_dve, 1)
            act.activation(lam[:, 2:4], lam[:, 0:2], ACT.Exp).then_inc(lam_exp, 1)

        def setup_dve(dve, step):
            dve.memset(ones[:], 1.0).then_inc(ones_set, 1)
            dve.wait_ge(const_in, CONSTS)
            dve.tensor_tensor(lamp, lamv[:, 0:2], lamv[:, 2:4], ALU.mult).then_inc(lam_prod, 1)
            for n in range(NB):
                dve.wait_ge(xt_full, n + 1)
                dve.tensor_copy(res_a[:, 4:8, n * P:(n + 1) * P], bank[:, 2 * (n % 2) + 1, :].rearrange("p (k t) -> p k t", k=4)).then_inc(xt_dve, 1)
            dve.wait_ge(set_mm, 1)
            dve.tensor_copy(vec[:].rearrange("p k v -> p (k v)"), bank[:, 4, 0:KD * NV])
            dve.tensor_copy(gcw[:].rearrange("p k v -> p (k v)"), bank[:, 5, 0:12 * GW])
            dve.tensor_copy(res_a[:, :, T:TT], bank[:, 5, 96:96 + KD * B].rearrange("p (k b) -> p k b", k=KD))
            dve.tensor_copy(gst[:].rearrange("p k b w -> p (k b w)"), bank[:, 6, 0:12 * B * (GW - 1)])
            dve.wait_ge(set_mm, 2)
            dve.tensor_copy(sbias[:].rearrange("p r h -> p (r h)"), bank[:, 0, 192:192 + 3 * H])
            dve.tensor_copy(merge[:].rearrange("p a l m -> p (a l m)"), merge_words)
            dve.memset(bsb[:, 256:384], NEG)
            dve.tensor_copy(bsb[:, 0:256], bank[0:H, 7, 0:256])
            step(dve.tensor_copy(lam[:, 0:2], bank[:, 0, 256:258]))
            dve.sem_inc(set_dve, 1)
            dve.wait_ge(lam_exp, 1)
            step(dve.tensor_tensor(lam[:, 4:5], lam[:, 3:4], lam[:, 2:3], ALU.subtract))
            step(dve.tensor_scalar(lam[:, 5:6], lam[:, 4:5], LAM0, None, ALU.subtract))

        qkv = tiles(0, 12)

        def copy_out(eng, g, par, rounds, dst):
            g.grant(eng, [par])
            with eng.Fori(0, rounds) as i:
                for j in range(par, g.per, 2):
                    g.wait_full(eng, i, j)
                    d = dst(i, j // NCH, j % NCH)
                    if par == 0:
                        eng.activation(d, bank[:, j % 6, 0:CH], ACT.Copy).then_inc(g.free[0], 1)
                    else:
                        eng.tensor_copy(d, bank[:, j % 6, 0:CH]).then_inc(g.free[1], 1)

        def att_dst(i, t, c):
            return big[:, ds(i * (4 * TT) + (t * TT + c * CH), CH)]

        x_parked = sem("x_parked")

        def pe_part1(pe):
            setup_pe(pe)
            norm_pe(pe, 0)
            pe.wait_ge(n_out, NCH * KD)
            project_pe(pe, g_att, res_b)

        def act_part1(act):
            setup_act(act)
            act.wait_ge(xt_dve, NB)
            act.wait_ge(set_dve, 1)
            norm_act(act, 0, res_a)
            copy_out(act, g_att, 0, 3, att_dst)

        def dve_part1(dve, step):
            setup_dve(dve, step)
            dve.wait_ge(xt_act, NB)
            norm_dve(dve, 0, res_a, res_b, V_MIX0)
            copy_out(dve, g_att, 1, 3, att_dst)

        def sp_part1(sp):
            setup_sp(sp)
            stream(sp, g_att, lambda i, s: cols(w_in0, i * 4 + s), None)
            sp.wait_ge(n_out, NCH * KD)
            sp.dma_start(park.ap(), res_a[:].rearrange("p k t -> p (k t)")).then_inc(x_parked, 16)
            sp.wait_ge(x_parked, 16)

        def pool_part1(pool, step):
            pool.wait_ge(set_dve, 1)
            pool.dma_start(brow.ap().rearrange("q h m -> h q m"), bsb.unsqueeze(1).to_broadcast([H, P, 384])).then_inc(bias_io, 16)
            pool.wait_ge(bias_io, 16)

        kv_full, k_copied, v_copied = sem("kv_full"), sem("k_copied"), sem("v_copied")
        k_out = [sem("k_out0"), sem("k_out1")]
        v_out = sem("v_out")
        skv_copied = sem("skv_copied")
        skv_out = sem("skv_out")
        ktok = flat(21600, 2, 512)
        vtok = res_a[:].rearrange("p k t -> p (k t)")[:, 4 * TT:4 * TT + NB * 512].rearrange("p (n e) -> p n e", n=NB)
        skv = flat(16480, 2, 512, parts=B)

        def kv_pe(pe):
            g_att.wait_all_read(pe)
            for n in range(NB):
                for kv in range(2):
                    if n >= 2:
                        pe.wait_ge((k_copied, v_copied)[kv], n - 1)
                    for h in range(H):
                        mm = pe.transpose(bank[:, 2 * (n % 2) + kv, h * P:(h + 1) * P], qkv[:, 4 + 4 * kv + h, n * P:(n + 1) * P], ident[:, :])
                    mm.then_inc(kv_full, 1)
            for kv in range(2):
                for h in range(H):
                    mm = pe.transpose(bank[0:B, 4 + kv, h * P:(h + 1) * P], qkv[:, 4 + 4 * kv + h, T:TT], ident[:, :])
            mm.then_inc(kv_full, 1)

        def kv_act(act):
            for n in range(NB):
                act.wait_ge(kv_full, 2 * n + 1)
                if n >= 2:
                    act.wait_ge(k_out[n % 2], 16 * (n // 2))
                act.activation(ktok[:, n % 2, :], bank[:, 2 * (n % 2), :], ACT.Copy).then_inc(k_copied, 1)

        def kv_dve(dve):
            for n in range(NB):
                dve.wait_ge(kv_full, 2 * n + 2)
                if n == 0:
                    dve.wait_ge(x_parked, 16)
                dve.tensor_copy(vtok[:, n, :], bank[:, 2 * (n % 2) + 1, :]).then_inc(v_copied, 1)
            dve.wait_ge(kv_full, 2 * NB + 1)
            dve.tensor_copy(skv[:, 0, :], bank[0:B, 4, :])
            dve.tensor_copy(skv[:, 1, :], bank[0:B, 5, :]).then_inc(skv_copied, 1)
            dve.tensor_copy(sq[:], qkv[:, :, T:TT]).then_inc(skv_copied, 1)

        def kv_pool(pool):
            kp = o["new_k_prompt"].rearrange("e o (n p) h d -> (e o n) p (h d)", p=P)
            vp = o["new_v_prompt"].rearrange("e o (n p) h d -> (e o n) p (h d)", p=P)
            for n in range(NB):
                pool.wait_ge(k_copied, n + 1)
                pool.dma_start(kp[n], ktok[:, n % 2, :]).then_inc(k_out[n % 2], 16)
                pool.wait_ge(v_copied, n + 1)
                pool.dma_start(vp[n], vtok[:, n, :]).then_inc(v_out, 16)
            pool.wait_ge(skv_copied, 1)
            pool.dma_start(o["new_k_sample"].rearrange("e b o h d -> (e b o) (h d)"), skv[:, 0, :]).then_inc(skv_out, 16)
            pool.dma_start(o["new_v_sample"].rearrange("e b o h d -> (e b o) (h d)"), skv[:, 1, :]).then_inc(skv_out, 16)

        mix = res_a
        prob = flat(12384, 2, 2, T)
        wT = flat(16480, 2, NB, P)
        biasT = flat(18528, H, 256)
        qs, ks = flat(19552, T), flat(20576, T)
        osb = flat(21600, NB, P)
        osq = tmp[:].rearrange("p s c -> p (s c)")[:, 0:NB * P].rearrange("p (n e) -> p n e", n=NB)
        far = small[:, 0:1]
        nmax = small[:, 4:8].rearrange("p (a m) -> p a m", a=2)
        psum_ = small[:, 8:12].rearrange("p (a m) -> p a m", a=2)
        prec = small[:, 12:16].rearrange("p (a m) -> p a m", a=2)
        ssq = small[:, 16:24]
        pbank = bank[:].rearrange("p b n -> p (b n)")
        head_in, s_full, z_late, z_early = sem("head_in"), sem("s_full"), sem("z_late"), sem("z_early")
        max_done, exp_done, a_full = sem("max_done"), sem("exp_done"), sem("a_full")
        at_full, at_copied, pv_full = sem("at_full"), sem("at_copied"), sem("pv_full")
        o_copied, o_sum, o_root, o_normed, ot_full, o_read = (sem(x) for x in ("o_copied", "o_sum", "o_root", "o_normed", "ot_full", "o_read"))
        GRP = [1, 2, 3, 4, 6, 8, 10, 12]

        def groups(i):
            return [(GRP[i] - 1 - (i // 4 - q), 4 * q, min(4 * q + 3, i)) for q in range(i // 4 + 1)]

        def att_pool(pool):
            pool.wait_ge(n_out, 1)
            pool.dma_start(biasT, bass.AP(tensor=brow, offset=P - 1, ap=[[H * 384 - 1, P], [384, H], [1, 256]])).then_inc(bias_io, 16)
            g_att.wait_all_read(pool)
            with pool.Fori(0, H) as h:
                pool.wait_ge(o_read, h + 1)
                pool.tensor_copy(qs, big[:, ds(h * TT, T)])
                pool.tensor_copy(far, sbias[:, 1, ds(h, 1)])
                pool.tensor_copy(ks, big[:, ds((h + 4) * TT, T)]).then_inc(head_in, 1)

        def att_pe(pe):
            pe.sem_inc(at_full, 3)
            pe.sem_inc(pv_full, 2)
            pe.wait_ge(k_copied, NB)
            pe.wait_ge(v_copied, NB)
            pe.wait_ge(skv_copied, 1)

            def scores(h, i):
                for m in range(2):
                    pe.wait_ge(z_late, 16 * h + 2 * i + m + 1)
                    if i == 0:
                        pe.wait_ge(z_early, 12 * h + m + 1)
                    elif i >= 3:
                        pe.wait_ge(z_early, 12 * h + 2 * (i - 3) + m + 3)
                    L = (i + 1) * P
                    for c0 in range(0, L, 512):
                        c1 = min(L, c0 + 512)
                        mm = pe.matmul(pbank[:, 1024 * m + c0:1024 * m + c1], qs[DA * m:DA * (m + 1), i * P:(i + 1) * P],
                                       ks[DA * m:DA * (m + 1), c0:c1], start=True, stop=True)
                    mm.then_inc(s_full, 1)

            with pe.Fori(0, H) as h:
                pe.wait_ge(head_in, h + 1)
                scores(h, 0)
                for i in range(NB):
                    if i + 1 < NB:
                        scores(h, i + 1)
                    pe.wait_ge(a_full, 8 * h + i + 1)
                    for gi, b0, b1 in groups(i):
                        pe.wait_ge(at_copied, 12 * h + gi + 1)
                        for b in range(b0, b1 + 1):
                            mm = pe.transpose(bank[:, 4 + gi % 2, (b - b0) * P:(b - b0 + 1) * P], prob[:, i % 2, 0, b * P:(b + 1) * P], ident[:, :])
                        mm.then_inc(at_full, 1)
                    pe.wait_ge(at_copied, 12 * h + GRP[i] + 2)
                    if i == 0:
                        pe.wait_ge(o_read, h + 1)
                    for b in range(i + 1):
                        mm = pe.matmul(bank[:, 6 + i // 4, i % 4 * P:(i % 4 + 1) * P], wT[:, i % 2, b, :],
                                       vflat[:, ds(h * P + (4 * TT + b * 512), P)], start=(b == 0), stop=(b == i))
                    mm.then_inc(pv_full, 1)
                pe.wait_ge(o_normed, h + 1)
                for n in range(NB):
                    mm = pe.transpose(bank[:, 6 + n // 4, n % 4 * P:(n % 4 + 1) * P], osb[:, n, :], ident[:, :])
                mm.then_inc(ot_full, 1)
        vflat = res_a[:].rearrange("p k t -> p (k t)")

        def att_act(act, step):
            act.sem_inc(z_early, 2)
            act.sem_inc(at_copied, 2)
            for s in range(2):
                act.wait_ge(k_out[s], 16 * (NB // 2))
            act.wait_ge(skv_out, 32)
            with act.Fori(0, H) as h:
                act.wait_ge(head_in, h + 1)
                for i in range(NB + 1):
                    if i < NB:
                        for m in range(2):
                            if i >= 2:
                                act.wait_ge(z_late, 16 * h + 2 * i + m + 3)
                                act.activation(prob[:, i % 2, m, 0:(i - 1) * P], pbank[:, 1024 * m:1024 * m + (i - 1) * P],
                                               ACT.Identity, bias=far, scale=DA ** -0.5).then_inc(z_early, 1)
                        for m in range(2):
                            act.wait_ge(max_done, 16 * h + 2 * i + m + 1)
                            act.activation(prob[:, i % 2, m, 0:(i + 1) * P], prob[:, i % 2, m, 0:(i + 1) * P], ACT.Exp,
                                           bias=nmax[:, i % 2, m:m + 1], accum_out=psum_[:, i % 2, m:m + 1]).then_inc(exp_done, 1)
                    if i:
                        b = i - 1
                        act.wait_ge(pv_full, 8 * h + b + 1)
                        for gi, b0, b1 in groups(b):
                            act.wait_ge(at_full, 12 * h + gi + 4)
                            act.activation(wT[:, b % 2, b0:b1 + 1, :], bank[:, 4 + gi % 2, 0:(b1 - b0 + 1) * P].rearrange("p (n q) -> p n q", q=P),
                                           ACT.Copy).then_inc(at_copied, 1)
                act.wait_ge(pv_full, 8 * h + NB + 2)
                for b in range(2):
                    act.activation(osb[:, 4 * b:4 * b + 4, :], bank[:, 6 + b, :].rearrange("p (n q) -> p n q", q=P), ACT.Copy).then_inc(o_copied, 1)
                act.wait_ge(o_sum, h + 1)
                act.activation(ssq, ssq, ACT.Sqrt).then_inc(o_root, 1)
                act.wait_ge(ot_full, h + 1)
                for b in range(2):
                    last = act.activation(vflat[:, ds(h * TT + 512 * b, 512)], bank[:, 6 + b, :], ACT.Copy, scale=hw[:, 0:1])
                last.then_inc(o_read, 1)

        def att_dve(dve, step):
            dve.sem_inc(z_late, 2)
            step(dve.tensor_scalar(hw[:, 0:1], hw[:, 0:1], 1.0 - LAM0, None, ALU.mult))
            dve.sem_inc(o_read, 1)
            dve.wait_ge(bias_io, 32)
            with dve.Fori(0, H) as h:
                step.enter(h, 4 * NB + 3)
                for i in range(NB + 1):
                    if i < NB:
                        L, L0 = (i + 1) * P, max(i - 1, 0) * P
                        dve.wait_ge(at_full, 12 * h + (1, 3)[i] if i < 2 else 12 * h + GRP[i - 2] + 3)
                        for m in range(2):
                            dve.wait_ge(s_full, 16 * h + 2 * i + m + 1)
                            dve.scalar_tensor_tensor(prob[:, i % 2, m, L0:L], pbank[:, 1024 * m + L0:1024 * m + L], DA ** -0.5,
                                                     big[:, ds(h * 256 + (18528 + 256 - (L - L0)), L - L0)], ALU.mult, ALU.add).then_inc(z_late, 1)
                        for m in range(2):
                            dve.wait_ge(z_late, 16 * h + 2 * i + m + 3)
                            if i >= 2:
                                dve.wait_ge(z_early, 12 * h + 2 * (i - 2) + m + 3)
                            dve.tensor_reduce(nmax[:, i % 2, m:m + 1], prob[:, i % 2, m, 0:L], AX.X, ALU.max, negate=True).then_inc(max_done, 1)
                    if i:
                        b = i - 1
                        L, s = (b + 1) * P, b % 2
                        dve.wait_ge(exp_done, 16 * h + 2 * b + 2)
                        step(dve.reciprocal(prec[:, s, :], psum_[:, s, :]))
                        step(dve.tensor_scalar(prec[:, s, 1:2], prec[:, s, 1:2], lam[:, 5:6], None, ALU.mult))
                        step(dve.tensor_scalar(prob[:, s, 0, 0:L], prob[:, s, 0, 0:L], prec[:, s, 0:1], None, ALU.mult))
                        step(dve.scalar_tensor_tensor(prob[:, s, 0, 0:L], prob[:, s, 1, 0:L], prec[:, s, 1:2], prob[:, s, 0, 0:L], ALU.mult, ALU.add))
                        dve.sem_inc(a_full, 1)
                dve.wait_ge(o_copied, 2 * h + 2)
                step(dve.tensor_tensor(osq, osb, osb, ALU.mult))
                step(dve.tensor_reduce(ssq, osq, AX.X, ALU.add))
                step(dve.tensor_scalar(ssq, ssq, 1.0 / P, 1e-5, ALU.mult, ALU.add))
                dve.reciprocal(ssq, ssq).then_inc(o_sum, 1)
                dve.wait_ge(o_root, h + 1)
                dve.tensor_tensor(osb, osb, ssq.unsqueeze(2).to_broadcast([P, NB, P]), ALU.mult).then_inc(o_normed, 1)
            step.leave(H)


        g_gdn = Gemm(g_sems, 4)
        RAW = T + GW - 1 + B
        raw = vflat[:, 4 * TT:4 * TT + 2 * RAW].rearrange("p (s t) -> p s t", s=2)
        diagq = vflat[:, 4 * TT + 2 * RAW:4 * TT + 2 * RAW + 1024].rearrange("p (s h d) -> p s h d", s=2, h=H)
        ring = flat(17 * TT, 4, 2, 512)
        prod = flat(17 * TT + 4096, 1024)
        ba = big[0:2 * H, 16 * TT:17 * TT]
        pflat = probs[:].rearrange("p b g x -> p (b g x)")
        page_in = [sem(f"page_in{s}") for s in range(4)]
        kpage_used = sem("kpage_used")
        qb_diag, qb_full, conv_done, raw_zero = sem("qb_diag"), sem("qb_full"), sem("conv_done"), sem("raw_zero")
        silu_done = sem("silu_done")
        z_gated = sem("z_gated")
        ba_in, ba_full, ba_copied = sem("ba_in"), sem("ba_full"), sem("ba_copied")
        sm_dve_marks = Marks(sem("sm_dve"), own_prod=1, sm_max=1, sm_diag=1, sm_exp_in=1, sm_part=1)
        sm_pe_marks = Marks(sem("sm_pe"), own_full=1, sm_turned=1, sm_bmax=1, sm_sum=1)
        sm_exp, aw_done = sem("sm_exp"), sem("aw_done")

        def load_pages(sp, cache, b, pair, slot):
            for u in range(2):
                page = sp.value_load(pages[0:1, ds(b * PG + (2 * pair + u), 1)], min_val=0, max_val=cache.shape[1] - 1)
                src = cache.rearrange("e n p h d -> (e n) p (h d)")[ds(page, 1)].rearrange("o p n -> (o p) n")
                sp.dma_start(ring[:, slot, u, :], src).then_inc(page_in[slot], 16)

        def gdn_in_sp(sp):
            sp.dma_start(wba[:], w_in0.rearrange("(k p) n -> p k n", p=P)[:, :, 28 * P:28 * P + 2 * H]).then_inc(ba_in, 16)

            def body(i):
                for t in range(4):
                    load_slab(sp, g_gdn, i, t, lambda i, s: cols(w_in0, i * 4 + (12 + s)), g_att)
                    for pp in range(4):
                        sp.wait_ge(kpage_used, i * 16 + (4 * t + pp + 13))
                        load_pages(sp, a["cache_attn_k"], i * 2 + t // 2, t % 2 * 4 + pp, pp)
            body(0)
            with sp.Fori(1, 3) as i:
                body(i)
            body(3)

        def gdn_in_pe(pe):
            pe.sem_inc(qb_full, 2)

            def body(i):
                for t in range(4):
                    if t % 2 == 0:
                        pe.wait_ge(qb_diag, i * 2 + t // 2 + 1)
                        pe.wait_ge(kpage_used, i * 16 + (4 * t + 8))
                        pe.matmul(bank[:, 6 + t // 2, :], ones[:, :], diagq[:, t // 2].rearrange("p h d -> p (h d)"), start=True, stop=True).then_inc(qb_full, 1)
                    wait_slab(pe, i, t)
                    for c in range(NCH):
                        job(pe, g_gdn, i, NCH * t + c, [(t, KD)], lambda k, j: res_b[:, k, chunk(j % NCH)])
            pe.wait_ge(o_read, H + 1)
            with pe.Fori(0, 3) as i:
                body(i)
            body(3)
            w_rounds[1] += 4
            pe.wait_ge(ba_in, 16)
            g_gdn.wait_all_read(pe)
            for c in range(NCH):
                for k in range(KD):
                    mm = pe.matmul(bank[0:2 * H, c, 0:CH], wba[:, k, :], res_b[:, k, chunk(c)], start=(k == 0), stop=(k == KD - 1))
                mm.then_inc(ba_full, 1)

        def gdn_in_act(act):
            g_gdn.grant(act, [0, 1])
            act.wait_ge(raw_zero, 1)

            def silu(i, t):
                act.wait_ge(conv_done, i * 4 + t + 1)
                d = big[:, ds((i * 4 + t) * TT, TT)]
                act.activation(d, d, ACT.Silu).then_inc(silu_done, 1)

            with act.Fori(0, 3) as i:
                for t in range(4):
                    for c in range(NCH):
                        g_gdn.wait_full(act, i, NCH * t + c)
                        act.activation(raw[:, t % 2, GW - 1 + c * CH:GW - 1 + (c + 1) * CH], bank[:, (NCH * t + c) % 6, 0:CH],
                                       ACT.Copy).then_inc(g_gdn.free[(NCH * t + c) % 2], 1)
                    if t:
                        silu(i, t - 1)
                silu(i, 3)
            for j in range(12):
                g_gdn.wait_full(act, 3, j)
                act.activation(tiles(12 + j // NCH, 1)[:, 0, chunk(j % NCH)], bank[:, j % 6, 0:CH], ACT.Copy).then_inc(g_gdn.free[j % 2], 1)
            g_gdn.wait_all_read(act)
            z = tiles(12, H)
            act.activation(z, z, ACT.Silu).then_inc(z_gated, 1)
            for c in range(NCH):
                act.wait_ge(ba_full, c + 1)
                act.activation(ba[:, chunk(c)], bank[0:2 * H, c, 0:CH], ACT.Copy).then_inc(ba_copied, 1)

        def gdn_in_pool(pool):
            pool.wait_ge(skv_copied, 2)
            for s in range(2):
                pool.wait_ge(o_read, H + 1)
            with pool.Fori(0, B // 2) as i:
                for s in range(2):
                    pool.wait_ge(qb_full, i * 2 + s + 1)
                    pool.tensor_tensor(diagq[:, s], ident[:].unsqueeze(1).to_broadcast([P, H, P]),
                                       sq[:, 0:H, ds(i * 2 + s, 1)].to_broadcast([P, H, P]), ALU.mult).then_inc(qb_diag, 1)

        def gdn_in_dve(dve, step):
            dve.wait_ge(pv_full, 8 * H + 2)
            dve.wait_ge(v_out, 16 * NB)
            dve.wait_ge(ot_full, H)
            dve.memset(raw[:, :, 0:GW - 1], 0.0).then_inc(raw_zero, 1)
            dve.sem_inc(kpage_used, 16)

            def score(i, t):
                b = i * 2 + t // 2
                for pp in range(4):
                    dve.wait_ge(page_in[pp], i * 128 + 32 * (t + 1))
                    if pp == 0 and t % 2 == 0:
                        dve.wait_ge(qb_full, b + 3)
                    dve.wait_ge(kpage_used, i * 16 + (4 * t + pp + 16))
                    step(dve.tensor_tensor(prod.rearrange("p (u n) -> p u n", u=2), ring[:, pp], bank[:, 6 + t // 2, :].unsqueeze(1).to_broadcast([P, 2, 512]), ALU.mult))
                    dve.tensor_reduce(pflat[:, ds(b * (PG * 2 * H) + 16 * (t % 2 * 4 + pp), 16)], prod.rearrange("p (x d) -> p x d", d=DA),
                                      AX.X, ALU.add).then_inc(kpage_used, 1)

            def conv(i, t):
                n = i * 4 + t
                for j in (NCH * t + 1, NCH * t + 2):
                    g_gdn.wait_read(dve, i, j)
                w = gcwf
                d = big[:, ds(n * TT, T)]
                e = big[:, ds(n * TT + T, B)]
                r = raw[:, t % 2]
                dve.tensor_copy(gnewf[:, ds(n * (GW - 1 + B), GW - 1 + B)], r[:, T:RAW])
                for q in range(GW):
                    s = gstf[:, ds(n * (B * (GW - 1)) + q, B, GW - 1)] if q < GW - 1 else r[:, T + GW - 1:RAW]
                    wc = w[:, ds(n * GW + q, 1)]
                    if q == 0:
                        dve.tensor_scalar(e, s, wc, None, ALU.mult)
                        step(dve.tensor_scalar(d, r[:, 0:T], wc, None, ALU.mult))
                    else:
                        dve.scalar_tensor_tensor(e, s, wc, e, ALU.mult, ALU.add)
                        step(dve.scalar_tensor_tensor(d, r[:, q:q + T], wc, d, ALU.mult, ALU.add))
                dve.sem_inc(conv_done, 1)

            with dve.Fori(0, 3) as i:
                step.enter(i, 4 * (GW + 4))
                for t in range(4):
                    conv(i, t)
                    score(i, t)
            step.leave(3)
            for t in range(4):
                score(3, t)
        gcwf, gnewf = gcw[:].rearrange("p k w -> p (k w)"), gnew[:].rearrange("p k w -> p (k w)")
        gstf = gst[:].rearrange("p k b w -> p (k b w)")

        X = B * 2 * H
        smx, own, bmx, ssum, coef = (small[:, 64 * (n + 1):64 * (n + 2)] for n in range(5))
        sdiag = small[0:X, 384:384 + X]
        smt = small[0:X, 448:449]
        ownw = small[:, 452:452 + B * H]
        zb = prod[:, 0:PG * 2 * H]
        qkp = prod[:, 256:256 + H * B]

        def sm_dve(dve, step):
            dve.wait_ge(kpage_used, 16 + B * PG // 2)
            dve.tensor_tensor(qkp.rearrange("p (h b) -> p h b", h=H), sq[:, 0:H, :], sq[:, H:2 * H, :], ALU.mult).then_inc(sm_dve_marks.sem, 1)
            zv = zb.rearrange("p (g h m) -> p g h m", g=PG, h=H)
            for m in range(2):
                dve.tensor_copy(zv[:, 0:PG - 1, :, m], sbias[:, 1, :].unsqueeze(1).to_broadcast([P, PG - 1, H]))
                step(dve.tensor_copy(zv[:, PG - 1, :, m], sbias[:, 0, :]))
            step(dve.scalar_tensor_tensor(pflat.rearrange("p (b x) -> p b x", b=B), pflat.rearrange("p (b x) -> p b x", b=B), DA ** -0.5,
                                          zb.unsqueeze(1).to_broadcast([P, B, PG * 2 * H]), ALU.mult, ALU.add))
            sm_pe_marks.wait(dve, "own_full", 1)
            ov = own.rearrange("p (b h m) -> p b h m", b=B, h=H)
            for m in range(2):
                step(dve.scalar_tensor_tensor(ov[:, :, :, m], bank[:, 3, m * 32:(m + 1) * 32].rearrange("p (h b) -> p b h", h=H), DA ** -0.5,
                                              sbias[:, 2, :].unsqueeze(1).to_broadcast([P, B, H]), ALU.mult, ALU.add))
            pv = probs[:].rearrange("p b g x -> p b x g")
            step(dve.tensor_reduce(smx, pv, AX.X, ALU.max))
            dve.tensor_tensor(smx, smx, own, ALU.max).then_inc(sm_dve_marks.sem, 1)
            sm_pe_marks.wait(dve, "sm_turned", 1)
            step(dve.tensor_reduce(smt, bank[0:X, 4, 0:P], AX.X, ALU.max))
            dve.tensor_scalar(sdiag, ident[0:X, 0:X], smt, None, ALU.mult).then_inc(sm_dve_marks.sem, 1)
            sm_pe_marks.wait(dve, "sm_bmax", 1)
            step(dve.tensor_copy(bmx, bank[:, 5, 0:X]))
            mb = bmx.rearrange("p (b x) -> p b x", b=B).unsqueeze(2).to_broadcast([P, B, PG, 2 * H])
            dve.tensor_tensor(own, own, bmx, ALU.subtract)
            dve.tensor_tensor(probs[:], probs[:], mb, ALU.subtract).then_inc(sm_dve_marks.sem, 1)
            dve.wait_ge(sm_exp, 2)
            dve.tensor_reduce(ssum, pv, AX.X, ALU.add).then_inc(sm_dve_marks.sem, 1)
            sm_pe_marks.wait(dve, "sm_sum", 1)
            step(dve.tensor_tensor(coef, bank[:, 4, 0:X], own, ALU.add))
            step(dve.reciprocal(coef, coef))
            cm = coef.rearrange("p (y m) -> p y m", m=2)
            step(dve.tensor_scalar(cm[:, :, 1], cm[:, :, 1], lam[:, 5:6], None, ALU.mult))
            dve.tensor_tensor(own, own, coef, ALU.mult)
            step(dve.tensor_tensor(probs[:], probs[:], coef.rearrange("p (b x) -> p b x", b=B).unsqueeze(2).to_broadcast([P, B, PG, 2 * H]), ALU.mult))
            dve.tensor_reduce(ownw, own.rearrange("p (y m) -> p y m", m=2), AX.X, ALU.add)
            dve.tensor_reduce(aw[:].rearrange("p b g h -> p (b g h)"), pflat.rearrange("p (y m) -> p y m", m=2), AX.X, ALU.add).then_inc(aw_done, 1)

        def sm_pe(pe):
            sm_dve_marks.wait(pe, "own_prod", 1)
            for m in range(2):
                mm = pe.matmul(bank[:, 3, m * 32:(m + 1) * 32], halves[:, m, :], qkp, start=True, stop=True)
            mm.then_inc(sm_pe_marks.sem, 1)
            sm_dve_marks.wait(pe, "sm_max", 1)
            pe.transpose(bank[0:X, 4, 0:P], smx, ident[:, :]).then_inc(sm_pe_marks.sem, 1)
            sm_dve_marks.wait(pe, "sm_diag", 1)
            pe.matmul(bank[:, 5, 0:X], ones[0:X, :], sdiag, start=True, stop=True).then_inc(sm_pe_marks.sem, 1)
            sm_dve_marks.wait(pe, "sm_part", 1)
            pe.matmul(bank[:, 4, 0:X], ones[:, :], ssum, start=True, stop=True).then_inc(sm_pe_marks.sem, 1)

        def sm_act(act):
            sm_dve_marks.wait(act, "sm_exp_in", 1)
            act.activation(own, own, ACT.Exp).then_inc(sm_exp, 1)
            act.activation(pflat, pflat, ACT.Exp).then_inc(sm_exp, 1)
        l2_sq, l2_mm, l2_log, l2_inv, l2_out = (sem(x) for x in ("l2_sq", "l2_mm", "l2_log", "l2_inv", "l2_out"))

        def l2_pe(pe):
            pe.sem_inc(l2_mm, 3)
            pe.wait_ge(ba_copied, NCH)
            with pe.Fori(0, 2 * H) as i:
                for c in range(NCH):
                    pe.wait_ge(l2_sq, i * NCH + c + 1)
                    pe.wait_ge(l2_log, i * NCH + c + 1)
                    pe.matmul(bank[:, c, 0:CH], ones[:, :], tmp[:, c, :], start=True, stop=True).then_inc(l2_mm, 1)

        def l2_act(act):
            act.sem_inc(l2_log, 3)

            def body(i, scale):
                for c in range(NCH):
                    act.wait_ge(l2_mm, i * NCH + c + 1)
                    act.activation(tmp[:, c, :], big[:, ds(i * TT + c * CH, CH)], ACT.Square).then_inc(l2_sq, 1)
                for c in range(NCH):
                    act.wait_ge(l2_mm, i * NCH + c + 4)
                    act.wait_ge(l2_out, i * NCH + c + 1)
                    act.activation(rstd[:, c, :], bank[:, c, 0:CH], ACT.Ln, bias=1e-6).then_inc(l2_log, 1)
                for c in range(NCH):
                    act.wait_ge(l2_log, i * NCH + c + 4)
                    act.activation(rstd[:, c, :], rstd[:, c, :], ACT.Exp, scale=-0.5, bias=math.log(scale)).then_inc(l2_inv, 1)
            act.wait_ge(silu_done, 12)
            with act.Fori(0, H) as i:
                body(i, P ** -0.5)
            with act.Fori(H, 2 * H) as i:
                body(i, 1.0)

        def l2_dve(dve):
            dve.sem_inc(l2_out, 3)
            dve.wait_ge(silu_done, 12)
            with dve.Fori(0, 2 * H) as i:
                for c in range(NCH):
                    dve.wait_ge(l2_inv, i * NCH + c + 1)
                    d = big[:, ds(i * TT + c * CH, CH)]
                    dve.tensor_tensor(d, d, rstd[:, c, :], ALU.mult).then_inc(l2_out, 1)

        NG = NB + B
        graw = small[:, 0:NG * 2 * H].rearrange("p (n r) -> p n r", n=NG)
        beta, ga, gsp, gg = (small[:, 128 + 64 * n:192 + 64 * n].rearrange("p (n h) -> p n h", n=NG) for n in range(4))
        decay_a = small[:, 384:388]
        bad = small[0:2 * H, 388:452].rearrange("p (r b) -> p r b", r=2 * H)
        gate_full, gate_act, gates_done = sem("gate_full"), sem("gate_act"), sem("gates_done")
        gate_marks = Marks(sem("gate_dve"), gate_diag=1, gate_raw=1, gate_abs=1)

        def gate_pe(pe):
            for n in range(NB):
                pe.transpose(bank[:, 3, n * 8:(n + 1) * 8], ba[:, n * P:(n + 1) * P], ident[0:2 * H, 0:2 * H])
            gate_marks.wait(pe, "gate_diag", 1)
            pe.matmul(bank[:, 3, 64:128], ones[0:2 * H, :], bad.rearrange("p r b -> p (r b)"), start=True, stop=True).then_inc(gate_full, 1)

        def gate_dve(dve, step):
            dve.wait_ge(ba_copied, NCH)
            dve.wait_ge(aw_done, 1)
            dve.tensor_tensor(bad, ba[:, T:TT].unsqueeze(1).to_broadcast([2 * H, 2 * H, B]),
                              ident[0:2 * H, 0:2 * H].unsqueeze(2).to_broadcast([2 * H, 2 * H, B]), ALU.mult).then_inc(gate_marks.sem, 1)
            dve.wait_ge(gate_full, 1)
            dve.tensor_copy(graw[:, 0:NB, :], bank[:, 3, 0:64].rearrange("p (n r) -> p n r", n=NB))
            step(dve.tensor_copy(graw[:, NB:NG, :], bank[:, 3, 64:128].rearrange("p (r b) -> p b r", b=B)))
            dve.sem_inc(gate_marks.sem, 1)
            step(dve.tensor_tensor(ga, graw[:, :, H:2 * H], gate0[:, 1, :].unsqueeze(1).to_broadcast([P, NG, H]), ALU.add))
            dve.scalar_tensor_tensor(gsp, ga, -1.0, ga, ALU.mult, ALU.max).then_inc(gate_marks.sem, 1)
            dve.wait_ge(gate_act, 4)
            step(dve.scalar_tensor_tensor(gsp, ga, 0.0, gsp, ALU.max, ALU.add))
            dve.scalar_tensor_tensor(gg, gsp, -1.0, decay_a.unsqueeze(1).to_broadcast([P, NG, H]), ALU.mult, ALU.mult).then_inc(gates_done, 1)

        def gate_act_fn(act):
            gate_marks.wait(act, "gate_raw", 1)
            act.activation(beta, graw[:, :, 0:H], ACT.Sigmoid).then_inc(gate_act, 1)
            act.activation(decay_a, gate0[:, 0, :], ACT.Exp).then_inc(gate_act, 1)
            gate_marks.wait(act, "gate_abs", 1)
            act.activation(gsp, gsp, ACT.Exp, scale=-1.0).then_inc(gate_act, 1)
            act.wait_ge(gate_act, 3)
            act.activation(gsp, gsp, ACT.Ln, bias=1.0).then_inc(gate_act, 1)

        rb = res_b[:].rearrange("p k t -> p (k t)")

        def hv(n):
            return rb[:, 1536 + 512 * n:2048 + 512 * n].rearrange("p (h t) -> p h t", h=H)
        qkvc = rb[:, 0:1536].rearrange("p (k t) -> p k t", k=12)
        decT, eR, lnT, inv_t, inv, xm, attnT, kbg, kdec, vb, qdec, nwT, vnew = (hv(n) for n in range(13))
        gcol = rb[:, 8192:8200].rearrange("p (a h) -> p a h", a=2)
        gexp = rb[:, 8200:8208].rearrange("p (a h) -> p a h", a=2)
        bge = rb[:, 8208:8212]
        gtri = prod[:, 0:512].rearrange("p (h t) -> p h t", h=H)
        bdiag = prod[:, 512:1024].rearrange("p (h t) -> p h t", h=H)
        c_in, gb_in, r_full, tr_full, dec_in, dec_exp, inv_id, inv0, m0_full, m0_copied = (sem(x) for x in (
            "c_in", "gb_in", "r_full", "tr_full", "dec_in", "dec_exp", "inv_id", "inv0", "m0_full", "m0_copied"))
        x_full, x_copied, p_full, pt_full, inv_up, invt_up = (sem(x) for x in ("x_full", "x_copied", "p_full", "pt_full", "inv_up", "invt_up"))
        kv_done, qdec_done, w_full, w_copied, vn_full, vn_copied, oc_full, oc_copied, sn_full, state_up = (sem(x) for x in (
            "kv_done", "qdec_done", "w_full", "w_copied", "vn_full", "vn_copied", "oc_full", "oc_copied", "sn_full", "state_up"))
        wait_carrier = sem("wait_carrier")
        state_zero, vpage_used = sem("state_zero"), sem("vpage_used")
        NL = LEVELS - 1

        def b4(n):
            return bank[:, n, :].rearrange("p (h t) -> p h t", h=H)

        def chunk_sp(sp):
            sp.wait_ge(kpage_used, 16 + B * PG // 2)
            with sp.Fori(0, B) as b:
                for pp in range(PG // 2):
                    sp.wait_ge(vpage_used, b * 8 + (pp + 1))
                    load_pages(sp, a["cache_attn_v"], b, pp, pp % 4)

        def chunk_pool(pool):
            pool.wait_ge(l2_out, 3 + NCH * 2 * H)
            pool.wait_ge(silu_done, 12)
            with pool.Fori(0, NB) as c:
                pool.wait_ge(tr_full, c + 1)
                pool.wait_ge(qdec_done, c + 1)
                pool.tensor_copy(qkvc, qkv[:, :, ds(c * P, P)]).then_inc(c_in, 1)
                pool.wait_ge(vn_full, c + 1)
                pool.sem_inc(wait_carrier, 1)
                pool.tensor_copy(inv_t, ident[:].unsqueeze(1).to_broadcast([P, H, P])).then_inc(inv_id, 1)
                pool.wait_ge(dec_exp, c + 1)
                pool.wait_ge(c_in, c + 1)
                pool.wait_ge(oc_full, c + 1)
                pool.tensor_tensor(qdec, qkvc[:, 0:H, :], eR, ALU.mult).then_inc(qdec_done, 1)

        def chunk_pe(pe):
            pe.sem_inc(tr_full, 1)
            pe.sem_inc(vn_full, 1)
            pe.sem_inc(oc_full, 1)
            pe.sem_inc(vpage_used, 4)
            pe.wait_ge(state_zero, 1)
            pe.matmul(bank[:, 7, 0:B * H], ones[:, :], state[:, 0, 0:B * H], start=True, stop=False, skip_group_check=True)
            pe.wait_ge(aw_done, 1)
            pe.wait_ge(l2_log, 3 + NCH * 2 * H)
            pe.wait_ge(gates_done, 1)

            def values(c, pp):
                pe.wait_ge(page_in[pp % 4], c * 64 + (512 + 32 * (pp // 4 + 1)))
                for u in range(2):
                    for h in range(H):
                        mm = pe.matmul(bank[:, 7, ds(c * H + h, 1)], ring[:, pp % 4, u, h * P:(h + 1) * P],
                                       awflat[:, ds(c * (PG * H) + ((2 * pp + u) * H + h), 1)], start=False, stop=False, skip_group_check=True)
                mm.then_inc(vpage_used, 1)

            with pe.Fori(0, NB) as c:
                pe.wait_ge(gb_in, c + 1)
                pe.wait_ge(invt_up, c * NL + 1)
                pe.matmul(bank[:, 0, :], ones[:, :], gtri.rearrange("p h t -> p (h t)"), start=True, stop=True)
                pe.matmul(bank[:, 1, :], ones[:, :], bdiag.rearrange("p h t -> p (h t)"), start=True, stop=True)
                pe.matmul(bank[:, 2, 0:H], triu[:, :], small[:, ds(c * H + 320, H)], start=True, stop=True).then_inc(r_full, 1)
                pe.wait_ge(c_in, c + 1)
                pe.wait_ge(w_copied, c + 1)
                pe.wait_ge(vn_copied, c + 1)
                pe.wait_ge(oc_copied, c + 1)
                pe.wait_ge(state_up, c + 1)
                for n, (l, r) in enumerate(((4, 4), (4, 0))):
                    for h in range(H):
                        pe.matmul(b4(3 + n)[:, h, :], qkvc[:, l + h, :], qkvc[:, r + h, :], start=True, stop=True)
                for n in range(2):
                    for h in range(H):
                        mm = pe.transpose(b4(5 + n)[:, h, :], qkvc[:, 4 + 4 * n + h, :], ident[:, :])
                mm.then_inc(tr_full, 1)
                values(c, 0)
                values(c, 1)
                pe.wait_ge(inv0, c + 1)
                for h in range(H):
                    mm = pe.transpose(b4(2)[:, h, :], inv_t[:, h, :], ident[:, :])
                mm.then_inc(m0_full, 1)
                for lv in range(NL):
                    if lv == 0:
                        pe.wait_ge(m0_copied, c + 1)
                    else:
                        pe.wait_ge(inv_up, c * (NL - 1) + lv)
                    for h in range(H):
                        mm = pe.matmul(b4(0)[:, h, :], lnT[:, h, :], inv[:, h, :], start=True, stop=True)
                    mm.then_inc(x_full, 1)
                    values(c, 2 + lv)
                    pe.wait_ge(x_copied, c * NL + lv + 1)
                    if lv:
                        pe.wait_ge(invt_up, c * NL + lv + 1)
                    if lv < NL - 1:
                        for h in range(H):
                            mm = pe.matmul(b4(1)[:, h, :], inv_t[:, h, :], xm[:, h, :], start=True, stop=True)
                        mm.then_inc(p_full, 1)
                    for h in range(H):
                        mm = pe.matmul(b4(2)[:, h, :], xm[:, h, :], inv_t[:, h, :], start=True, stop=True)
                    mm.then_inc(pt_full, 1)
                pe.wait_ge(kv_done, c + 1)
                pe.wait_ge(invt_up, c * NL + NL + 1)
                for h in range(H):
                    mm = pe.matmul(b4(3)[:, h, :], kbg[:, h, :], inv_t[:, h, :], start=True, stop=True)
                mm.then_inc(w_full, 1)
                pe.wait_ge(w_copied, c + 2)
                for h in range(H):
                    pe.matmul(b4(4)[:, h, :], inv_t[:, h, :], vb[:, h, :], start=True, stop=False)
                    mm = pe.matmul(b4(4)[:, h, :], nwT[:, h, :], state[:, h, :], start=False, stop=True)
                mm.then_inc(vn_full, 1)
                pe.wait_ge(vn_copied, c + 2)
                pe.wait_ge(qdec_done, c + 2)
                for h in range(H):
                    pe.matmul(b4(5)[:, h, :], state[:, h, :], qdec[:, h, :], start=True, stop=False)
                    mm = pe.matmul(b4(5)[:, h, :], vnew[:, h, :], attnT[:, h, :], start=False, stop=True)
                mm.then_inc(oc_full, 1)
                for h in range(H):
                    mm = pe.matmul(b4(6)[:, h, :], kdec[:, h, :], vnew[:, h, :], start=True, stop=True)
                mm.then_inc(sn_full, 1)
        awflat = aw[:].rearrange("p b g h -> p (b g h)")

        def chunk_act(act):
            for s in (w_copied, vn_copied, oc_copied):
                act.sem_inc(s, 1)
            with act.Fori(0, NB) as c:
                act.wait_ge(dec_in, c + 1)
                act.activation(decT, decT, ACT.Exp)
                act.wait_ge(qdec_done, c + 1)
                act.wait_ge(state_up, c + 1)
                act.activation(eR, b4(0), ACT.Exp)
                act.activation(gexp, gcol, ACT.Exp).then_inc(dec_exp, 1)
                act.wait_ge(m0_full, c + 1)
                act.activation(inv, b4(2), ACT.Copy).then_inc(m0_copied, 1)
                for lv in range(NL):
                    act.wait_ge(x_full, c * NL + lv + 1)
                    act.activation(xm, b4(0), ACT.Copy).then_inc(x_copied, 1)
                act.wait_ge(w_full, c + 1)
                act.activation(nwT, b4(3), ACT.Copy, scale=-1.0).then_inc(w_copied, 1)
                act.wait_ge(vn_full, c + 2)
                act.activation(vnew, b4(4), ACT.Copy).then_inc(vn_copied, 1)
                act.wait_ge(oc_full, c + 2)
                act.activation(res_a[:, H:2 * H, ds(c * P, P)], b4(5), ACT.Copy).then_inc(oc_copied, 1)

        def chunk_dve(dve, step):
            dve.memset(state[:], 0.0).then_inc(state_zero, 1)
            dve.wait_ge(state_zero, 1)
            dve.sem_inc(invt_up, 1)
            dve.sem_inc(state_up, 1)
            dve.wait_ge(gates_done, 1)
            bcast = (P, H, P)
            with dve.Fori(0, NB) as c:
                step.enter(c, 4)
                gc_ = small[:, ds(c * H + 320, H)]
                bc_ = small[:, ds(c * H + 128, H)]
                if True:
                    dve.tensor_tensor(gtri, triu[:].unsqueeze(1).to_broadcast([P, H, P]), gc_.unsqueeze(2).to_broadcast([P, H, P]), ALU.mult)
                    dve.tensor_tensor(bdiag, ident[:].unsqueeze(1).to_broadcast([P, H, P]), bc_.unsqueeze(2).to_broadcast([P, H, P]), ALU.mult).then_inc(gb_in, 1)
                dve.wait_ge(r_full, c + 1)
                step(dve.tensor_copy(gcol[:, 0, :], bank[:, 2, 0:H]))
                dve.tensor_tensor(gcol[:, 1, :], b4(0)[:, :, P - 1], gcol[:, 0, :], ALU.subtract)
                for h in range(H):
                    last = dve.scalar_tensor_tensor(decT[:, h, :], b4(0)[:, h, :], gcol[:, 0, h:h + 1], causal[:, :], ALU.subtract, ALU.add)
                last.then_inc(dec_in, 1)
                dve.wait_ge(dec_exp, c + 1)
                dve.wait_ge(tr_full, c + 2)
                step(dve.scalar_tensor_tensor(lnT, b4(3), -1.0, decT, ALU.mult, ALU.mult))
                step(dve.tensor_tensor(lnT, lnT, b4(1), ALU.mult))
                dve.wait_ge(inv_id, c + 1)
                dve.sem_inc(wait_carrier, 1)
                dve.copy_predicated(inv_t, merge[:, 1, 0, :].unsqueeze(1).to_broadcast([P, H, P]), lnT).then_inc(inv0, 1)
                dve.tensor_tensor(attnT, b4(4), decT, ALU.mult)
                step(dve.tensor_tensor(bge, gexp[:, 0, :], bc_, ALU.mult))
                dve.tensor_tensor(kbg, b4(5), bge.unsqueeze(2).to_broadcast([P, H, P]), ALU.mult)
                dve.tensor_tensor(kdec, b4(5), gexp[:, 1, :].unsqueeze(2).to_broadcast([P, H, P]), ALU.mult)
                dve.tensor_tensor(vb, b4(6), bc_.unsqueeze(2).to_broadcast([P, H, P]), ALU.mult).then_inc(kv_done, 1)
                dve.wait_ge(m0_copied, c + 1)
                for lv in range(NL):
                    if lv < NL - 1:
                        dve.wait_ge(p_full, c * (NL - 1) + lv + 1)
                        dve.sem_inc(wait_carrier, 1)
                        dve.copy_predicated(inv, merge[:, 0, lv + 1, :].unsqueeze(1).to_broadcast([P, H, P]), b4(1)).then_inc(inv_up, 1)
                    dve.wait_ge(pt_full, c * NL + lv + 1)
                    dve.sem_inc(wait_carrier, 1)
                    dve.copy_predicated(inv_t, merge[:, 1, lv + 1, :].unsqueeze(1).to_broadcast([P, H, P]), b4(2)).then_inc(invt_up, 1)
                dve.wait_ge(sn_full, c + 1)
                for h in range(H):
                    last = dve.scalar_tensor_tensor(state[:, h, :], state[:, h, :], eR[:, h, P - 1:P], b4(6)[:, h, :], ALU.mult, ALU.add)
                last.then_inc(state_up, 1)
            step.leave(NB)

        s_att, s_asq, s_arstd = small[:, 0:32], small[:, 32:64], small[:, 64:96]
        s_k, s_q, s_v = small[:, 96:128], small[:, 388:420], small[:, 420:452]
        s_eg, s_vn = small[:, 192:224], small[:, 224:256]
        s_beta = small[:, 160:192]
        U = B * H
        sst = rb[:, 0:U * P].rearrange("p (u e) -> p u e", u=U)
        vbig = rb[0:U, U * P:2 * U * P].rearrange("p (u e) -> p u e", u=U)
        srow = tmp[:].rearrange("p s c -> p (s c)")[0:U, 0:2 * P]
        s_dve = Marks(sem("sample_dve"), sa_sq=1, s_cols=1, s_mixed=1, vn_s=1, vbig_done=1)
        s_pe = Marks(sem("sample_pe"), gn_full=1, sa_mm=1, ks_full=1, row_full=1)
        s_act = Marks(sem("sample_act"), s_egs=1, sa_log=1, sa_rstd=1, gn_copied=3, row_copied=1)
        sst_in, sst_mm, sst_add, so_full, s_done = (sem(x) for x in ("sst_in", "sst_mm", "sst_add", "so_full", "s_done"))
        x_back = sem("x_back")
        misc_out = sem("misc_out")
        grow = prod
        grow3 = flat(17 * TT, CQ, parts=GW - 1 + B)
        STORES = 7

        def store(pool, dst, src):
            pool.dma_start(dst, src).then_inc(misc_out, 16)

        def sample_pool(pool):
            pool.wait_ge(state_up, NB + 1)
            store(pool, o["new_gdn_s_prompt"].rearrange("e b h d v -> d (e b h) v"), state[:])
            pool.wait_ge(oc_copied, NB + 1)
            pool.dma_start(sst, a["state_gdn_s"].rearrange("e b h d v -> d (e b h) v")).then_inc(sst_in, 16)
            store(pool, o["new_gdn_conv_sample"][0, :, 0:GW - 2, :], a["state_gdn_conv"][0, :, 1:GW - 1, :])
            store(pool, o["new_conv_buf_sample"][0, :, 0:CW - 2, :], a["state_conv_buf"][0, :, 1:CW - 1, :])
            s_act.wait(pool, "gn_copied", 3)
            store(pool, o["new_gdn_conv_prompt"].rearrange("e b w c -> (e b w) c"), grow3[0:GW - 1, :])
            store(pool, o["new_gdn_conv_sample"][0, :, GW - 2, :], grow3[GW - 1:GW - 1 + B, :])
            pool.wait_ge(sst_add, 8)
            pool.dma_start(o["new_gdn_s_sample"].rearrange("e b h d v -> d (e b h) v"), sst).then_inc(sst_in, 16)
            pool.wait_ge(so_full, 1)
            pool.wait_ge(sst_in, 32)
            pool.dma_start(rb, park.ap()).then_inc(x_back, 16)

        def sample_pe(pe):
            pe.wait_ge(state_up, NB + 1)
            pe.wait_ge(oc_copied, NB + 1)
            pe.wait_ge(invt_up, NB * NL + 1)
            for k in range(12):
                mm = pe.transpose(bank[0:GW - 1 + B, 3 + k // 4, k % 4 * P:(k % 4 + 1) * P], gnew[:, k, :], ident[:, :])
            mm.then_inc(s_pe.sem, 1)
            s_dve.wait(pe, "sa_sq", 1)
            pe.matmul(bank[:, 2, 0:U], ones[:, :], s_asq, start=True, stop=True).then_inc(s_pe.sem, 1)
            pe.wait_ge(sst_in, 16)
            s_dve.wait(pe, "s_cols", 1)
            for u in range(U):
                mm = pe.matmul(bank[:, 0, u:u + 1], sst[:, u, :], s_k[:, u:u + 1], start=True, stop=True)
            mm.then_inc(s_pe.sem, 1)
            s_dve.wait(pe, "vn_s", 1)
            pe.transpose(bank[0:U, 1, 0:P], s_vn, ident[:, :])
            pe.transpose(bank[0:U, 1, P:2 * P], s_k, ident[:, :]).then_inc(s_pe.sem, 1)
            s_dve.wait(pe, "vbig_done", 1)
            s_act.wait(pe, "gn_copied", 3)
            for j in range(8):
                if j >= 4:
                    pe.wait_ge(sst_add, j - 3)
                pe.matmul(bank[:, 3 + j % 4, :], srow[:, P:2 * P], vbig[:, 4 * j:4 * j + 4, :].rearrange("p u e -> p (u e)"), start=True, stop=True).then_inc(sst_mm, 1)
            pe.wait_ge(sst_add, 8)
            for u in range(U):
                mm = pe.matmul(bank[:, 0, u:u + 1], sst[:, u, :], s_q[:, u:u + 1], start=True, stop=True)
            mm.then_inc(so_full, 1)

        def sample_act(act):
            act.wait_ge(gates_done, 1)
            act.activation(s_eg, small[:, 320 + 32:384], ACT.Exp).then_inc(s_act.sem, 1)
            s_pe.wait(act, "sa_mm", 1)
            act.activation(s_arstd, bank[:, 2, 0:U], ACT.Ln, scale=1.0 / P, bias=1e-5).then_inc(s_act.sem, 1)
            s_act.wait(act, "sa_log", 1)
            act.activation(s_arstd, s_arstd, ACT.Exp, scale=-0.5).then_inc(s_act.sem, 1)
            s_pe.wait(act, "gn_full", 1)
            for n in range(3):
                act.activation(grow3[:, n * 512:(n + 1) * 512], bank[0:GW - 1 + B, 3 + n, :], ACT.Copy).then_inc(s_act.sem, 1)
            s_pe.wait(act, "row_full", 1)
            act.activation(srow, bank[0:U, 1, 0:2 * P], ACT.Copy).then_inc(s_act.sem, 1)

        def sample_dve(dve, step):
            dve.wait_ge(vpage_used, 4 + B * PG // 2)
            dve.wait_ge(l2_out, 3 + NCH * 2 * H)
            step(dve.tensor_tensor(s_att.rearrange("p (b h) -> p b h", b=B), ownw.rearrange("p (b h) -> p b h", b=B),
                                   sq[:, 2 * H:3 * H, :].rearrange("p h b -> p b h"), ALU.mult))
            step(dve.tensor_tensor(s_att, s_att, bank[:, 7, 0:U], ALU.add))
            dve.tensor_tensor(s_asq, s_att, s_att, ALU.mult).then_inc(s_dve.sem, 1)
            for d, k in ((s_q, 0), (s_k, H), (s_v, 2 * H)):
                last = dve.tensor_copy(d.rearrange("p (b h) -> p b h", b=B), qkv[:, k:k + H, T:TT].rearrange("p h b -> p b h"))
            last.then_inc(s_dve.sem, 1)
            s_dve.wait(dve, "s_cols", 1)
            s_act.wait(dve, "sa_rstd", 1)
            dve.scalar_tensor_tensor(mix[:, 0:H, T:TT].rearrange("p h b -> p b h"), s_att.rearrange("p (b h) -> p b h", b=B), hw[:, 0:1],
                                     s_arstd.rearrange("p (b h) -> p b h", b=B), ALU.mult, ALU.mult).then_inc(s_dve.sem, 1)
            s_pe.wait(dve, "ks_full", 1)
            s_act.wait(dve, "s_egs", 1)
            step(dve.tensor_tensor(s_vn, bank[:, 0, 0:U], s_eg, ALU.mult))
            step(dve.tensor_tensor(s_vn, s_v, s_vn, ALU.subtract))
            dve.tensor_tensor(s_vn, s_vn, s_beta, ALU.mult).then_inc(s_dve.sem, 1)
            step(dve.tensor_tensor(sst, sst, s_eg.unsqueeze(2).to_broadcast([P, U, P]), ALU.mult))
            s_act.wait(dve, "row_copied", 1)
            dve.tensor_tensor(vbig, ident[0:U, 0:U].unsqueeze(2).to_broadcast([U, U, P]), srow[:, 0:P].unsqueeze(1).to_broadcast([U, U, P]),
                              ALU.mult).then_inc(s_dve.sem, 1)
            for j in range(8):
                dve.wait_ge(sst_mm, j + 1)
                d = sst[:, 4 * j:4 * j + 4, :]
                dve.tensor_tensor(d, d, bank[:, 3 + j % 4, :].rearrange("p (u e) -> p u e", u=4), ALU.add).then_inc(sst_add, 1)
            dve.wait_ge(so_full, 1)
            dve.tensor_copy(mix[:, H:2 * H, T:TT].rearrange("p h b -> p b h"), bank[:, 0, 0:U].rearrange("p (b h) -> p b h", b=B)).then_inc(s_done, 1)

        on_sq, on_mm, on_log, on_rstd, on_scaled, on_out = l2_sq, l2_mm, l2_log, l2_inv, l2_out, sem("on_out")
        L2 = NCH * 2 * H

        def onorm_pe(pe):
            pe.wait_ge(s_done, 1)
            with pe.Fori(0, H) as i:
                for c in range(NCH):
                    pe.wait_ge(on_sq, i * NCH + (L2 + c + 1))
                    pe.wait_ge(on_log, i * NCH + (L2 + c + 1))
                    pe.matmul(bank[:, 4 + c, 0:CH], ones[:, :], tmp[:, c, :], start=True, stop=True).then_inc(on_mm, 1)

        def onorm_act(act):
            act.wait_ge(s_done, 1)
            with act.Fori(0, H) as i:
                for c in range(NCH):
                    act.wait_ge(on_mm, i * NCH + (L2 + c + 1))
                    act.activation(tmp[:, c, :], vflat[:, ds(i * TT + (4 * TT + c * CH), CH)], ACT.Square).then_inc(on_sq, 1)
                for c in range(NCH):
                    act.wait_ge(on_mm, i * NCH + (L2 + c + 4))
                    act.wait_ge(on_scaled, i * NCH + (L2 + c + 1))
                    act.activation(rstd[:, c, :], bank[:, 4 + c, 0:CH], ACT.Ln, scale=1.0 / P, bias=1e-6).then_inc(on_log, 1)
                for c in range(NCH):
                    act.wait_ge(on_log, i * NCH + (L2 + c + 4))
                    act.activation(rstd[:, c, :], rstd[:, c, :], ACT.Exp, scale=-0.5).then_inc(on_rstd, 1)

        def onorm_dve(dve):
            dve.wait_ge(z_gated, 1)
            with dve.Fori(0, H) as i:
                for c in range(NCH):
                    dve.wait_ge(on_rstd, i * NCH + (L2 + c + 1))
                    d = vflat[:, ds(i * TT + (4 * TT + c * CH), CH)]
                    dve.scalar_tensor_tensor(d, d, hw[:, 1:2], rstd[:, c, :], ALU.mult, ALU.mult).then_inc(on_scaled, 1)
                for c in range(NCH):
                    dve.wait_ge(on_scaled, i * NCH + (L2 + c + 4))
                    d = vflat[:, ds(i * TT + (4 * TT + c * CH), CH)]
                    dve.tensor_tensor(d, d, big[:, ds(i * TT + (12 * TT + c * CH), CH)], ALU.mult).then_inc(on_out, 1)

        g_out = Gemm(g_sems, 2)
        x, xn = res_b, res_a
        xf = rb

        def add_out(dve, g, tile_of, bias=None):
            g.grant(dve, [0, 1])
            with dve.Fori(0, g.rounds) as i:
                for j in range(g.per):
                    g.wait_full(dve, i, j)
                    n, c = tile_of(i, j)
                    d = xf[:, ds(n * TT + c * CH, CH)]
                    if bias is None:
                        dve.tensor_tensor(d, d, bank[:, j % 6, 0:CH], ALU.add).then_inc(g.free[j % 2], 1)
                    else:
                        dve.scalar_tensor_tensor(d, bank[:, j % 6, 0:CH], vecf[:, ds(n * NV + bias, 1)], d, ALU.add, ALU.add).then_inc(g.free[j % 2], 1)
        vecf = vec[:].rearrange("p k v -> p (k v)")

        def four_tiles(i, j):
            return i * 4 + j // NCH, j % NCH

        def two_tiles(i, j):
            return i * 2 + j // NCH, j % NCH

        def out_pe(pe):
            s_dve.wait(pe, "s_mixed", 1)
            pe.wait_ge(on_out, NCH * H)
            project_pe(pe, g_out, mix)
            
        def out_dve(dve):
            dve.wait_ge(x_back, 16)
            add_out(dve, g_out, four_tiles)

        w_out0 = a["w_out"].rearrange("e k n -> (e k) n")

        class Ffn:
            UP, ROUND = 12, 12 + KD * NCH

            def __init__(self, layer, nn):
                self.layer, self.nn = layer, nn
                self.gemm = self.down = Gemm(g_sems, KF // 2, (self.ROUND - 1,) * 4)
                self.units0 = layer * 6 * (KF // 2)
                self.hid0 = layer * 6 * (KF // 2)

        HID = KD * TT
        SPL = HID + 4 * TT
        xh = rounded("xh", "res_a", 0, [P, KD, TT])
        xl = rounded("xl", "big", 0, [P, KD, TT])
        x_scaled = flat(0, KD, TT)
        hh = rounded("hh", "big", HID, [P, 2, TT])
        hl = rounded("hl", "big", HID + 2 * TT, [P, 2, TT])
        WQ = 3
        wflat = wring[:].rearrange("p s k n -> p (s k n)")
        raw_w = [wflat[:, r * D:(r + 1) * D] for r in range(WQ)]
        wh = [rounded(f"wh{u}", "big", SPL + u * 2 * D, [P, D]) for u in range(5)] + [rounded("wh5", "wring", WQ * D, [P, D])]
        wl = [rounded(f"wl{u}", "big", SPL + u * 2 * D + D, [P, D]) for u in range(5)] + [rounded("wl5", "wring", (WQ + 1) * D, [P, D])]
        raw_in = [sem(f"raw_in{r}") for r in range(WQ)]
        wh_done, w_cut = sem("wh_done"), sem("w_cut")
        xh_done, x_cut = sem("xh_done"), sem("x_cut")
        hid_cut = sem("hid_cut")

        f0 = Ffn(0, 1)

        def pair_pe(pe, g, xin):
            with pe.Fori(0, g.rounds) as i:
                for t in range(2):
                    wait_slab(pe, i, 2 * t)
                    wait_slab(pe, i, 2 * t + 1)
                    for c in range(NCH):
                        for u in range(2):
                            job(pe, g, i, 6 * t + 2 * c + u, [(2 * t + u, KD)], lambda k, j, c=c: xin[:, k, chunk(c)])
            w_rounds[1] += g.rounds

        def ffn_sp(sp, f, before):
            wg, wu, wd = (a[n][f.layer] for n in ("ffn_w_gate", "ffn_w_up", "ffn_w_down"))
            before.wait_full(sp, before.rounds - 1, before.per - 1)

            def unit(i, u, first=False):
                if not first:
                    sp.wait_ge(w_cut, i * 6 + (f.units0 + u - WQ + 1))
                if u < 4:
                    src, dst = cols((wg, wu)[u % 2], i * 2 + u // 2), raw_w[u % WQ].rearrange("p (k n) -> p k n", k=KD)
                else:
                    src, dst = wd[ds(i * (2 * P) + (u - 4) * P, P), :], raw_w[u % WQ]
                sp.dma_start(dst, src).then_inc(raw_in[u % WQ], 16)

            for u in range(6):
                unit(0, u, f.layer == 0 and u < WQ)
            with sp.Fori(1, KF // 2) as i:
                for u in range(6):
                    unit(i, u)

        def cut_products(pe, bank_out, terms, done):
            for n, (h, l, mh, ml) in enumerate(terms):
                pe.matmul(bank_out, h, mh, start=(n == 0), stop=False)
                pe.matmul(bank_out, h, ml, start=False, stop=False)
                mm = pe.matmul(bank_out, l, mh, start=False, stop=(n == len(terms) - 1))
            mm.then_inc(done, 1)

        def ffn_pe(pe, f):
            norm_pe(pe, f.nn)
            g = f.gemm
            with pe.Fori(0, g.rounds) as i:
                for t in range(2):
                    for c in range(NCH):
                        if t == 0:
                            pe.wait_ge(x_cut, NCH * f.layer + c + 1)
                        for u in range(2):
                            if c == 0:
                                pe.wait_ge(w_cut, i * 6 + (f.units0 + 2 * t + u + 1))
                            j, s = 6 * t + 2 * c + u, 2 * t + u
                            g.wait_bank(pe, i, j)
                            cut_products(pe, bank[:, j % 6, 0:CH], [(wh[s][:, k * P:(k + 1) * P], wl[s][:, k * P:(k + 1) * P],
                                         xh[:, k, chunk(c)], xl[:, k, chunk(c)]) for k in range(KD)], g.full)
                pe.wait_ge(w_cut, i * 6 + (f.units0 + 6))
                for c in range(NCH):
                    pe.wait_ge(hid_cut, i * 6 + (f.hid0 + 3 + NCH + c + 1))
                    for n in range(KD):
                        j = f.UP + KD * c + n
                        g.wait_bank(pe, i, j)
                        cut_products(pe, bank[:, j % 6, 0:CH], [(wh[4 + k][:, n * P:(n + 1) * P], wl[4 + k][:, n * P:(n + 1) * P],
                                     hh[:, k, chunk(c)], hl[:, k, chunk(c)]) for k in range(2)], g.full)

        def ffn_act(act, f, before):
            before.wait_all_read(act)
            if f.layer:
                act.wait_ge(misc_out, 16 * STORES)

            def cut(i, u):
                act.wait_ge(raw_in[u % WQ], i * 32 + 16 * (f.units0 // WQ + u // WQ + 1))
                act.activation(wh[u][:, :], raw_w[u % WQ], ACT.Copy).then_inc(wh_done, 1)

            def gates(i, t):
                for c in range(NCH):
                    g.wait_full(act, i, 6 * t + 2 * c)
                    act.wait_ge(hid_cut, i * 6 + (f.hid0 + NCH * t + c + 1))
                    act.activation(tmp[:, c, :], bank[:, 2 * c, 0:CH], ACT.Silu).then_inc(g.free[0], 1)

            g = f.gemm
            before.wait_full(act, before.rounds - 1, before.per - 1)
            for u in range(4):
                cut(0, u)
            norm_act(act, f.nn, x, copy=lambda c: stream_high(act, f, c))
            act.wait_ge(n_mm, KD * NCH * (f.nn + 1))

            def body(i, last):
                g.wait_full(act, i, -1)
                cut(i, 4)
                cut(i, 5)
                g.wait_read(act, i, -2)
                gates(i, 0)
                if not last:
                    g.wait_full(act, i, 5)
                    cut(i + 1, 0)
                    cut(i + 1, 1)
                gates(i, 1)
                if not last:
                    g.wait_full(act, i, 11)
                    cut(i + 1, 2)
                    cut(i + 1, 3)

            with act.Fori(0, g.rounds - 1) as i:
                body(i, False)
            body(g.rounds - 1, True)

        def stream_high(act, f, c):
            act.wait_ge(n_out, KD * (NCH * f.nn + c + 1))
            act.activation(xh[:, :, chunk(c)], x_scaled[:, :, chunk(c)], ACT.Copy).then_inc(xh_done, 1)

        def ffn_pool(pool, f):
            def cut(i, u):
                pool.wait_ge(wh_done, i * 6 + (f.units0 + u + 1))
                pool.tensor_tensor(wl[u][:, :], raw_w[u % WQ], wh[u][:, :].bitcast(F32), ALU.subtract).then_inc(w_cut, 1)

            for u in range(4):
                cut(0, u)
            for c in range(NCH):
                pool.wait_ge(xh_done, NCH * f.layer + c + 1)
                pool.tensor_tensor(xl[:, :, chunk(c)], x_scaled[:, :, chunk(c)], xh[:, :, chunk(c)].bitcast(F32), ALU.subtract).then_inc(x_cut, 1)
            cut(0, 4)
            cut(0, 5)
            with pool.Fori(1, KF // 2) as i:
                for u in range(6):
                    cut(i, u)

        def ffn_dve(dve, f, before, step):
            before.wait_all_read(dve)
            if f.layer:
                dve.wait_ge(misc_out, 16 * STORES)
            norm_dve(dve, f.nn, x, x_scaled, V_FFN0 + f.layer)
            g = f.gemm
            if f.layer == 0:
                dve.sem_inc(hid_cut, 3)
            with dve.Fori(0, g.rounds) as i:
                step.enter(i, 6)
                for t in range(2):
                    for c in range(NCH):
                        g.wait_full(dve, i, 6 * t + 2 * c + 1)
                        g.wait_pair(dve, i, 6 * t + 2 * c, 0)
                        dve.tensor_tensor(tmp[:, c, :], bank[:, 2 * c + 1, 0:CH], tmp[:, c, :], ALU.mult).then_inc(g.free[1], 1)
                        g.wait_pair(dve, i, 6 * t + 2 * c, 1)
                        step(dve.tensor_copy(hh[:, t, chunk(c)], tmp[:, c, :]))
                        dve.tensor_tensor(hl[:, t, chunk(c)], tmp[:, c, :], hh[:, t, chunk(c)].bitcast(F32), ALU.subtract).then_inc(hid_cut, 1)
                for c in range(NCH):
                    for n in range(KD):
                        j = f.UP + KD * c + n
                        g.wait_full(dve, i, j)
                        dve.tensor_tensor(x[:, n, chunk(c)], x[:, n, chunk(c)], bank[:, j % 6, 0:CH], ALU.add).then_inc(g.free[j % 2], 1)
            step.leave(g.rounds)

        g_pw1 = Gemm(g_sems, 4, (4, 5, 10, 11))
        g_pw2 = Gemm(g_sems, 2)
        f1 = Ffn(1, 4)
        w_pw1 = a["conv_w_pw1"].rearrange("e k n -> (e k) n")
        w_pw2 = a["conv_w_pw2"].rearrange("e k n -> (e k) n")
        HIST = CW - 1
        glu = flat(0, KD, GL)
        cout = flat(KD * GL, KD, TT)
        coutf = big[:, KD * GL:KD * (GL + TT)]
        C1 = KD * (GL + TT)
        shist = flat(C1, KD, B, HIST)
        ssum8 = flat(C1 + KD * B * HIST, KD, B)
        C2 = C1 + KD * B * HIST + KD * B
        srows2 = flat(C2, 2, D, parts=B * HIST // 2)
        wprod = flat(C2, 2, T)
        wacc = flat(C2 + 2 * T, T)
        NPOOL = 10
        TAPS = CW - NPOOL
        crow = flat(C2, D, parts=HIST + B)
        hist_zero, hist_in, hist_full, hist_copied = (sem(x) for x in ("hist_zero", "hist_in", "hist_full", "hist_copied"))
        tap_in, tap_added, tile_conv = sem("tap_in"), sem("tap_added"), sem("tile_conv")
        crow_full, crow_copied, samples_conv = sem("crow_full"), sem("crow_copied"), sem("samples_conv")
        mu_full, mu_in, centred, ln_silu = sem("mu_full"), sem("mu_in"), sem("centred"), sem("ln_silu")

        def conf_pool(pool, step):
            f0.down.wait_all_read(pool)
            for u in range(2):
                src = a["state_conv_buf"].rearrange("e b w d -> (e b w) d")[120 * u:120 * (u + 1), :]
                pool.dma_start(srows2[:, u, :], src).then_inc(hist_in, 16)
            pool.wait_ge(hist_full, 1)
            pool.sem_inc(tap_added, 2)
            with pool.Fori(0, KD) as n:
                step.enter(n, NPOOL - 1)
                for q in range(NPOOL - 1):
                    pool.wait_ge(tap_in, n * NPOOL + q + 2)
                    step(pool.tensor_tensor(wacc, wacc, wprod[:, q % 2, :], ALU.add))
                    pool.sem_inc(tap_added, 1)
            step.leave(KD)
            pool.wait_ge(crow_copied, 2)
            store(pool, o["new_conv_buf_prompt"].rearrange("e b w c -> (e b w) c"), crow[0:HIST, :])
            store(pool, o["new_conv_buf_sample"][0, :, HIST - 1, :], crow[HIST:HIST + B, :])

        def conf_pe(pe):
            norm_pe(pe, 2)
            pe.wait_ge(hist_in, 32)
            for u in range(2):
                for k in range(KD):
                    mm = pe.transpose(bank[:, 2 * u + k // 4, k % 4 * 120:(k % 4 + 1) * 120], srows2[:, u, k * P:(k + 1) * P], ident[0:120, 0:120])
            mm.then_inc(hist_full, 1)
            pe.wait_ge(hist_copied, 4)
            pe.wait_ge(n_out, NCH * KD * 3)
            pair_pe(pe, g_pw1, xn)
            g_pw1.wait_all_read(pe)
            for k in range(KD):
                mm = pe.transpose(bank[0:HIST + B, k // 4, k % 4 * P:(k % 4 + 1) * P], glu[:, k, T:GL], ident[:, :])
            mm.then_inc(crow_full, 1)
            pe.wait_ge(tile_conv, KD)
            pe.wait_ge(samples_conv, 1)
            for c in range(NCH):
                for k in range(KD):
                    mm = pe.matmul(bank[:, 2 + c, 0:CH], ones[:, :], cout[:, k, chunk(c)], start=(k == 0), stop=(k == KD - 1))
                mm.then_inc(mu_full, 1)
            norm_pe(pe, 3)
            pe.wait_ge(crow_copied, 2)
            pe.wait_ge(ln_silu, NCH * KD)
            project_pe(pe, g_pw2, cout)

        def conf_act(act):
            f0.down.wait_all_read(act)
            norm_act(act, 2, x)
            act.wait_ge(hist_full, 1)
            for u in range(2):
                for v in range(2):
                    d = shist[:, 4 * v:4 * v + 4, :, :].rearrange("p k b w -> p k (b w)")[:, :, 120 * u:120 * u + 120]
                    act.activation(d, bank[:, 2 * u + v, 0:480].rearrange("p (k r) -> p k r", k=4), ACT.Copy).then_inc(hist_copied, 1)
            g = g_pw1
            g.grant(act, [0])
            act.wait_ge(n_mm, KD * NCH * 3)

            def taps(n, q0, q1):
                for q in range(q0, q1):
                    src = big[:, ds(n * GL + (TAPS + q), T)]
                    w = vecf[:, ds(n * NV + (V_WDW + TAPS + q), 1)]
                    if q == 0:
                        act.wait_ge(tile_conv, n)
                        act.sem_inc(wait_carrier, 1)
                        act.activation(wacc, src, ACT.Copy, scale=w).then_inc(tap_in, 1)
                    else:
                        act.wait_ge(tap_added, n * (NPOOL - 1) + q)
                        act.sem_inc(wait_carrier, 1)
                        act.activation(wprod[:, (q - 1) % 2, :], src, ACT.Copy, scale=w).then_inc(tap_in, 1)

            def gate(i, t, c):
                g.wait_full(act, i, 6 * t + 2 * c)
                g.wait_pair(act, i, 6 * t + 2 * c - 6, 1)
                act.sem_inc(wait_carrier, 1)
                act.activation(tmp[:, c, :], bank[:, 2 * c, 0:CH], ACT.Sigmoid, bias=vecf[:, ds(i * (2 * NV) + (t * NV + V_BG), 1)]).then_inc(g.free[0], 1)

            for t in range(2):
                for c in range(NCH):
                    gate(0, t, c)
                    if t == 1:
                        g.wait_pair(act, 0, 4, 1)
                        act.wait_ge(hist_zero, 1)
                        taps0(act, taps, c)
            with act.Fori(1, g.rounds) as i:
                for t in range(2):
                    for c in range(NCH):
                        gate(i, t, c)
                        g.wait_pair(act, i, 6 * t - 2, 1)
                        taps(i * 2 + (t - 1), *SPLIT[c])
            g.wait_all_read(act)
            taps(KD - 1, 0, NPOOL)
            act.wait_ge(crow_full, 1)
            act.wait_ge(tap_added, 2 + KD * (NPOOL - 1))
            act.wait_ge(tile_conv, KD)
            for u in range(2):
                act.activation(crow[:, 512 * u:512 * (u + 1)], bank[0:HIST + B, u, :], ACT.Copy).then_inc(crow_copied, 1)
            for c in range(NCH):
                act.wait_ge(mu_full, c + 1)
                act.activation(rstd[:, c, :], bank[:, 2 + c, 0:CH], ACT.Copy, scale=1.0 / D).then_inc(mu_in, 1)
            act.wait_ge(centred, NCH * KD)
            norm_act(act, 3, cout, LN_EPS)
            for c in range(NCH):
                for k in range(KD):
                    act.wait_ge(n_out, KD * (3 * 3 + c) + k + 1)
                    act.activation(cout[:, k, chunk(c)], cout[:, k, chunk(c)], ACT.Silu, bias=vcol(V_LB, k)).then_inc(ln_silu, 1)

        SPLIT = [(0, 4), (4, 7), (7, NPOOL)]

        def taps0(act, taps, c):
            taps_first(act, *SPLIT[c])

        def taps_first(act, q0, q1):
            for q in range(q0, q1):
                src, w = glu[:, 0, TAPS + q:TAPS + q + T], vec[:, 0, V_WDW + TAPS + q:V_WDW + TAPS + q + 1]
                if q == 0:
                    act.activation(wacc, src, ACT.Copy, scale=w).then_inc(tap_in, 1)
                else:
                    act.wait_ge(tap_added, q)
                    act.activation(wprod[:, (q - 1) % 2, :], src, ACT.Copy, scale=w).then_inc(tap_in, 1)

        def conf_dve(dve, step):
            f0.down.wait_all_read(dve)
            norm_dve(dve, 2, x, xn, V_MIX1)
            dve.memset(glu[:, :, 0:HIST], 0.0).then_inc(hist_zero, 1)
            dve.wait_ge(hist_copied, 4)
            wd = vec[:, :, V_WDW:V_WDW + HIST].unsqueeze(2).to_broadcast([P, KD, B, HIST])
            step(dve.tensor_tensor(shist, shist, wd, ALU.mult))
            step(dve.tensor_reduce(ssum8, shist, AX.X, ALU.add))
            g = g_pw1
            g.grant(dve, [1])

            def glu_job(i, t, c):
                g.wait_full(dve, i, 6 * t + 2 * c + 1)
                g.wait_pair(dve, i, 6 * t + 2 * c, 0)
                dve.scalar_tensor_tensor(big[:, ds(i * (2 * GL) + (t * GL + HIST + c * CH), CH)], bank[:, 2 * c + 1, 0:CH],
                                         vecf[:, ds(i * (2 * NV) + (t * NV + V_BA), 1)], tmp[:, c, :], ALU.add, ALU.mult).then_inc(g.free[1], 1)

            def conv(n, q0, q1):
                d = big[:, ds(n * TT + KD * GL, T)]
                for q in range(q0, min(q1, TAPS)):
                    src = big[:, ds(n * GL + q, T)]
                    w = vecf[:, ds(n * NV + (V_WDW + q), 1)]
                    if q == 0:
                        step(dve.tensor_scalar(d, src, w, vecf[:, ds(n * NV + V_BDW, 1)], ALU.mult, ALU.add))
                    else:
                        step(dve.scalar_tensor_tensor(d, src, w, d, ALU.mult, ALU.add))
                if q1 > TAPS:
                    dve.wait_ge(tap_added, n * (NPOOL - 1) + (NPOOL - 1 + 2))
                    dve.tensor_tensor(d, d, wacc, ALU.add).then_inc(tile_conv, 1)

            PARTS = [(0, TAPS // 3), (TAPS // 3, 2 * TAPS // 3), (2 * TAPS // 3, TAPS + 1)]
            dve.wait_ge(hist_zero, 1)
            for t in range(2):
                for c in range(NCH):
                    glu_job(0, t, c)
                    if t == 1:
                        if c == 0:
                            g.wait_pair(dve, 0, 4, 1)
                        conv(0, *PARTS[c])
            with dve.Fori(1, g.rounds) as i:
                step.enter(i - 1, 2 * TAPS)
                for t in range(2):
                    for c in range(NCH):
                        glu_job(i, t, c)
                        if c == 0:
                            g.wait_pair(dve, i, 6 * t - 2, 1)
                        conv(i * 2 + (t - 1), *PARTS[c])
            step.leave(g.rounds - 1)
            g.wait_all_read(dve)
            conv(KD - 1, 0, TAPS + 1)
            snew_ = glu[:, :, HIST + T:GL]
            wl = vec[:, :, V_WDW + HIST].unsqueeze(2).to_broadcast([P, KD, B])
            cs = cout[:, :, T:TT]
            step(dve.tensor_tensor(cs, snew_, wl, ALU.mult))
            step(dve.tensor_tensor(cs, cs, ssum8, ALU.add))
            dve.tensor_tensor(cs, cs, vec[:, :, V_BDW].unsqueeze(2).to_broadcast([P, KD, B]), ALU.add).then_inc(samples_conv, 1)
            for c in range(NCH):
                dve.wait_ge(mu_in, c + 1)
                for k in range(KD):
                    dve.tensor_tensor(cout[:, k, chunk(c)], cout[:, k, chunk(c)], rstd[:, c, :], ALU.subtract).then_inc(centred, 1)
            dve.wait_ge(centred, NCH * KD)
            norm_dve(dve, 3, cout, cout, V_LG)
            add_out(dve, g_pw2, four_tiles, V_BPW2)

        y_full, y_copied = sem("y_full"), [sem("y_copied0"), sem("y_copied1")]
        y_out = [sem("y_out0"), sem("y_out1")]
        yrow = flat(0, 2, D)

        def final_pe(pe):
            norm_pe(pe, 5)
            for n in range(NB + 1):
                pe.wait_ge(n_out, KD * (3 * 5) + KD * min(NCH, 1 + min(TT - 1, (n + 1) * P - 1) // CH))
                if n >= 2:
                    for e in range(2):
                        pe.wait_ge(y_copied[e], n - 1)
                w = P if n < NB else B
                for k in range(KD):
                    mm = pe.transpose(bank[0:w, 2 * (n % 2) + k // 4, k % 4 * P:(k % 4 + 1) * P], xn[:, k, n * P:n * P + w], ident[:, :])
                mm.then_inc(y_full, 1)

        def final_copy(eng, e):
            for n in range(NB + 1):
                w = P if n < NB else B
                eng.wait_ge(y_full, n + 1)
                if n >= 2:
                    eng.wait_ge(y_out[n % 2], 16 * (n // 2))
                s, d = bank[0:w, 2 * (n % 2) + e, :], yrow[0:w, n % 2, 512 * e:512 * (e + 1)]
                if e == 0:
                    eng.activation(d, s, ACT.Copy).then_inc(y_copied[e], 1)
                else:
                    eng.tensor_copy(d, s).then_inc(y_copied[e], 1)

        def final_sp(sp):
            yp = o["y_prompt"].rearrange("o (n p) d -> (o n) p d", p=P)
            for n in range(NB + 1):
                for e in range(2):
                    sp.wait_ge(y_copied[e], n + 1)
                if n < NB:
                    sp.dma_start(yp[n], yrow[:, n % 2, :]).then_inc(y_out[n % 2], 16)
                else:
                    sp.dma_start(o["y_sample"].rearrange("b o d -> (b o) d"), yrow[0:B, n % 2, :]).then_inc(y_out[n % 2], 16)
            sp.wait_ge(y_out[0], 16 * (NB // 2 + 1))
            sp.wait_ge(y_out[1], 16 * (NB // 2))

        def pe_rest(pe):
            kv_pe(pe)
            att_pe(pe)
            gdn_in_pe(pe)
            sm_pe(pe)
            l2_pe(pe)
            gate_pe(pe)
            chunk_pe(pe)
            sample_pe(pe)
            onorm_pe(pe)
            out_pe(pe)
            ffn_pe(pe, f0)
            conf_pe(pe)
            ffn_pe(pe, f1)
            final_pe(pe)

        def act_rest(act, step):
            kv_act(act)
            att_act(act, step)
            gdn_in_act(act)
            sm_act(act)
            l2_act(act)
            gate_act_fn(act)
            chunk_act(act)
            sample_act(act)
            onorm_act(act)
            ffn_act(act, f0, g_out)
            conf_act(act)
            ffn_act(act, f1, g_pw2)
            f1.down.wait_all_read(act)
            norm_act(act, 5, x)
            final_copy(act, 0)

        def dve_rest(dve, step):
            kv_dve(dve)
            att_dve(dve, step)
            gdn_in_dve(dve, step)
            sm_dve(dve, step)
            l2_dve(dve)
            gate_dve(dve, step)
            chunk_dve(dve, step)
            sample_dve(dve, step)
            onorm_dve(dve)
            out_dve(dve)
            ffn_dve(dve, f0, g_out, step)
            conf_dve(dve, step)
            ffn_dve(dve, f1, g_pw2, step)
            f1.down.wait_all_read(dve)
            norm_dve(dve, 5, x, xn, V_FIN)
            final_copy(dve, 1)

        def sp_rest(sp):
            gdn_in_sp(sp)
            chunk_sp(sp)
            stream(sp, g_out, lambda i, s: cols(w_out0, i * 4 + s), g_gdn)
            ffn_sp(sp, f0, g_out)
            stream(sp, g_pw1, lambda i, s: cols(w_pw1, i * 2 + (s // 2 + KD * (1 - s % 2))), f0.down)
            stream(sp, g_pw2, lambda i, s: cols(w_pw2, i * 4 + s), g_pw1)
            ffn_sp(sp, f1, g_pw2)
            final_sp(sp)

        def pool_rest(pool, step):
            kv_pool(pool)
            att_pool(pool)
            pool.wait_ge(v_out, 16 * NB)
            gdn_in_pool(pool)
            pool.sem_inc(qdec_done, 1)
            chunk_pool(pool)
            sample_pool(pool)
            ffn_pool(pool, f0)
            conf_pool(pool, step)
            ffn_pool(pool, f1)
            pool.wait_ge(misc_out, 16 * STORES)

        @blk.sync
        def _(sp):
            sp_part1(sp)
            sp_rest(sp)

        @blk.tensor
        def _(pe):
            pe_part1(pe)
            pe_rest(pe)

        @blk.scalar
        def _(act):
            step = Chain(act, act_step)
            act_part1(act)
            act_rest(act, step)

        @blk.vector
        def _(dve):
            step = Chain(dve, dve_step)
            dve_part1(dve, step)
            dve_rest(dve, step)

        @blk.gpsimd
        def _(pool):
            step = Chain(pool, pool_step)
            pool_part1(pool, step)
            pool_rest(pool, step)


INS = ["x_prompt", "x_sample", "cache_attn_k", "cache_attn_v", "page_table", "state_gdn_conv", "state_gdn_s",
       "state_conv_buf", "norm_mix", "norm_ffn", "norm_final", "w_in", "w_out", "gdn_conv_w", "gdn_A_log",
       "gdn_dt_bias", "gdn_norm_w", "lam_q1", "lam_k1", "lam_q2", "lam_k2", "diff_subln_w", "rel_bias",
       "conv_w_pw1", "conv_b_pw1", "conv_w_dw", "conv_b_dw", "conv_ln_g", "conv_ln_b", "conv_w_pw2",
       "conv_b_pw2", "ffn_w_gate", "ffn_w_up", "ffn_w_down"]
OUTS = [("y_prompt", (1, T, D)), ("y_sample", (B, 1, D)), ("new_k_prompt", (1, 1, T, H, P)), ("new_v_prompt", (1, 1, T, H, P)),
        ("new_k_sample", (1, B, 1, H, P)), ("new_v_sample", (1, B, 1, H, P)), ("new_gdn_conv_prompt", (1, 1, GW - 1, CQ)),
        ("new_gdn_conv_sample", (1, B, GW - 1, CQ)), ("new_gdn_s_prompt", (1, 1, H, P, P)), ("new_gdn_s_sample", (1, B, H, P, P)),
        ("new_conv_buf_prompt", (1, 1, CW - 1, D)), ("new_conv_buf_sample", (1, B, CW - 1, D))]


def kernel(**inputs):
    import concourse.bacc as bacc
    from concourse.bass_utils import run_bass_kernel_spmd
    nc = bacc.Bacc("TRN2", target_bir_lowering=False, num_devices=1)
    arrays, a = {}, {}
    for name, v in {**{n: inputs[n] for n in INS}, **shape_constants()}.items():
        v = np.ascontiguousarray(v)
        arrays[f"in_{name}"] = v
        a[name] = nc.dram_tensor(f"in_{name}", v.shape, mybir.dt.from_np(v.dtype), kind="ExternalInput").ap()
    o = {name: nc.dram_tensor(f"out_{name}", shape, F32, kind="ExternalOutput").ap() for name, shape in OUTS}
    build(nc, a, o)
    r = run_bass_kernel_spmd(nc, [arrays], core_ids=[0])
    return tuple(r.results[0][f"out_{name}"] for name, _ in OUTS)
```

```python
import math
from contextlib import ExitStack

import numpy as np

import concourse.bass as bass
from concourse import mybir

F32, I32, U8, F32R = mybir.dt.float32, mybir.dt.int32, mybir.dt.uint8, mybir.dt.float32r
ALU = mybir.AluOpType
ACT = mybir.ActivationFunctionType
AX = mybir.AxisListType
ds = bass.ds

P = 128
D = 1024
KD = D // P
T = 1024
NB = T // P
B = 8
TT = T + B
NCH = 3
CH = TT // NCH
H = 4
DA = 64
FF = 2816
KF = FF // P
SLAB = KF // 2
CW = 31
GW = 4
CQ = 1536
PAST = 2048
PG = 16
NBUCKET, MAXD = 32, 128
NEG = -1e30
LN_EPS = 1e-5
LAM0 = 0.8 - 0.6 * math.exp(-0.3 * 0)
LEVELS = 7
GL = T + CW - 1 + B

V_MIX0, V_MIX1, V_FFN0, V_FFN1, V_FIN, V_BA, V_BG, V_BDW, V_LG, V_LB, V_BPW2, V_WDW = range(12)
NV = V_WDW + CW


def bucket(n):
    exact = NBUCKET // 2
    if n < exact:
        return n
    return min(exact + int(math.log(n / exact) / math.log(MAXD / exact) * (NBUCKET - exact) + 1e-9), NBUCKET - 1)


def shape_constants():
    i = np.arange(P)
    ident = np.eye(P, dtype=np.float32)
    triu = (i[:, None] <= i[None, :]).astype(np.float32)
    causal = np.where(i[None, :] >= i[:, None], 0.0, NEG).astype(np.float32)
    merge = np.zeros((P, 2, LEVELS, P), np.int32)
    for lv in range(LEVELS):
        s = 1 << lv
        m = (i[:, None] // (2 * s) == i[None, :] // (2 * s)) & (i[:, None] // s % 2 == 1) & (i[None, :] // s % 2 == 0)
        merge[:, 0, lv] = m
        merge[:, 1, lv] = m.T
    hot = np.zeros((NBUCKET, 384), np.float32)
    for m in range(256):
        hot[bucket(255 - m), m] = 1
    hots = np.zeros((NBUCKET, 3, P), np.float32)
    for r in range(P):
        hots[bucket(P - r), 0, r] = 1
        hots[NBUCKET - 1, 1, r] = 1
        hots[0, 2, r] = 1
    halves = np.zeros((P, 2, P), np.float32)
    halves[:DA, 0] = 1
    halves[DA:, 1] = 1
    return dict(c_ident=ident, c_triu=triu, c_causal=causal, c_merge=merge.reshape(P, -1), c_hot=hot,
                c_hots=hots.reshape(NBUCKET, -1), c_halves=halves.reshape(P, -1))


class Chain:

    def __init__(self, eng, sem):
        self.eng, self.sem, self.n, self.i, self.per = eng, sem, 0, None, 0

    def __call__(self, ins):
        ins.then_inc(self.sem, 1)
        self.n += 1
        self.eng.wait_ge(self.sem, self.n if self.i is None else self.i * self.per + self.n)

    def lagged(self, ins):
        ins.then_inc(self.sem, 1)
        self.n += 1
        self.eng.wait_ge(self.sem, self.n - 1 if self.i is None else self.i * self.per + (self.n - 1))

    def settle(self):
        self.eng.wait_ge(self.sem, self.n if self.i is None else self.i * self.per + self.n)

    def enter(self, i, per_round):
        self.i, self.per, self.start = i, per_round, self.n

    def leave(self, rounds):
        assert self.n - self.start == self.per, (self.n - self.start, self.per)
        self.n = self.start + rounds * self.per
        self.i = None


class Marks:

    def __init__(self, sem, **steps):
        self.sem, self.steps = sem, steps

    def wait(self, eng, name, n=1):
        before = list(self.steps)[:list(self.steps).index(name)]
        eng.wait_ge(self.sem, sum(self.steps[x] for x in before) + n)


class Gemm:

    def __init__(self, sems, rounds, last=(2, 5, 8, 11)):
        self.full, self.free = sems["full"], sems["free"]
        self.last = last
        self.per, self.rounds = last[3] + 1, rounds
        self.jobs0 = sems["jobs"]
        sems["jobs"] += self.per * rounds

    def grant(self, eng, parities):
        if self.jobs0 == 0:
            for p in parities:
                eng.sem_inc(self.free[p], 3)

    def wait_bank(self, pe, i, j):
        pe.wait_ge(self.free[j % 2], i * (self.per // 2) + (self.jobs0 // 2 + j // 2 + 1))

    def wait_full(self, eng, i, j):
        eng.wait_ge(self.full, i * self.per + (self.jobs0 + j + 1))

    def wait_read(self, eng, i, j):
        self.wait_pair(eng, i, j, j % 2)

    def wait_pair(self, eng, i, j, parity):
        eng.wait_ge(self.free[parity], i * (self.per // 2) + (self.jobs0 // 2 + j // 2 + 4))

    def wait_all_read(self, eng):
        for p in (0, 1):
            eng.wait_ge(self.free[p], 3 + (self.jobs0 + self.rounds * self.per) // 2)


def build(nc, a, o):
    with ExitStack() as ctx:
        def sb(name, shape, dt=F32):
            return ctx.enter_context(nc.sbuf_tensor(name, shape, dt))

        def sem(name):
            return ctx.enter_context(nc.semaphore(name))

        bank = ctx.enter_context(nc.psum_tensor("bank", [P, 8, 512], F32))
        place = {"res_a": -(-nc.sbuf_base // 32) * 32}
        res_a = sb("res_a", [P, KD, TT])
        res_b = sb("res_b", [P, KD, TT])
        place["big"] = -(-nc.sbuf_base // 32) * 32
        big = sb("big", [P, KF * TT])
        place["wring"] = -(-nc.sbuf_base // 32) * 32
        wring = sb("wring", [P, 4, SLAB, P])

        def rounded(name, where, off, shape):
            return nc.alloc_sbuf_tensor_at(name, shape, F32R, offset=place[where] + 4 * off)
        tmp = sb("tmp", [P, 4, CH])
        rstd = sb("rstd", [P, NCH, CH])
        ident = sb("ident", [P, P])
        ones = sb("ones", [P, P])
        triu = sb("triu", [P, P])
        causal = sb("causal", [P, P])
        merge = sb("merge", [P, 2, LEVELS, P], U8)
        halves = sb("halves", [P, 2, P])
        vec = sb("vec", [P, KD, NV])
        gcw = sb("gcw", [P, 12, GW])
        gst = sb("gst", [P, 12, B, GW - 1])
        sbias = sb("sbias", [P, 3, H])
        gate0 = sb("gate0", [P, 2, H])
        hw = sb("hw", [P, 2])
        lam = sb("lam", [P, 8])
        pages = sb("pages", [1, P], I32)
        aw = sb("aw", [P, B, PG, H])
        gnew = sb("gnew", [P, 12, GW - 1 + B])
        wba = sb("wba", [P, KD, 2 * H])
        sq = sb("sq", [P, 12, B])
        probs = sb("probs", [P, B, PG, 2 * H])
        state = sb("state", [P, H, P])
        small = sb("small", [P, 512])
        park = nc.dram_tensor("park", (P, KD * TT), F32, kind="Internal")
        brow = nc.dram_tensor("brow", (P, H, 384), F32, kind="Internal")

        def tiles(n0, n):
            return big[:, n0 * TT:(n0 + n) * TT].rearrange("p (n t) -> p n t", n=n)

        def flat(off, *shape, parts=P):
            n = int(np.prod(shape))
            v = big[0:parts, off:off + n]
            names = "abc"[:len(shape)]
            if len(shape) == 1:
                return v
            return v.rearrange(f"p ({' '.join(names)}) -> p {' '.join(names)}", **{k: s for k, s in zip(names[1:], shape[1:])})

        def vcol(v, k):
            return vec[:, k, v:v + 1]

        xrows = flat(8192, NB, D)
        vrows = flat(0, D, parts=NV)
        grows = flat(1024, CQ, parts=GW)
        srows = flat(2560, CQ, parts=B * (GW - 1))
        hot = flat(4096, 384, parts=NBUCKET)
        hots = flat(4480, 3, P, parts=NBUCKET)
        xsrows = flat(4864, D, parts=B)
        rel = flat(5888, H, parts=NBUCKET)
        merge_words = flat(16384, 2 * LEVELS * P).bitcast(I32)
        lamv = flat(5892, 4, parts=DA)
        lamp = flat(5896, 2, parts=DA)
        bsb = small[0:H, 0:384]

        x_in = [sem("x_in0"), sem("x_in1")]
        ident_in, const_in = sem("ident_in"), sem("const_in")
        ones_set = sem("ones_set")
        xt_full = sem("xt_full")
        xt_act = sem("xt_act")
        xt_dve = sem("xt_dve")
        set_mm = sem("set_mm")
        lam_prod = sem("lam_prod")
        set_dve = sem("set_dve")
        lam_exp = sem("lam_exp")
        bias_io = sem("bias_io")
        dve_step, pool_step = sem("dve_step"), sem("pool_step")

        w_in = [sem(f"w_in{s}") for s in range(4)]
        w_rounds = [0, 0]

        n_act, n_dve = sem("n_act"), sem("n_dve")
        n_mm = sem("n_mm")
        n_log = sem("n_log")
        n_rstd = sem("n_rstd")
        n_out = sem("n_out")

        def chunk(c):
            return slice(c * CH, (c + 1) * CH)

        def norm_pe(pe, nn):
            for c in range(NCH):
                q = 3 * nn + c
                if q >= 2:
                    pe.wait_ge(n_log, q - 1)
                for k in range(KD):
                    pe.wait_ge((n_act, n_dve)[k % 2], 4 * q + k // 2 + 1)
                    pe.matmul(bank[:, 6 + q % 2, 0:CH], ones[:, :], tmp[:, k % 4, :],
                              start=(k == 0), stop=(k == KD - 1)).then_inc(n_mm, 1)

        def norm_squares(eng, nn, c, x, par):
            for k in range(par, KD, 2):
                m = KD * (3 * nn + c) + k
                if m >= 4:
                    eng.wait_ge(n_mm, m - 3)
                if par == 0:
                    eng.activation(tmp[:, k % 4, :], x[:, k, chunk(c)], ACT.Square).then_inc(n_act, 1)
                else:
                    eng.tensor_tensor(tmp[:, k % 4, :], x[:, k, chunk(c)], x[:, k, chunk(c)], ALU.mult).then_inc(n_dve, 1)

        def norm_act(act, nn, x, eps=1e-6, copy=None):
            for c in range(NCH + (2 if copy else 1)):
                if c < NCH:
                    norm_squares(act, nn, c, x, 0)
                if 0 < c <= NCH:
                    q = 3 * nn + c - 1
                    act.wait_ge(n_mm, KD * (q + 1))
                    act.activation(rstd[:, c - 1, :], bank[:, 6 + q % 2, 0:CH], ACT.Ln, scale=1.0 / D, bias=eps).then_inc(n_log, 1)
                    act.wait_ge(n_log, q + 1)
                    act.activation(rstd[:, c - 1, :], rstd[:, c - 1, :], ACT.Exp, scale=-0.5).then_inc(n_rstd, 1)
                if copy and c >= 2:
                    copy(c - 2)

        def norm_dve(dve, nn, x, out, wv, after=None):
            for c in range(NCH + (2 if after else 1)):
                if c < NCH:
                    norm_squares(dve, nn, c, x, 1)
                if 0 < c <= NCH:
                    norm_apply(dve, nn, c - 1, x, out, wv)
                if after and c >= 2:
                    after(c - 2)

        def norm_apply(dve, nn, c, x, out, wv):
            dve.wait_ge(n_rstd, 3 * nn + c + 1)
            for k in range(KD):
                dve.scalar_tensor_tensor(out[:, k, chunk(c)], x[:, k, chunk(c)], vcol(wv, k), rstd[:, c, :],
                                         ALU.mult, ALU.mult).then_inc(n_out, 1)

        def load_slab(sp, g, i, s, source, before):
            if not isinstance(i, int):
                g.wait_full(sp, i, g.last[s] - g.per)
            elif i:
                g.wait_full(sp, i - 1, g.last[s])
            elif before is not None:
                before.wait_full(sp, before.rounds - 1, before.last[s])
            w = source(i, s)
            sp.dma_start(wring[:, s, 0:w.shape[1], :], w).then_inc(w_in[s], 16)

        def stream(sp, g, source, before):
            for s in range(4):
                load_slab(sp, g, 0, s, source, before)
            with sp.Fori(1, g.rounds) as i:
                for s in range(4):
                    load_slab(sp, g, i, s, source, before)

        def job(pe, g, i, j, slots, rhs):
            g.wait_bank(pe, i, j)
            total, k = sum(n for _, n in slots), 0
            for s, n in slots:
                for kk in range(n):
                    mm = pe.matmul(bank[:, j % 6, 0:CH], wring[:, s, kk, :], rhs(k, j), start=(k == 0), stop=(k == total - 1))
                    k += 1
            mm.then_inc(g.full, 1)
            return mm

        def wait_slab(pe, i, s):
            pe.wait_ge(w_in[s], 16 * (i + w_rounds[1] + 1))

        def project_pe(pe, g, x, ready=None):
            with pe.Fori(0, g.rounds) as i:
                for s in range(4):
                    wait_slab(pe, i, s)
                    for c in range(NCH):
                        if ready and s == 0:
                            ready(c)
                        job(pe, g, i, NCH * s + c, [(s, KD)], lambda k, j: x[:, k, chunk(j % NCH)])
            w_rounds[1] += g.rounds

        def cols(w, n):
            return w.rearrange("(k p) n -> p k n", p=P)[:, :, ds(n * P, P)]

        g_sems = {"full": sem("job_full"), "free": [sem("bank_free_even"), sem("bank_free_odd")], "jobs": 0}
        g_att = Gemm(g_sems, 3)

        w_in0 = a["w_in"].rearrange("e k n -> (e k) n")
        blk = ctx.enter_context(nc.Block())

        def setup_sp(sp):
            xp = a["x_prompt"].rearrange("o (n p) d -> p (o n) d", p=P)
            sp.dma_start(ident[:], a["c_ident"]).then_inc(ident_in, 16)
            for n in range(NB):
                sp.dma_start(xrows[:, n, :], xp[:, n, :]).then_inc(x_in[n // 4], 16)
            rows = [(a["norm_mix"], V_MIX0, 2), (a["norm_ffn"], V_FFN0, 2), (a["norm_final"].rearrange("(o d) -> o d", o=1), V_FIN, 1),
                    (a["conv_b_pw1"].rearrange("o (g d) -> (o g) d", g=2), V_BA, 2), (a["conv_b_dw"], V_BDW, 1),
                    (a["conv_ln_g"], V_LG, 1), (a["conv_ln_b"], V_LB, 1), (a["conv_b_pw2"], V_BPW2, 1),
                    (a["conv_w_dw"].rearrange("o w d -> (o w) d"), V_WDW, CW)]
            n = 0
            for src, r, m in rows:
                sp.dma_start(vrows[r:r + m, :], src).then_inc(const_in, 16)
                n += 1
            lams = [a[k].rearrange("o (d u) -> (o d) u", u=1) for k in ("lam_q1", "lam_q2", "lam_k1", "lam_k2")]
            rest = [(xsrows, a["x_sample"].rearrange("b o d -> (b o) d")), (grows, a["gdn_conv_w"].rearrange("o w d -> (o w) d")),
                    (srows, a["state_gdn_conv"].rearrange("o b w d -> (o b w) d")), (triu[:], a["c_triu"]), (causal[:], a["c_causal"]),
                    (merge_words, a["c_merge"]), (halves[:].rearrange("p a m -> p (a m)"), a["c_halves"]),
                    (hot, a["c_hot"]), (hots.rearrange("p a m -> p (a m)"), a["c_hots"]), (rel, a["rel_bias"]),
                    (pages[:], a["page_table"].rearrange("(o b) g -> o (b g)", o=1)),
                    (gate0[:, 0, :], a["gdn_A_log"].broadcast_to([P, H])), (gate0[:, 1, :], a["gdn_dt_bias"].broadcast_to([P, H])),
                    (hw[:, 0:1], a["diff_subln_w"].rearrange("o (d u) -> (o d) u", u=1)),
                    (hw[:, 1:2], a["gdn_norm_w"].rearrange("o (d u) -> (o d) u", u=1))]
            rest += [(lamv[:, q:q + 1], lams[q]) for q in range(4)]
            for dst, src in rest:
                sp.dma_start(dst, src).then_inc(const_in, 16)
                n += 1
            return 16 * n
        CONSTS = 16 * (9 + 19)

        def setup_pe(pe):
            pe.wait_ge(ident_in, 16)
            for n in range(NB):
                pe.wait_ge(x_in[n // 4], 64)
                if n >= 2:
                    pe.wait_ge(xt_act, n - 1)
                    pe.wait_ge(xt_dve, n - 1)
                for k in range(KD):
                    mm = pe.transpose(bank[:, 2 * (n % 2) + k // 4, k % 4 * P:(k % 4 + 1) * P], xrows[:, n, k * P:(k + 1) * P], ident[:, :])
                mm.then_inc(xt_full, 1)
            pe.wait_ge(const_in, CONSTS)
            for k in range(KD):
                pe.transpose(bank[:, 4, k * NV:(k + 1) * NV], vrows[:, k * P:(k + 1) * P], ident[0:NV, 0:NV])
            for k in range(12):
                pe.transpose(bank[:, 5, k * GW:(k + 1) * GW], grows[:, k * P:(k + 1) * P], ident[0:GW, 0:GW])
            for k in range(KD):
                pe.transpose(bank[:, 5, 96 + k * B:96 + (k + 1) * B], xsrows[:, k * P:(k + 1) * P], ident[0:B, 0:B])
            R = B * (GW - 1)
            for k in range(12):
                mm = pe.transpose(bank[:, 6, k * R:(k + 1) * R], srows[:, k * P:(k + 1) * P], ident[0:R, 0:R])
            mm.then_inc(set_mm, 1)
            pe.wait_ge(xt_act, NB)
            for r in range(3):
                pe.matmul(bank[:, 0, 192 + r * H:192 + (r + 1) * H], hots[:, r, :], rel, start=True, stop=True)
            pe.wait_ge(lam_prod, 1)
            pe.wait_ge(ones_set, 1)
            pe.matmul(bank[:, 0, 256:258], ones[0:DA, :], lamp, start=True, stop=True)
            pe.matmul(bank[0:H, 7, 0:384], rel, hot, start=True, stop=True).then_inc(set_mm, 1)

        def setup_act(act):
            for n in range(NB):
                act.wait_ge(xt_full, n + 1)
                act.activation(res_a[:, 0:4, n * P:(n + 1) * P], bank[:, 2 * (n % 2), :].rearrange("p (k t) -> p k t", k=4), ACT.Copy).then_inc(xt_act, 1)
            act.wait_ge(set_dve, 1)
            act.activation(lam[:, 2:4], lam[:, 0:2], ACT.Exp).then_inc(lam_exp, 1)

        def setup_dve(dve, step):
            dve.memset(ones[:], 1.0).then_inc(ones_set, 1)
            for n in range(NB):
                dve.wait_ge(xt_full, n + 1)
                dve.tensor_copy(res_a[:, 4:8, n * P:(n + 1) * P], bank[:, 2 * (n % 2) + 1, :].rearrange("p (k t) -> p k t", k=4)).then_inc(xt_dve, 1)
            dve.wait_ge(const_in, CONSTS)
            dve.tensor_tensor(lamp, lamv[:, 0:2], lamv[:, 2:4], ALU.mult).then_inc(lam_prod, 1)
            dve.wait_ge(set_mm, 1)
            dve.tensor_copy(vec[:].rearrange("p k v -> p (k v)"), bank[:, 4, 0:KD * NV])
            dve.tensor_copy(gcw[:].rearrange("p k v -> p (k v)"), bank[:, 5, 0:12 * GW])
            dve.tensor_copy(res_a[:, :, T:TT], bank[:, 5, 96:96 + KD * B].rearrange("p (k b) -> p k b", k=KD))
            dve.tensor_copy(gst[:].rearrange("p k b w -> p (k b w)"), bank[:, 6, 0:12 * B * (GW - 1)])
            dve.wait_ge(set_mm, 2)
            dve.tensor_copy(sbias[:].rearrange("p r h -> p (r h)"), bank[:, 0, 192:192 + 3 * H])
            dve.tensor_copy(merge[:].rearrange("p a l m -> p (a l m)"), merge_words)
            dve.memset(bsb[:, 256:384], NEG)
            dve.tensor_copy(bsb[:, 0:256], bank[0:H, 7, 0:256])
            step(dve.tensor_copy(lam[:, 0:2], bank[:, 0, 256:258]))
            dve.sem_inc(set_dve, 1)
            dve.wait_ge(lam_exp, 1)
            step(dve.tensor_tensor(lam[:, 4:5], lam[:, 3:4], lam[:, 2:3], ALU.subtract))
            step(dve.tensor_scalar(lam[:, 5:6], lam[:, 4:5], LAM0, None, ALU.subtract))

        qkv = tiles(0, 12)

        def copy_out(eng, g, par, rounds, dst):
            g.grant(eng, [par])
            with eng.Fori(0, rounds) as i:
                for j in range(par, g.per, 2):
                    g.wait_full(eng, i, j)
                    d = dst(i, j // NCH, j % NCH)
                    if par == 0:
                        eng.activation(d, bank[:, j % 6, 0:CH], ACT.Copy).then_inc(g.free[0], 1)
                    else:
                        eng.tensor_copy(d, bank[:, j % 6, 0:CH]).then_inc(g.free[1], 1)

        def att_dst(i, t, c):
            return big[:, ds(i * (4 * TT) + (t * TT + c * CH), CH)]

        x_parked = sem("x_parked")

        def pe_part1(pe):
            setup_pe(pe)
            norm_pe(pe, 0)
            project_pe(pe, g_att, res_b, lambda c: pe.wait_ge(n_out, KD * (c + 1)))

        def act_part1(act):
            setup_act(act)
            act.wait_ge(xt_dve, NB)
            act.wait_ge(set_dve, 1)
            norm_act(act, 0, res_a)
            copy_out(act, g_att, 0, 3, att_dst)

        def dve_part1(dve, step):
            setup_dve(dve, step)
            dve.wait_ge(xt_act, NB)
            norm_dve(dve, 0, res_a, res_b, V_MIX0)
            copy_out(dve, g_att, 1, 3, att_dst)

        def sp_part1(sp):
            setup_sp(sp)
            stream(sp, g_att, lambda i, s: cols(w_in0, i * 4 + s), None)
            sp.wait_ge(n_out, NCH * KD)
            sp.dma_start(park.ap(), res_a[:].rearrange("p k t -> p (k t)")).then_inc(x_parked, 16)
            sp.wait_ge(x_parked, 16)

        def pool_part1(pool, step):
            pool.wait_ge(set_dve, 1)
            pool.dma_start(brow.ap().rearrange("q h m -> h q m"), bsb.unsqueeze(1).to_broadcast([H, P, 384])).then_inc(bias_io, 16)
            pool.wait_ge(bias_io, 16)

        kv_full, k_copied, v_copied = sem("kv_full"), sem("k_copied"), sem("v_copied")
        k_out = [sem("k_out0"), sem("k_out1")]
        v_out = sem("v_out")
        skv_copied = sem("skv_copied")
        skv_out = sem("skv_out")
        ktok = flat(21600, 2, 512)
        vtok = res_a[:].rearrange("p k t -> p (k t)")[:, 4 * TT:4 * TT + NB * 512].rearrange("p (n e) -> p n e", n=NB)
        skv = flat(16480, 2, 512, parts=B)

        def kv_pe(pe):
            g_att.wait_all_read(pe)
            for n in range(NB):
                for kv in range(2):
                    if n >= 2:
                        pe.wait_ge((k_copied, v_copied)[kv], n - 1)
                    for h in range(H):
                        mm = pe.transpose(bank[:, 2 * (n % 2) + kv, h * P:(h + 1) * P], qkv[:, 4 + 4 * kv + h, n * P:(n + 1) * P], ident[:, :])
                    mm.then_inc(kv_full, 1)
            for kv in range(2):
                for h in range(H):
                    mm = pe.transpose(bank[0:B, 4 + kv, h * P:(h + 1) * P], qkv[:, 4 + 4 * kv + h, T:TT], ident[:, :])
            mm.then_inc(kv_full, 1)

        def kv_act(act):
            for n in range(NB):
                act.wait_ge(kv_full, 2 * n + 1)
                if n >= 2:
                    act.wait_ge(k_out[n % 2], 16 * (n // 2))
                act.activation(ktok[:, n % 2, :], bank[:, 2 * (n % 2), :], ACT.Copy).then_inc(k_copied, 1)

        def kv_dve(dve):
            for n in range(NB):
                dve.wait_ge(kv_full, 2 * n + 2)
                if n == 0:
                    dve.wait_ge(x_parked, 16)
                dve.tensor_copy(vtok[:, n, :], bank[:, 2 * (n % 2) + 1, :]).then_inc(v_copied, 1)
            dve.wait_ge(kv_full, 2 * NB + 1)
            dve.tensor_copy(skv[:, 0, :], bank[0:B, 4, :])
            dve.tensor_copy(skv[:, 1, :], bank[0:B, 5, :]).then_inc(skv_copied, 1)
            dve.tensor_copy(sq[:], qkv[:, :, T:TT]).then_inc(skv_copied, 1)

        def kv_sp(sp):
            kp = o["new_k_prompt"].rearrange("e o (n p) h d -> (e o n) p (h d)", p=P)
            vp = o["new_v_prompt"].rearrange("e o (n p) h d -> (e o n) p (h d)", p=P)
            for n in range(NB):
                sp.wait_ge(k_copied, n + 1)
                sp.dma_start(kp[n], ktok[:, n % 2, :]).then_inc(k_out[n % 2], 16)
                sp.wait_ge(v_copied, n + 1)
                sp.dma_start(vp[n], vtok[:, n, :]).then_inc(v_out, 16)
            sp.wait_ge(skv_copied, 1)
            sp.dma_start(o["new_k_sample"].rearrange("e b o h d -> (e b o) (h d)"), skv[:, 0, :]).then_inc(skv_out, 16)
            sp.dma_start(o["new_v_sample"].rearrange("e b o h d -> (e b o) (h d)"), skv[:, 1, :]).then_inc(skv_out, 16)

        mix = res_a
        PROB2 = 2 * SLAB * P
        prob = [flat(12384, 2, T), flat(12384 + 2 * T, 2, T),
                wring[:].rearrange("p s k n -> p (s k n)")[:, PROB2:PROB2 + 2 * T].rearrange("p (m t) -> p m t", m=2)]
        wT = flat(16480, 2, NB, P)
        biasT = flat(18528, H, 256)
        qs, ks = flat(19552, T), flat(20576, T)
        osb = flat(21600, NB, P)
        osq = tmp[:].rearrange("p s c -> p (s c)")[:, 0:NB * P].rearrange("p (n e) -> p n e", n=NB)
        far = small[:, 0:1]
        nmax = small[:, 4:8].rearrange("p (a m) -> p a m", a=2)
        psum_ = small[:, 8:12].rearrange("p (a m) -> p a m", a=2)
        prec = small[:, 12:16].rearrange("p (a m) -> p a m", a=2)
        ssq = small[:, 16:24]
        pbank = bank[:].rearrange("p b n -> p (b n)")
        head_in, s_full, z_late, z_early = sem("head_in"), sem("s_full"), sem("z_late"), sem("z_early")
        max_done, exp_done, a_full = sem("max_done"), sem("exp_done"), sem("a_full")
        at_full, at_copied, pv_full = sem("at_full"), sem("at_copied"), sem("pv_full")
        o_copied, o_sum, o_root, o_normed, ot_full, o_read = (sem(x) for x in ("o_copied", "o_sum", "o_root", "o_normed", "ot_full", "o_read"))
        GRP = [1, 2, 3, 4, 6, 8, 10, 12]

        def groups(i):
            return [(GRP[i] - 1 - (i // 4 - q), 4 * q, min(4 * q + 3, i)) for q in range(i // 4 + 1)]

        def att_pool(pool):
            pool.wait_ge(n_out, 1)
            pool.dma_start(biasT, bass.AP(tensor=brow, offset=P - 1, ap=[[H * 384 - 1, P], [384, H], [1, 256]])).then_inc(bias_io, 16)
            g_att.wait_all_read(pool)
            with pool.Fori(0, H) as h:
                pool.wait_ge(z_late, 16 * h + 2)
                pool.wait_ge(z_early, 12 * h + 2)
                pool.tensor_copy(qs, big[:, ds(h * TT, T)])
                pool.tensor_copy(far, sbias[:, 1, ds(h, 1)])
                pool.tensor_copy(ks, big[:, ds((h + 4) * TT, T)]).then_inc(head_in, 1)

        def att_pe(pe):
            pe.sem_inc(at_full, 3)
            pe.sem_inc(pv_full, 2)
            pe.wait_ge(k_copied, NB)
            pe.wait_ge(v_copied, NB)
            pe.wait_ge(skv_copied, 1)

            def scores(h, i):
                for m in range(2):
                    pe.wait_ge(z_late, 16 * h + 2 * i + m + 1)
                    if i == 0:
                        pe.wait_ge(z_early, 12 * h + m + 1)
                    elif i >= 3:
                        pe.wait_ge(z_early, 12 * h + 2 * (i - 3) + m + 3)
                    L = (i + 1) * P
                    for c0 in range(0, L, 512):
                        c1 = min(L, c0 + 512)
                        mm = pe.matmul(pbank[:, 1024 * m + c0:1024 * m + c1], qs[DA * m:DA * (m + 1), i * P:(i + 1) * P],
                                       ks[DA * m:DA * (m + 1), c0:c1], start=True, stop=True)
                    mm.then_inc(s_full, 1)

            def turn_weights(h, i):
                pe.wait_ge(a_full, 8 * h + i + 1)
                for gi, b0, b1 in groups(i):
                    pe.wait_ge(at_copied, 12 * h + gi + 1)
                    for b in range(b0, b1 + 1):
                        mm = pe.transpose(bank[:, 4 + gi % 2, (b - b0) * P:(b - b0 + 1) * P], prob[i % 3][:, 0, b * P:(b + 1) * P], ident[:, :])
                    mm.then_inc(at_full, 1)

            def weigh(h, i):
                pe.wait_ge(at_copied, 12 * h + GRP[i] + 2)
                if i == 0:
                    pe.wait_ge(o_read, h + 1)
                for b in range(i + 1):
                    mm = pe.matmul(bank[:, 6 + i // 4, i % 4 * P:(i % 4 + 1) * P], wT[:, i % 2, b, :],
                                   vflat[:, ds(h * P + (4 * TT + b * 512), P)], start=(b == 0), stop=(b == i))
                mm.then_inc(pv_full, 1)

            def turn_output(h):
                pe.wait_ge(o_normed, h + 1)
                for n in range(NB):
                    mm = pe.transpose(bank[:, 6 + n // 4, n % 4 * P:(n % 4 + 1) * P], osb[:, n, :], ident[:, :])
                mm.then_inc(ot_full, 1)

            def head(h, first):
                pe.wait_ge(head_in, h + 1)
                for s in range(NB + 3):
                    if s < NB:
                        scores(h, s)
                    if 2 <= s < NB + 2:
                        turn_weights(h, s - 2)
                    if s == 2 and not first:
                        turn_output(h - 1)
                    if s >= 3:
                        weigh(h, s - 3)

            head(0, True)
            with pe.Fori(1, H) as h:
                head(h, False)
            turn_output(H - 1)
        vflat = res_a[:].rearrange("p k t -> p (k t)")

        def att_act(act):
            act.sem_inc(z_early, 2)
            act.sem_inc(at_copied, 2)
            for s in range(2):
                act.wait_ge(k_out[s], 16 * (NB // 2))
            act.wait_ge(skv_out, 32)

            def early(h, i):
                for m in range(2):
                    act.wait_ge(z_late, 16 * h + 2 * i + m + 3)
                    act.activation(prob[i % 3][:, m, 0:(i - 1) * P], pbank[:, 1024 * m:1024 * m + (i - 1) * P],
                                   ACT.Identity, bias=far, scale=DA ** -0.5).then_inc(z_early, 1)

            def exps(h, i):
                for m in range(2):
                    act.wait_ge(max_done, 16 * h + 2 * i + m + 1)
                    act.activation(prob[i % 3][:, m, 0:(i + 1) * P], prob[i % 3][:, m, 0:(i + 1) * P], ACT.Exp,
                                   bias=nmax[:, i % 2, m:m + 1], accum_out=psum_[:, i % 2, m:m + 1]).then_inc(exp_done, 1)

            def copy_turned(h, b):
                act.wait_ge(pv_full, 8 * h + b + 1)
                for gi, b0, b1 in groups(b):
                    act.wait_ge(at_full, 12 * h + gi + 4)
                    act.activation(wT[:, b % 2, b0:b1 + 1, :], bank[:, 4 + gi % 2, 0:(b1 - b0 + 1) * P].rearrange("p (n q) -> p n q", q=P),
                                   ACT.Copy).then_inc(at_copied, 1)

            def output(h):
                act.wait_ge(pv_full, 8 * h + NB + 2)
                for b in range(2):
                    act.activation(osb[:, 4 * b:4 * b + 4, :], bank[:, 6 + b, :].rearrange("p (n q) -> p n q", q=P), ACT.Copy).then_inc(o_copied, 1)

            def root(h):
                act.wait_ge(o_sum, h + 1)
                act.activation(ssq, ssq, ACT.Sqrt).then_inc(o_root, 1)

            def output_turned(h):
                act.wait_ge(ot_full, h + 1)
                for b in range(2):
                    last = act.activation(vflat[:, ds(h * TT + 512 * b, 512)], bank[:, 6 + b, :], ACT.Copy, scale=hw[:, 0:1])
                last.then_inc(o_read, 1)

            def head(h, first):
                for s in range(NB + 2):
                    if s == 0 and not first:
                        output(h - 1)
                    if 2 <= s < NB:
                        early(h, s)
                    if s >= 2:
                        copy_turned(h, s - 2)
                    if s < NB:
                        exps(h, s)
                    if s == 1 and not first:
                        root(h - 1)
                    if s == 2 and not first:
                        output_turned(h - 1)

            head(0, True)
            with act.Fori(1, H) as h:
                head(h, False)
            output(H - 1)
            root(H - 1)
            output_turned(H - 1)

        def att_dve(dve, step):
            dve.sem_inc(z_late, 2)
            step(dve.tensor_scalar(hw[:, 0:1], hw[:, 0:1], 1.0 - LAM0, None, ALU.mult))
            dve.sem_inc(o_read, 1)
            dve.wait_ge(bias_io, 32)

            def late_max(h, i):
                L, L0 = (i + 1) * P, max(i - 1, 0) * P
                if i != 2:
                    dve.wait_ge(at_full, 12 * h + ((1, 3)[i] if i < 2 else GRP[i - 3] + 3))
                for m in range(2):
                    dve.wait_ge(s_full, 16 * h + 2 * i + m + 1)
                    dve.scalar_tensor_tensor(prob[i % 3][:, m, L0:L], pbank[:, 1024 * m + L0:1024 * m + L], DA ** -0.5,
                                             big[:, ds(h * 256 + (18528 + 256 - (L - L0)), L - L0)], ALU.mult, ALU.add).then_inc(z_late, 1)
                for m in range(2):
                    dve.wait_ge(z_late, 16 * h + 2 * i + m + 3)
                    if i >= 2:
                        dve.wait_ge(z_early, 12 * h + 2 * (i - 2) + m + 3)
                    dve.tensor_reduce(nmax[:, i % 2, m:m + 1], prob[i % 3][:, m, 0:L], AX.X, ALU.max, negate=True).then_inc(max_done, 1)

            def combine(h, b):
                L, s = (b + 1) * P, b % 2
                p1, p2 = (prob[b % 3][:, m, 0:L] for m in range(2))
                dve.wait_ge(exp_done, 16 * h + 2 * b + 2)
                step(dve.reciprocal(prec[:, s, :], psum_[:, s, :]))
                step(dve.tensor_scalar(prec[:, s, 1:2], prec[:, s, 1:2], lam[:, 5:6], None, ALU.mult))
                step(dve.tensor_scalar(p1, p1, prec[:, s, 0:1], None, ALU.mult))
                step(dve.scalar_tensor_tensor(p1, p2, prec[:, s, 1:2], p1, ALU.mult, ALU.add))
                dve.sem_inc(a_full, 1)

            def output_sum(h):
                dve.wait_ge(o_copied, 2 * h + 2)
                step(dve.tensor_tensor(osq, osb, osb, ALU.mult))
                step(dve.tensor_reduce(ssq, osq, AX.X, ALU.add))
                step(dve.tensor_scalar(ssq, ssq, 1.0 / P, 1e-5, ALU.mult, ALU.add))
                dve.reciprocal(ssq, ssq).then_inc(o_sum, 1)

            def output_norm(h):
                dve.wait_ge(o_root, h + 1)
                dve.tensor_tensor(osb, osb, ssq.unsqueeze(2).to_broadcast([P, NB, P]), ALU.mult).then_inc(o_normed, 1)

            def head(h, first):
                for s in range(NB + 1):
                    if s < NB:
                        late_max(h, s)
                    if s == 0 and not first:
                        output_sum(h - 1)
                    if s:
                        combine(h, s - 1)
                    if s == 1 and not first:
                        output_norm(h - 1)

            head(0, True)
            with dve.Fori(1, H) as h:
                step.enter(h - 1, 4 * NB + 3)
                head(h, False)
            step.leave(H - 1)
            output_sum(H - 1)
            output_norm(H - 1)

        g_gdn = Gemm(g_sems, 4)
        RAW = T + GW - 1 + B
        raw = vflat[:, 4 * TT:4 * TT + 2 * RAW].rearrange("p (s t) -> p s t", s=2)
        diagq = vflat[:, 4 * TT + 2 * RAW:4 * TT + 2 * RAW + 1024].rearrange("p (s h d) -> p s h d", s=2, h=H)
        ring = flat(17 * TT, 4, 2, 512)
        prod = flat(17 * TT + 4096, 1024)
        prods = [prod, vflat[:, 4 * TT + 2 * RAW + 1024:4 * TT + 2 * RAW + 2048]]
        ba = big[0:2 * H, 16 * TT:17 * TT]
        pflat = probs[:].rearrange("p b g x -> p (b g x)")
        page_in = [sem(f"page_in{s}") for s in range(4)]
        kpage_used = sem("kpage_used")
        qb_diag, qb_full, conv_done, raw_zero = sem("qb_diag"), sem("qb_full"), sem("conv_done"), sem("raw_zero")
        silu_done = sem("silu_done")
        z_gated = sem("z_gated")
        ba_in, ba_full, ba_copied = sem("ba_in"), sem("ba_full"), sem("ba_copied")
        sm_dve_marks = Marks(sem("sm_dve"), own_prod=1, sm_max=1, sm_diag=1, sm_exp_in=1, sm_part=1)
        sm_pe_marks = Marks(sem("sm_pe"), own_full=1, sm_turned=1, sm_bmax=1, sm_sum=1)
        sm_exp, aw_done = sem("sm_exp"), sem("aw_done")

        def load_pages(sp, cache, b, pair, slot):
            for u in range(2):
                page = sp.value_load(pages[0:1, ds(b * PG + (2 * pair + u), 1)], min_val=0, max_val=cache.shape[1] - 1)
                src = cache.rearrange("e n p h d -> (e n) p (h d)")[ds(page, 1)].rearrange("o p n -> (o p) n")
                sp.dma_start(ring[:, slot, u, :], src).then_inc(page_in[slot], 16)

        def gdn_in_sp(sp):
            sp.dma_start(wba[:], w_in0.rearrange("(k p) n -> p k n", p=P)[:, :, 28 * P:28 * P + 2 * H]).then_inc(ba_in, 16)

            def slab(i, s):
                load_slab(sp, g_gdn, i, s, lambda i, s: cols(w_in0, i * 4 + (12 + s)), g_att)

            def body(i, last=False):
                for t in range(4):
                    if t < 2:
                        slab(i, t + 2)
                    elif not last:
                        slab(i + 1, t - 2)
                    for pp in range(4):
                        sp.wait_ge(kpage_used, i * 16 + (4 * t + pp + 13))
                        load_pages(sp, a["cache_attn_k"], i * 2 + t // 2, t % 2 * 4 + pp, pp)
            slab(0, 0)
            slab(0, 1)
            sp.wait_ge(at_full, 3 + GRP[NB - 1] * H)
            body(0)
            with sp.Fori(1, 3) as i:
                body(i)
            body(3, True)

        def gdn_in_pe(pe):
            pe.sem_inc(qb_full, 2)

            def body(i):
                for t in range(4):
                    if t % 2 == 0:
                        pe.wait_ge(qb_diag, i * 2 + t // 2 + 1)
                        pe.wait_ge(kpage_used, i * 16 + (4 * t + 8))
                        pe.matmul(bank[:, 6 + t // 2, :], ones[:, :], diagq[:, t // 2].rearrange("p h d -> p (h d)"), start=True, stop=True).then_inc(qb_full, 1)
                    wait_slab(pe, i, t)
                    for c in range(NCH):
                        job(pe, g_gdn, i, NCH * t + c, [(t, KD)], lambda k, j: res_b[:, k, chunk(j % NCH)])
            pe.wait_ge(o_read, H + 1)
            with pe.Fori(0, 3) as i:
                body(i)
            body(3)
            w_rounds[1] += 4
            pe.wait_ge(ba_in, 16)
            g_gdn.wait_all_read(pe)
            for c in range(NCH):
                for k in range(KD):
                    mm = pe.matmul(bank[0:2 * H, c, 0:CH], wba[:, k, :], res_b[:, k, chunk(c)], start=(k == 0), stop=(k == KD - 1))
                mm.then_inc(ba_full, 1)

        def gdn_in_act(act):
            g_gdn.grant(act, [0, 1])
            act.wait_ge(raw_zero, 1)

            def silu(i, t):
                act.wait_ge(conv_done, i * 4 + t + 1)
                d = big[:, ds((i * 4 + t) * TT, TT)]
                act.activation(d, d, ACT.Silu).then_inc(silu_done, 1)

            with act.Fori(0, 3) as i:
                for t in range(4):
                    for c in range(NCH):
                        g_gdn.wait_full(act, i, NCH * t + c)
                        act.activation(raw[:, t % 2, GW - 1 + c * CH:GW - 1 + (c + 1) * CH], bank[:, (NCH * t + c) % 6, 0:CH],
                                       ACT.Copy).then_inc(g_gdn.free[(NCH * t + c) % 2], 1)
                    if t:
                        silu(i, t - 1)
                silu(i, 3)
            for j in range(12):
                g_gdn.wait_full(act, 3, j)
                act.activation(tiles(12 + j // NCH, 1)[:, 0, chunk(j % NCH)], bank[:, j % 6, 0:CH], ACT.Copy).then_inc(g_gdn.free[j % 2], 1)
            g_gdn.wait_all_read(act)
            z = tiles(12, H)
            act.activation(z, z, ACT.Silu).then_inc(z_gated, 1)
            for c in range(NCH):
                act.wait_ge(ba_full, c + 1)
                act.activation(ba[:, chunk(c)], bank[0:2 * H, c, 0:CH], ACT.Copy).then_inc(ba_copied, 1)

        def gdn_in_pool(pool):
            pool.wait_ge(skv_copied, 2)
            pool.wait_ge(o_read, H + 1)
            with pool.Fori(0, B // 2) as i:
                for s in range(2):
                    pool.wait_ge(qb_full, i * 2 + s + 1)
                    pool.tensor_tensor(diagq[:, s], ident[:].unsqueeze(1).to_broadcast([P, H, P]),
                                       sq[:, 0:H, ds(i * 2 + s, 1)].to_broadcast([P, H, P]), ALU.mult).then_inc(qb_diag, 1)

        def gdn_in_dve(dve, step):
            dve.wait_ge(pv_full, 8 * H + 2)
            dve.wait_ge(v_out, 16 * NB)
            dve.wait_ge(ot_full, H)
            dve.memset(raw[:, :, 0:GW - 1], 0.0).then_inc(raw_zero, 1)
            dve.sem_inc(kpage_used, 16)

            def score(i, t):
                b = i * 2 + t // 2
                def heads_sum(pp):
                    dve.tensor_reduce(pflat[:, ds(b * (PG * 2 * H) + 16 * (t % 2 * 4 + pp), 16)], prods[pp % 2].rearrange("p (x d) -> p x d", d=DA),
                                      AX.X, ALU.add).then_inc(kpage_used, 1)

                for pp in range(4):
                    dve.wait_ge(page_in[pp], i * 128 + 32 * (t + 1))
                    if pp == 0 and t % 2 == 0:
                        dve.wait_ge(qb_full, b + 3)
                    dve.wait_ge(kpage_used, i * 16 + (4 * t + pp + 15))
                    step.lagged(dve.tensor_tensor(prods[pp % 2].rearrange("p (u n) -> p u n", u=2), ring[:, pp],
                                                  bank[:, 6 + t // 2, :].unsqueeze(1).to_broadcast([P, 2, 512]), ALU.mult))
                    if pp:
                        heads_sum(pp - 1)
                step.settle()
                heads_sum(3)

            def conv(i, t):
                n = i * 4 + t
                for j in (NCH * t + 1, NCH * t + 2):
                    g_gdn.wait_read(dve, i, j)
                w = gcwf
                e = big[:, ds(n * TT + T, B)]
                r = raw[:, t % 2]
                dve.tensor_copy(gnewf[:, ds(n * (GW - 1 + B), GW - 1 + B)], r[:, T:RAW])
                for q in range(GW):
                    s = gstf[:, ds(n * (B * (GW - 1)) + q, B, GW - 1)] if q < GW - 1 else r[:, T + GW - 1:RAW]
                    wc = w[:, ds(n * GW + q, 1)]
                    if q == 0:
                        dve.tensor_scalar(e, s, wc, None, ALU.mult)
                    else:
                        dve.scalar_tensor_tensor(e, s, wc, e, ALU.mult, ALU.add)
                    for v in range(2):
                        d, src = big[:, ds(n * TT + v * T // 2, T // 2)], r[:, q + v * T // 2:q + (v + 1) * T // 2]
                        if q == 0:
                            step.lagged(dve.tensor_scalar(d, src, wc, None, ALU.mult))
                        else:
                            step.lagged(dve.scalar_tensor_tensor(d, src, wc, d, ALU.mult, ALU.add))
                step.settle()
                dve.sem_inc(conv_done, 1)

            with dve.Fori(0, 3) as i:
                step.enter(i, 4 * (2 * GW + 4))
                for t in range(4):
                    conv(i, t)
                    score(i, t)
            step.leave(3)
            for t in range(4):
                score(3, t)
        gcwf, gnewf = gcw[:].rearrange("p k w -> p (k w)"), gnew[:].rearrange("p k w -> p (k w)")
        gstf = gst[:].rearrange("p k b w -> p (k b w)")

        X = B * 2 * H
        smx, own, bmx, ssum, coef = (small[:, 64 * (n + 1):64 * (n + 2)] for n in range(5))
        sdiag = small[0:X, 384:384 + X]
        smt = small[0:X, 448:449]
        ownw = small[:, 452:452 + B * H]
        zb = prod[:, 0:PG * 2 * H]
        qkp = prod[:, 256:256 + H * B]

        def sm_dve(dve, step):
            dve.wait_ge(kpage_used, 16 + B * PG // 2)
            dve.tensor_tensor(qkp.rearrange("p (h b) -> p h b", h=H), sq[:, 0:H, :], sq[:, H:2 * H, :], ALU.mult).then_inc(sm_dve_marks.sem, 1)
            zv = zb.rearrange("p (g h m) -> p g h m", g=PG, h=H)
            for m in range(2):
                dve.tensor_copy(zv[:, 0:PG - 1, :, m], sbias[:, 1, :].unsqueeze(1).to_broadcast([P, PG - 1, H]))
                step(dve.tensor_copy(zv[:, PG - 1, :, m], sbias[:, 0, :]))
            step(dve.scalar_tensor_tensor(pflat.rearrange("p (b x) -> p b x", b=B), pflat.rearrange("p (b x) -> p b x", b=B), DA ** -0.5,
                                          zb.unsqueeze(1).to_broadcast([P, B, PG * 2 * H]), ALU.mult, ALU.add))
            sm_pe_marks.wait(dve, "own_full", 1)
            ov = own.rearrange("p (b h m) -> p b h m", b=B, h=H)
            for m in range(2):
                step(dve.scalar_tensor_tensor(ov[:, :, :, m], bank[:, 3, m * 32:(m + 1) * 32].rearrange("p (h b) -> p b h", h=H), DA ** -0.5,
                                              sbias[:, 2, :].unsqueeze(1).to_broadcast([P, B, H]), ALU.mult, ALU.add))
            pv = probs[:].rearrange("p b g x -> p b x g")
            step(dve.tensor_reduce(smx, pv, AX.X, ALU.max))
            dve.tensor_tensor(smx, smx, own, ALU.max).then_inc(sm_dve_marks.sem, 1)
            sm_pe_marks.wait(dve, "sm_turned", 1)
            step(dve.tensor_reduce(smt, bank[0:X, 4, 0:P], AX.X, ALU.max))
            dve.tensor_scalar(sdiag, ident[0:X, 0:X], smt, None, ALU.mult).then_inc(sm_dve_marks.sem, 1)
            sm_pe_marks.wait(dve, "sm_bmax", 1)
            step(dve.tensor_copy(bmx, bank[:, 5, 0:X]))
            mb = bmx.rearrange("p (b x) -> p b x", b=B).unsqueeze(2).to_broadcast([P, B, PG, 2 * H])
            dve.tensor_tensor(own, own, bmx, ALU.subtract)
            dve.tensor_tensor(probs[:], probs[:], mb, ALU.subtract).then_inc(sm_dve_marks.sem, 1)
            dve.wait_ge(sm_exp, 2)
            dve.tensor_reduce(ssum, pv, AX.X, ALU.add).then_inc(sm_dve_marks.sem, 1)
            sm_pe_marks.wait(dve, "sm_sum", 1)
            step(dve.tensor_tensor(coef, bank[:, 4, 0:X], own, ALU.add))
            step(dve.reciprocal(coef, coef))
            cm = coef.rearrange("p (y m) -> p y m", m=2)
            step(dve.tensor_scalar(cm[:, :, 1], cm[:, :, 1], lam[:, 5:6], None, ALU.mult))
            dve.tensor_tensor(own, own, coef, ALU.mult)
            step(dve.tensor_tensor(probs[:], probs[:], coef.rearrange("p (b x) -> p b x", b=B).unsqueeze(2).to_broadcast([P, B, PG, 2 * H]), ALU.mult))
            dve.tensor_reduce(ownw, own.rearrange("p (y m) -> p y m", m=2), AX.X, ALU.add)
            dve.tensor_reduce(aw[:].rearrange("p b g h -> p (b g h)"), pflat.rearrange("p (y m) -> p y m", m=2), AX.X, ALU.add).then_inc(aw_done, 1)

        def sm_pe(pe):
            sm_dve_marks.wait(pe, "own_prod", 1)
            for m in range(2):
                mm = pe.matmul(bank[:, 3, m * 32:(m + 1) * 32], halves[:, m, :], qkp, start=True, stop=True)
            mm.then_inc(sm_pe_marks.sem, 1)
            sm_dve_marks.wait(pe, "sm_max", 1)
            pe.transpose(bank[0:X, 4, 0:P], smx, ident[:, :]).then_inc(sm_pe_marks.sem, 1)
            sm_dve_marks.wait(pe, "sm_diag", 1)
            pe.matmul(bank[:, 5, 0:X], ones[0:X, :], sdiag, start=True, stop=True).then_inc(sm_pe_marks.sem, 1)
            sm_dve_marks.wait(pe, "sm_part", 1)
            pe.matmul(bank[:, 4, 0:X], ones[:, :], ssum, start=True, stop=True).then_inc(sm_pe_marks.sem, 1)

        def sm_act(act):
            sm_dve_marks.wait(act, "sm_exp_in", 1)
            act.activation(own, own, ACT.Exp).then_inc(sm_exp, 1)
            act.activation(pflat, pflat, ACT.Exp).then_inc(sm_exp, 1)
        rb = res_b[:].rearrange("p k t -> p (k t)")

        l2_sq, l2_mm, l2_log, l2_inv, l2_out = (sem(x) for x in ("l2_sq", "l2_mm", "l2_log", "l2_inv", "l2_out"))

        l2x = res_b
        big_qk = qkv[:, 0:2 * H, :]

        def l2_pe(pe):
            pe.sem_inc(l2_mm, 3)
            with pe.Fori(0, 2 * H) as i:
                pe.wait_ge(l2_sq, (i + 1) * NCH)
                for c in range(NCH):
                    pe.wait_ge(l2_log, i * NCH + c + 1)
                    pe.matmul(bank[:, c, 0:CH], ones[:, :], rb[:, ds(i * TT + c * CH, CH)], start=True, stop=True).then_inc(l2_mm, 1)

        def l2_squares(act):
            act.wait_ge(ba_full, NCH)
            act.wait_ge(silu_done, 12)
            for u in range(2):
                act.activation(l2x[:, H * u:H * (u + 1), :], big_qk[:, H * u:H * (u + 1), :], ACT.Square).then_inc(l2_sq, NCH * H)

        def l2_act(act):
            act.sem_inc(l2_log, 3)
            for u in range(2):
                with act.Fori(H * u, H * (u + 1)) as i:
                    for c in range(NCH):
                        act.wait_ge(l2_mm, i * NCH + c + 4)
                        act.activation(rb[:, ds(i * TT + c * CH, CH)], bank[:, c, 0:CH], ACT.Ln, bias=1e-6).then_inc(l2_log, 1)
                act.wait_ge(l2_log, 3 + NCH * H * (u + 1))
                act.activation(l2x[:, H * u:H * (u + 1), :], l2x[:, H * u:H * (u + 1), :], ACT.Exp, scale=-0.5,
                               bias=(math.log(P ** -0.5), 0.0)[u]).then_inc(l2_inv, NCH * H)

        def l2_dve(dve):
            dve.sem_inc(l2_out, 3)
            dve.wait_ge(silu_done, 12)
            for u in range(2):
                dve.wait_ge(l2_inv, NCH * H * (u + 1))
                d = big_qk[:, H * u:H * (u + 1), :]
                dve.tensor_tensor(d, d, l2x[:, H * u:H * (u + 1), :], ALU.mult).then_inc(l2_out, NCH * H)

        NG = NB + B
        graw = small[:, 0:NG * 2 * H].rearrange("p (n r) -> p n r", n=NG)
        beta, ga, gsp, gg = (small[:, 128 + 64 * n:192 + 64 * n].rearrange("p (n h) -> p n h", n=NG) for n in range(4))
        decay_a = small[:, 384:388]
        bad = small[0:2 * H, 388:452].rearrange("p (r b) -> p r b", r=2 * H)
        gate_full, gate_act, gates_done = sem("gate_full"), sem("gate_act"), sem("gates_done")
        gate_marks = Marks(sem("gate_dve"), gate_diag=1, gate_raw=1, gate_abs=1)

        def gate_pe(pe):
            for n in range(NB):
                pe.transpose(bank[:, 3, n * 8:(n + 1) * 8], ba[:, n * P:(n + 1) * P], ident[0:2 * H, 0:2 * H])
            gate_marks.wait(pe, "gate_diag", 1)
            pe.matmul(bank[:, 3, 64:128], ones[0:2 * H, :], bad.rearrange("p r b -> p (r b)"), start=True, stop=True).then_inc(gate_full, 1)

        def gate_dve(dve, step):
            dve.wait_ge(ba_copied, NCH)
            dve.wait_ge(aw_done, 1)
            dve.tensor_tensor(bad, ba[:, T:TT].unsqueeze(1).to_broadcast([2 * H, 2 * H, B]),
                              ident[0:2 * H, 0:2 * H].unsqueeze(2).to_broadcast([2 * H, 2 * H, B]), ALU.mult).then_inc(gate_marks.sem, 1)
            dve.wait_ge(gate_full, 1)
            dve.tensor_copy(graw[:, 0:NB, :], bank[:, 3, 0:64].rearrange("p (n r) -> p n r", n=NB))
            step(dve.tensor_copy(graw[:, NB:NG, :], bank[:, 3, 64:128].rearrange("p (r b) -> p b r", b=B)))
            dve.sem_inc(gate_marks.sem, 1)
            step(dve.tensor_tensor(ga, graw[:, :, H:2 * H], gate0[:, 1, :].unsqueeze(1).to_broadcast([P, NG, H]), ALU.add))
            dve.scalar_tensor_tensor(gsp, ga, -1.0, ga, ALU.mult, ALU.max).then_inc(gate_marks.sem, 1)
            dve.wait_ge(gate_act, 4)
            step(dve.scalar_tensor_tensor(gsp, ga, 0.0, gsp, ALU.max, ALU.add))
            dve.scalar_tensor_tensor(gg, gsp, -1.0, decay_a.unsqueeze(1).to_broadcast([P, NG, H]), ALU.mult, ALU.mult).then_inc(gates_done, 1)

        def gate_act_fn(act):
            gate_marks.wait(act, "gate_raw", 1)
            act.activation(beta, graw[:, :, 0:H], ACT.Sigmoid).then_inc(gate_act, 1)
            act.activation(decay_a, gate0[:, 0, :], ACT.Exp).then_inc(gate_act, 1)
            gate_marks.wait(act, "gate_abs", 1)
            act.activation(gsp, gsp, ACT.Exp, scale=-1.0).then_inc(gate_act, 1)
            act.wait_ge(gate_act, 3)
            act.activation(gsp, gsp, ACT.Ln, bias=1.0).then_inc(gate_act, 1)

        def hv(n):
            return rb[:, 1536 + 512 * n:2048 + 512 * n].rearrange("p (h t) -> p h t", h=H)
        qkvc = rb[:, 0:1536].rearrange("p (k t) -> p k t", k=12)
        decT, eR, lnT, inv_t, inv, xm, attnT, kbg, kdec, vb, qdec, nwT, vnew = (hv(n) for n in range(13))
        gcol = rb[:, 8192:8200].rearrange("p (a h) -> p a h", a=2)
        gexp = rb[:, 8200:8208].rearrange("p (a h) -> p a h", a=2)
        bge = rb[:, 8208:8212]
        gtri = prod[:, 0:512].rearrange("p (h t) -> p h t", h=H)
        bdiag = prod[:, 512:1024].rearrange("p (h t) -> p h t", h=H)
        c_in, gb_in, r_full, tr_full, dec_in, dec_exp, inv_id, inv0, m0_full, m0_copied = (sem(x) for x in (
            "c_in", "gb_in", "r_full", "tr_full", "dec_in", "dec_exp", "inv_id", "inv0", "m0_full", "m0_copied"))
        x_full, x_copied, p_full, pt_full, inv_up, invt_up = (sem(x) for x in ("x_full", "x_copied", "p_full", "pt_full", "inv_up", "invt_up"))
        kv_done, qdec_done, w_full, w_copied, vn_full, vn_copied, oc_full, oc_copied, sn_full, state_up = (sem(x) for x in (
            "kv_done", "qdec_done", "w_full", "w_copied", "vn_full", "vn_copied", "oc_full", "oc_copied", "sn_full", "state_up"))
        wait_carrier = sem("wait_carrier")
        state_zero, vpage_used = sem("state_zero"), sem("vpage_used")
        pacc_used = sem("pacc_used")
        pacc = tmp[:].rearrange("p s c -> p (s c)")[:, 0:H * P].rearrange("p (h e) -> p h e", h=H)
        NL = LEVELS - 1

        def b4(n):
            return bank[:, n, :].rearrange("p (h t) -> p h t", h=H)

        def chunk_sp(sp):
            sp.wait_ge(kpage_used, 16 + B * PG // 2)
            with sp.Fori(0, B) as b:
                for pp in range(PG // 2):
                    sp.wait_ge(vpage_used, b * 8 + (pp + 1))
                    load_pages(sp, a["cache_attn_v"], b, pp, pp % 4)

        def chunk_pool(pool):
            pool.wait_ge(l2_out, 3 + NCH * 2 * H)
            pool.wait_ge(silu_done, 12)
            with pool.Fori(0, NB) as c:
                pool.wait_ge(tr_full, c + 1)
                pool.wait_ge(qdec_done, c + 1)
                pool.tensor_copy(qkvc, qkv[:, :, ds(c * P, P)]).then_inc(c_in, 1)
                pool.wait_ge(vn_full, c + 1)
                pool.sem_inc(wait_carrier, 1)
                pool.tensor_copy(inv_t, ident[:].unsqueeze(1).to_broadcast([P, H, P])).then_inc(inv_id, 1)
                pool.wait_ge(dec_exp, c + 1)
                pool.wait_ge(c_in, c + 1)
                pool.wait_ge(oc_full, c + 1)
                pool.tensor_tensor(qdec, qkvc[:, 0:H, :], eR, ALU.mult).then_inc(qdec_done, 1)

        def chunk_pe(pe):
            pe.sem_inc(tr_full, 1)
            pe.sem_inc(vn_full, 1)
            pe.sem_inc(oc_full, 1)
            pe.wait_ge(state_zero, 1)
            pe.matmul(bank[:, 7, 0:B * H], ones[:, :], state[:, 0, 0:B * H], start=True, stop=False, skip_group_check=True)
            pe.wait_ge(l2_log, 3 + NCH * 2 * H)
            pe.wait_ge(gates_done, 1)

            def sums(c):
                pe.wait_ge(gb_in, c + 1)
                pe.matmul(bank[:, 0, :], ones[:, :], gtri.rearrange("p h t -> p (h t)"), start=True, stop=True)
                pe.matmul(bank[:, 1, :], ones[:, :], bdiag.rearrange("p h t -> p (h t)"), start=True, stop=True)
                pe.matmul(bank[:, 2, 0:H], triu[:, :], small[:, ds(c * H + 320, H)], start=True, stop=True).then_inc(r_full, 1)

            def body(c, last):
                pe.wait_ge(c_in, c + 1)
                pe.wait_ge(w_copied, c + 1)
                pe.wait_ge(vn_copied, c + 1)
                pe.wait_ge(oc_copied, c + 1)
                pe.wait_ge(state_up, c + 1)
                for n, (l, r) in enumerate(((4, 4), (4, 0))):
                    for h in range(H):
                        pe.matmul(b4(3 + n)[:, h, :], qkvc[:, l + h, :], qkvc[:, r + h, :], start=True, stop=True)
                for n in range(2):
                    for h in range(H):
                        mm = pe.transpose(b4(5 + n)[:, h, :], qkvc[:, 4 + 4 * n + h, :], ident[:, :])
                mm.then_inc(tr_full, 1)
                pe.wait_ge(inv0, c + 1)
                for h in range(H):
                    mm = pe.transpose(b4(2)[:, h, :], inv_t[:, h, :], ident[:, :])
                mm.then_inc(m0_full, 1)
                for lv in range(NL):
                    if lv == 0:
                        pe.wait_ge(m0_copied, c + 1)
                    else:
                        pe.wait_ge(inv_up, c * (NL - 1) + lv)
                    for h in range(H):
                        mm = pe.matmul(b4(0)[:, h, :], lnT[:, h, :], inv[:, h, :], start=True, stop=True)
                    mm.then_inc(x_full, 1)
                    pe.wait_ge(x_copied, c * NL + lv + 1)
                    if lv:
                        pe.wait_ge(invt_up, c * NL + lv + 1)
                    if lv < NL - 1:
                        for h in range(H):
                            mm = pe.matmul(b4(1)[:, h, :], inv_t[:, h, :], xm[:, h, :], start=True, stop=True)
                        mm.then_inc(p_full, 1)
                    for h in range(H):
                        mm = pe.matmul(b4(2)[:, h, :], xm[:, h, :], inv_t[:, h, :], start=True, stop=True)
                    mm.then_inc(pt_full, 1)
                pe.wait_ge(kv_done, c + 1)
                pe.wait_ge(invt_up, c * NL + NL + 1)
                for h in range(H):
                    mm = pe.matmul(b4(3)[:, h, :], kbg[:, h, :], inv_t[:, h, :], start=True, stop=True)
                mm.then_inc(w_full, 1)
                pe.wait_ge(w_copied, c + 2)
                for h in range(H):
                    pe.matmul(b4(4)[:, h, :], inv_t[:, h, :], vb[:, h, :], start=True, stop=False)
                    mm = pe.matmul(b4(4)[:, h, :], nwT[:, h, :], state[:, h, :], start=False, stop=True)
                mm.then_inc(vn_full, 1)
                if not last:
                    sums(c + 1)
                pe.wait_ge(vn_copied, c + 2)
                pe.wait_ge(qdec_done, c + 2)
                for h in range(H):
                    pe.matmul(b4(5)[:, h, :], state[:, h, :], qdec[:, h, :], start=True, stop=False)
                    mm = pe.matmul(b4(5)[:, h, :], vnew[:, h, :], attnT[:, h, :], start=False, stop=True)
                mm.then_inc(oc_full, 1)
                for h in range(H):
                    mm = pe.matmul(b4(6)[:, h, :], kdec[:, h, :], vnew[:, h, :], start=True, stop=True)
                mm.then_inc(sn_full, 1)
                pe.wait_ge(vpage_used, c * 8 + 12)
                for h in range(H):
                    mm = pe.matmul(bank[:, 7, ds(c * H + h, 1)], pacc[:, h, :], ones[:, 0:1], start=False, stop=False, skip_group_check=True)
                mm.then_inc(pacc_used, 1)

            sums(0)
            with pe.Fori(0, NB - 1) as c:
                body(c, False)
            body(NB - 1, True)
        awflat = aw[:].rearrange("p b g h -> p (b g h)")

        def chunk_act(act):
            for s in (w_copied, vn_copied, oc_copied):
                act.sem_inc(s, 1)
            with act.Fori(0, NB) as c:
                act.wait_ge(dec_in, c + 1)
                act.activation(decT, decT, ACT.Exp)
                act.wait_ge(qdec_done, c + 1)
                act.wait_ge(state_up, c + 1)
                act.activation(eR, b4(0), ACT.Exp)
                act.activation(gexp, gcol, ACT.Exp).then_inc(dec_exp, 1)
                act.wait_ge(m0_full, c + 1)
                act.activation(inv, b4(2), ACT.Copy).then_inc(m0_copied, 1)
                for lv in range(NL):
                    act.wait_ge(x_full, c * NL + lv + 1)
                    act.activation(xm, b4(0), ACT.Copy).then_inc(x_copied, 1)
                act.wait_ge(w_full, c + 1)
                act.activation(nwT, b4(3), ACT.Copy, scale=-1.0).then_inc(w_copied, 1)
                act.wait_ge(vn_full, c + 2)
                act.activation(vnew, b4(4), ACT.Copy).then_inc(vn_copied, 1)
                act.wait_ge(oc_full, c + 2)
                act.activation(res_a[:, H:2 * H, ds(c * P, P)], b4(5), ACT.Copy).then_inc(oc_copied, 1)

        def chunk_dve(dve, step):
            dve.memset(state[:], 0.0).then_inc(state_zero, 1)
            dve.wait_ge(state_zero, 1)
            dve.sem_inc(invt_up, 1)
            dve.sem_inc(state_up, 1)
            dve.wait_ge(gates_done, 1)
            dve.sem_inc(vpage_used, 4)
            dve.sem_inc(pacc_used, 1)

            def values(c, pp):
                dve.wait_ge(page_in[pp % 4], c * 64 + (512 + 32 * (pp // 4 + 1)))
                if pp == 0:
                    dve.wait_ge(pacc_used, c + 1)
                dve.sem_inc(wait_carrier, 1)
                for u in range(2):
                    for h in range(H):
                        v = ring[:, pp % 4, u, h * P:(h + 1) * P]
                        w = awflat[:, ds(c * (PG * H) + ((2 * pp + u) * H + h), 1)]
                        if pp == u == 0:
                            last = dve.tensor_scalar(pacc[:, h, :], v, w, None, ALU.mult)
                        else:
                            last = dve.scalar_tensor_tensor(pacc[:, h, :], v, w, pacc[:, h, :], ALU.mult, ALU.add)
                    if u == 0:
                        step(last)
                    else:
                        last.then_inc(vpage_used, 1)
                        dve.wait_ge(vpage_used, c * 8 + (pp + 5))

            def gates_spread(c):
                gc_ = small[:, ds(c * H + 320, H)]
                bc_ = small[:, ds(c * H + 128, H)]
                dve.tensor_tensor(gtri, triu[:].unsqueeze(1).to_broadcast([P, H, P]), gc_.unsqueeze(2).to_broadcast([P, H, P]), ALU.mult)
                dve.tensor_tensor(bdiag, ident[:].unsqueeze(1).to_broadcast([P, H, P]), bc_.unsqueeze(2).to_broadcast([P, H, P]), ALU.mult).then_inc(gb_in, 1)

            def decays(c):
                dve.wait_ge(r_full, c + 1)
                step(dve.tensor_copy(gcol[:, 0, :], bank[:, 2, 0:H]))
                dve.tensor_tensor(gcol[:, 1, :], b4(0)[:, :, P - 1], gcol[:, 0, :], ALU.subtract)
                for h in range(H):
                    last = dve.scalar_tensor_tensor(decT[:, h, :], b4(0)[:, h, :], gcol[:, 0, h:h + 1], causal[:, :], ALU.subtract, ALU.add)
                last.then_inc(dec_in, 1)

            def body(c, last_chunk):
                bc_ = small[:, ds(c * H + 128, H)]
                values(c, 0)
                dve.wait_ge(dec_exp, c + 1)
                dve.wait_ge(tr_full, c + 2)
                step(dve.scalar_tensor_tensor(lnT, b4(3), -1.0, decT, ALU.mult, ALU.mult))
                step(dve.tensor_tensor(lnT, lnT, b4(1), ALU.mult))
                dve.wait_ge(inv_id, c + 1)
                dve.sem_inc(wait_carrier, 1)
                dve.copy_predicated(inv_t, merge[:, 1, 0, :].unsqueeze(1).to_broadcast([P, H, P]), lnT).then_inc(inv0, 1)
                dve.tensor_tensor(attnT, b4(4), decT, ALU.mult)
                step(dve.tensor_tensor(bge, gexp[:, 0, :], bc_, ALU.mult))
                dve.tensor_tensor(kbg, b4(5), bge.unsqueeze(2).to_broadcast([P, H, P]), ALU.mult)
                dve.tensor_tensor(kdec, b4(5), gexp[:, 1, :].unsqueeze(2).to_broadcast([P, H, P]), ALU.mult)
                dve.tensor_tensor(vb, b4(6), bc_.unsqueeze(2).to_broadcast([P, H, P]), ALU.mult).then_inc(kv_done, 1)
                values(c, 1)
                dve.wait_ge(m0_copied, c + 1)
                for lv in range(NL):
                    if lv < NL - 1:
                        dve.wait_ge(p_full, c * (NL - 1) + lv + 1)
                        dve.sem_inc(wait_carrier, 1)
                        dve.copy_predicated(inv, merge[:, 0, lv + 1, :].unsqueeze(1).to_broadcast([P, H, P]), b4(1)).then_inc(inv_up, 1)
                    dve.wait_ge(pt_full, c * NL + lv + 1)
                    dve.sem_inc(wait_carrier, 1)
                    dve.copy_predicated(inv_t, merge[:, 1, lv + 1, :].unsqueeze(1).to_broadcast([P, H, P]), b4(2)).then_inc(invt_up, 1)
                    if lv == NL - 1 and not last_chunk:
                        gates_spread(c + 1)
                    values(c, 2 + lv)
                if not last_chunk:
                    decays(c + 1)
                dve.wait_ge(sn_full, c + 1)
                for h in range(H):
                    last = dve.scalar_tensor_tensor(state[:, h, :], state[:, h, :], eR[:, h, P - 1:P], b4(6)[:, h, :], ALU.mult, ALU.add)
                last.then_inc(state_up, 1)

            gates_spread(0)
            decays(0)
            with dve.Fori(0, NB - 1) as c:
                step.enter(c, 12)
                body(c, False)
            step.leave(NB - 1)
            body(NB - 1, True)

        s_att, s_asq, s_arstd = small[:, 0:32], small[:, 32:64], small[:, 64:96]
        s_k, s_q, s_v = small[:, 96:128], small[:, 388:420], small[:, 420:452]
        s_eg, s_vn = small[:, 192:224], small[:, 224:256]
        s_beta = small[:, 160:192]
        U = B * H
        sst = rb[:, 0:U * P].rearrange("p (u e) -> p u e", u=U)
        vbig = rb[0:U, U * P:2 * U * P].rearrange("p (u e) -> p u e", u=U)
        srow = tmp[:].rearrange("p s c -> p (s c)")[0:U, 0:2 * P]
        s_dve = Marks(sem("sample_dve"), sa_sq=1, s_cols=1, s_mixed=1, vn_s=1, vbig_done=1)
        s_pe = Marks(sem("sample_pe"), gn_full=1, sa_mm=1, ks_full=1, row_full=1)
        s_act = Marks(sem("sample_act"), s_egs=1, sa_log=1, sa_rstd=1, gn_copied=3, row_copied=1)
        sst_in, sst_mm, sst_add, so_full, s_done = (sem(x) for x in ("sst_in", "sst_mm", "sst_add", "so_full", "s_done"))
        x_back = sem("x_back")
        misc_out = sem("misc_out")
        grow = prod
        grow3 = flat(17 * TT, CQ, parts=GW - 1 + B)
        STORES = 7

        def store(pool, dst, src):
            pool.dma_start(dst, src).then_inc(misc_out, 16)

        def sample_pool(pool):
            pool.wait_ge(state_up, NB + 1)
            store(pool, o["new_gdn_s_prompt"].rearrange("e b h d v -> d (e b h) v"), state[:])
            pool.wait_ge(oc_copied, NB + 1)
            pool.dma_start(sst, a["state_gdn_s"].rearrange("e b h d v -> d (e b h) v")).then_inc(sst_in, 16)
            store(pool, o["new_gdn_conv_sample"][0, :, 0:GW - 2, :], a["state_gdn_conv"][0, :, 1:GW - 1, :])
            store(pool, o["new_conv_buf_sample"][0, :, 0:CW - 2, :], a["state_conv_buf"][0, :, 1:CW - 1, :])
            s_act.wait(pool, "gn_copied", 3)
            store(pool, o["new_gdn_conv_prompt"].rearrange("e b w c -> (e b w) c"), grow3[0:GW - 1, :])
            store(pool, o["new_gdn_conv_sample"][0, :, GW - 2, :], grow3[GW - 1:GW - 1 + B, :])
            pool.wait_ge(sst_add, 8)
            pool.dma_start(o["new_gdn_s_sample"].rearrange("e b h d v -> d (e b h) v"), sst).then_inc(sst_in, 16)
            pool.wait_ge(so_full, 1)
            pool.wait_ge(sst_in, 32)
            pool.dma_start(rb, park.ap()).then_inc(x_back, 16)

        def sample_pe(pe):
            pe.wait_ge(state_up, NB + 1)
            pe.wait_ge(oc_copied, NB + 1)
            pe.wait_ge(invt_up, NB * NL + 1)
            for k in range(12):
                mm = pe.transpose(bank[0:GW - 1 + B, 3 + k // 4, k % 4 * P:(k % 4 + 1) * P], gnew[:, k, :], ident[:, :])
            mm.then_inc(s_pe.sem, 1)
            s_dve.wait(pe, "sa_sq", 1)
            pe.matmul(bank[:, 2, 0:U], ones[:, :], s_asq, start=True, stop=True).then_inc(s_pe.sem, 1)
            pe.wait_ge(sst_in, 16)
            s_dve.wait(pe, "s_cols", 1)
            for u in range(U):
                mm = pe.matmul(bank[:, 0, u:u + 1], sst[:, u, :], s_k[:, u:u + 1], start=True, stop=True)
            mm.then_inc(s_pe.sem, 1)
            s_dve.wait(pe, "vn_s", 1)
            pe.transpose(bank[0:U, 1, 0:P], s_vn, ident[:, :])
            pe.transpose(bank[0:U, 1, P:2 * P], s_k, ident[:, :]).then_inc(s_pe.sem, 1)
            s_dve.wait(pe, "vbig_done", 1)
            s_act.wait(pe, "gn_copied", 3)
            for j in range(8):
                if j >= 4:
                    pe.wait_ge(sst_add, j - 3)
                pe.matmul(bank[:, 3 + j % 4, :], srow[:, P:2 * P], vbig[:, 4 * j:4 * j + 4, :].rearrange("p u e -> p (u e)"), start=True, stop=True).then_inc(sst_mm, 1)
            pe.wait_ge(sst_add, 8)
            for u in range(U):
                mm = pe.matmul(bank[:, 0, u:u + 1], sst[:, u, :], s_q[:, u:u + 1], start=True, stop=True)
            mm.then_inc(so_full, 1)

        def sample_act(act):
            act.wait_ge(gates_done, 1)
            act.activation(s_eg, small[:, 320 + 32:384], ACT.Exp).then_inc(s_act.sem, 1)
            s_pe.wait(act, "sa_mm", 1)
            act.activation(s_arstd, bank[:, 2, 0:U], ACT.Ln, scale=1.0 / P, bias=1e-5).then_inc(s_act.sem, 1)
            s_act.wait(act, "sa_log", 1)
            act.activation(s_arstd, s_arstd, ACT.Exp, scale=-0.5).then_inc(s_act.sem, 1)
            s_pe.wait(act, "gn_full", 1)
            for n in range(3):
                act.activation(grow3[:, n * 512:(n + 1) * 512], bank[0:GW - 1 + B, 3 + n, :], ACT.Copy).then_inc(s_act.sem, 1)
            s_pe.wait(act, "row_full", 1)
            act.activation(srow, bank[0:U, 1, 0:2 * P], ACT.Copy).then_inc(s_act.sem, 1)

        def sample_dve(dve, step):
            dve.wait_ge(pacc_used, 1 + B)
            dve.wait_ge(l2_out, 3 + NCH * 2 * H)
            step(dve.tensor_tensor(s_att.rearrange("p (b h) -> p b h", b=B), ownw.rearrange("p (b h) -> p b h", b=B),
                                   sq[:, 2 * H:3 * H, :].rearrange("p h b -> p b h"), ALU.mult))
            step(dve.tensor_tensor(s_att, s_att, bank[:, 7, 0:U], ALU.add))
            dve.tensor_tensor(s_asq, s_att, s_att, ALU.mult).then_inc(s_dve.sem, 1)
            for d, k in ((s_q, 0), (s_k, H), (s_v, 2 * H)):
                last = dve.tensor_copy(d.rearrange("p (b h) -> p b h", b=B), qkv[:, k:k + H, T:TT].rearrange("p h b -> p b h"))
            last.then_inc(s_dve.sem, 1)
            s_dve.wait(dve, "s_cols", 1)
            s_act.wait(dve, "sa_rstd", 1)
            dve.scalar_tensor_tensor(mix[:, 0:H, T:TT].rearrange("p h b -> p b h"), s_att.rearrange("p (b h) -> p b h", b=B), hw[:, 0:1],
                                     s_arstd.rearrange("p (b h) -> p b h", b=B), ALU.mult, ALU.mult).then_inc(s_dve.sem, 1)
            s_pe.wait(dve, "ks_full", 1)
            s_act.wait(dve, "s_egs", 1)
            step(dve.tensor_tensor(s_vn, bank[:, 0, 0:U], s_eg, ALU.mult))
            step(dve.tensor_tensor(s_vn, s_v, s_vn, ALU.subtract))
            dve.tensor_tensor(s_vn, s_vn, s_beta, ALU.mult).then_inc(s_dve.sem, 1)
            step(dve.tensor_tensor(sst, sst, s_eg.unsqueeze(2).to_broadcast([P, U, P]), ALU.mult))
            s_act.wait(dve, "row_copied", 1)
            dve.tensor_tensor(vbig, ident[0:U, 0:U].unsqueeze(2).to_broadcast([U, U, P]), srow[:, 0:P].unsqueeze(1).to_broadcast([U, U, P]),
                              ALU.mult).then_inc(s_dve.sem, 1)
            for j in range(8):
                dve.wait_ge(sst_mm, j + 1)
                d = sst[:, 4 * j:4 * j + 4, :]
                dve.tensor_tensor(d, d, bank[:, 3 + j % 4, :].rearrange("p (u e) -> p u e", u=4), ALU.add).then_inc(sst_add, 1)
            dve.wait_ge(so_full, 1)
            dve.tensor_copy(mix[:, H:2 * H, T:TT].rearrange("p h b -> p b h"), bank[:, 0, 0:U].rearrange("p (b h) -> p b h", b=B)).then_inc(s_done, 1)

        on_sq, on_mm, on_log, on_rstd, on_scaled, on_out = l2_sq, l2_mm, l2_log, l2_inv, l2_out, sem("on_out")
        L2 = NCH * 2 * H

        def onorm_pe(pe):
            pe.wait_ge(s_done, 1)
            with pe.Fori(0, H) as i:
                for c in range(NCH):
                    pe.wait_ge(on_sq, i * NCH + (L2 + c + 1))
                    pe.wait_ge(on_log, i * NCH + (L2 + c + 1))
                    pe.matmul(bank[:, 4 + c, 0:CH], ones[:, :], tmp[:, c, :], start=True, stop=True).then_inc(on_mm, 1)

        def onorm_act(act):
            act.wait_ge(s_done, 1)
            with act.Fori(0, H) as i:
                for c in range(NCH):
                    act.wait_ge(on_mm, i * NCH + (L2 + c + 1))
                    act.activation(tmp[:, c, :], vflat[:, ds(i * TT + (4 * TT + c * CH), CH)], ACT.Square).then_inc(on_sq, 1)
                for c in range(NCH):
                    act.wait_ge(on_mm, i * NCH + (L2 + c + 4))
                    act.wait_ge(on_scaled, i * NCH + (L2 + c + 1))
                    act.activation(rstd[:, c, :], bank[:, 4 + c, 0:CH], ACT.Ln, scale=1.0 / P, bias=1e-6).then_inc(on_log, 1)
                for c in range(NCH):
                    act.wait_ge(on_log, i * NCH + (L2 + c + 4))
                    act.activation(rstd[:, c, :], rstd[:, c, :], ACT.Exp, scale=-0.5).then_inc(on_rstd, 1)

        def onorm_dve(dve):
            dve.wait_ge(z_gated, 1)
            with dve.Fori(0, H) as i:
                for c in range(NCH):
                    dve.wait_ge(on_rstd, i * NCH + (L2 + c + 1))
                    d = vflat[:, ds(i * TT + (4 * TT + c * CH), CH)]
                    dve.scalar_tensor_tensor(d, d, hw[:, 1:2], rstd[:, c, :], ALU.mult, ALU.mult).then_inc(on_scaled, 1)
                for c in range(NCH):
                    dve.wait_ge(on_scaled, i * NCH + (L2 + c + 4))
                    d = vflat[:, ds(i * TT + (4 * TT + c * CH), CH)]
                    dve.tensor_tensor(d, d, big[:, ds(i * TT + (12 * TT + c * CH), CH)], ALU.mult).then_inc(on_out, 1)

        g_out = Gemm(g_sems, 2)
        x, xn = res_b, res_a
        xf = rb

        def add_out(dve, g, tile_of, bias=None):
            g.grant(dve, [0, 1])
            with dve.Fori(0, g.rounds) as i:
                for j in range(g.per):
                    g.wait_full(dve, i, j)
                    n, c = tile_of(i, j)
                    d = xf[:, ds(n * TT + c * CH, CH)]
                    if bias is None:
                        dve.tensor_tensor(d, d, bank[:, j % 6, 0:CH], ALU.add).then_inc(g.free[j % 2], 1)
                    else:
                        dve.scalar_tensor_tensor(d, bank[:, j % 6, 0:CH], vecf[:, ds(n * NV + bias, 1)], d, ALU.add, ALU.add).then_inc(g.free[j % 2], 1)
        vecf = vec[:].rearrange("p k v -> p (k v)")

        def four_tiles(i, j):
            return i * 4 + j // NCH, j % NCH

        def two_tiles(i, j):
            return i * 2 + j // NCH, j % NCH

        def out_pe(pe):
            s_dve.wait(pe, "s_mixed", 1)
            pe.wait_ge(on_out, NCH * H)
            project_pe(pe, g_out, mix)
            
        def out_dve(dve):
            dve.wait_ge(x_back, 16)
            add_out(dve, g_out, four_tiles)

        w_out0 = a["w_out"].rearrange("e k n -> (e k) n")

        class Ffn:
            UP, ROUND = 12, 12 + KD * NCH

            def __init__(self, layer, nn):
                self.layer, self.nn = layer, nn
                self.gemm = self.down = Gemm(g_sems, KF // 2, (self.ROUND - 1,) * 4)
                self.units0 = layer * 6 * (KF // 2)
                self.hid0 = layer * 6 * (KF // 2)

        HID = KD * TT
        SPL = HID + 4 * TT
        xh = rounded("xh", "res_a", 0, [P, KD, TT])
        xl = rounded("xl", "big", 0, [P, KD, TT])
        x_scaled = flat(0, KD, TT)
        hh = rounded("hh", "big", HID, [P, 2, TT])
        hl = rounded("hl", "big", HID + 2 * TT, [P, 2, TT])
        WQ = 3
        wflat = wring[:].rearrange("p s k n -> p (s k n)")
        raw_w = [wflat[:, r * D:(r + 1) * D] for r in range(WQ)]
        wh = [rounded(f"wh{u}", "big", SPL + u * 2 * D, [P, D]) for u in range(5)] + [rounded("wh5", "wring", WQ * D, [P, D])]
        wl = [rounded(f"wl{u}", "big", SPL + u * 2 * D + D, [P, D]) for u in range(5)] + [rounded("wl5", "wring", (WQ + 1) * D, [P, D])]
        raw_in = [sem(f"raw_in{r}") for r in range(WQ)]
        wh_done, w_cut = sem("wh_done"), sem("w_cut")
        xh_done, x_cut = sem("xh_done"), sem("x_cut")
        hid_cut = sem("hid_cut")

        f0 = Ffn(0, 1)

        def pair_pe(pe, g, xin, ready):
            with pe.Fori(0, g.rounds) as i:
                for t in range(2):
                    wait_slab(pe, i, 2 * t)
                    wait_slab(pe, i, 2 * t + 1)
                    for c in range(NCH):
                        if t == 0:
                            ready(c)
                        for u in range(2):
                            job(pe, g, i, 6 * t + 2 * c + u, [(2 * t + u, KD)], lambda k, j, c=c: xin[:, k, chunk(c)])
            w_rounds[1] += g.rounds

        def ffn_sp(sp, f, before):
            wg, wu, wd = (a[n][f.layer] for n in ("ffn_w_gate", "ffn_w_up", "ffn_w_down"))
            before.wait_full(sp, before.rounds - 1, before.per - 1)

            def unit(i, u, first=False):
                if not first:
                    sp.wait_ge(w_cut, i * 6 + (f.units0 + u - WQ + 1))
                if u < 4:
                    src, dst = cols((wg, wu)[u % 2], i * 2 + u // 2), raw_w[u % WQ].rearrange("p (k n) -> p k n", k=KD)
                else:
                    src, dst = wd[ds(i * (2 * P) + (u - 4) * P, P), :], raw_w[u % WQ]
                sp.dma_start(dst, src).then_inc(raw_in[u % WQ], 16)

            for u in range(6):
                unit(0, u, f.layer == 0 and u < WQ)
            with sp.Fori(1, KF // 2) as i:
                for u in range(6):
                    unit(i, u)

        def cut_products(pe, bank_out, terms, done):
            for n, (h, l, mh, ml) in enumerate(terms):
                pe.matmul(bank_out, h, mh, start=(n == 0), stop=False)
                pe.matmul(bank_out, h, ml, start=False, stop=False)
                mm = pe.matmul(bank_out, l, mh, start=False, stop=(n == len(terms) - 1))
            mm.then_inc(done, 1)

        def ffn_pe(pe, f):
            norm_pe(pe, f.nn)
            g = f.gemm
            with pe.Fori(0, g.rounds) as i:
                for t in range(2):
                    for c in range(NCH):
                        if t == 0:
                            pe.wait_ge(x_cut, NCH * f.layer + c + 1)
                        for u in range(2):
                            if c == 0:
                                pe.wait_ge(w_cut, i * 6 + (f.units0 + 2 * t + u + 1))
                            j, s = 6 * t + 2 * c + u, 2 * t + u
                            g.wait_bank(pe, i, j)
                            cut_products(pe, bank[:, j % 6, 0:CH], [(wh[s][:, k * P:(k + 1) * P], wl[s][:, k * P:(k + 1) * P],
                                         xh[:, k, chunk(c)], xl[:, k, chunk(c)]) for k in range(KD)], g.full)
                pe.wait_ge(w_cut, i * 6 + (f.units0 + 6))
                for c in range(NCH):
                    pe.wait_ge(hid_cut, i * 6 + (f.hid0 + 3 + NCH + c + 1))
                    for n in range(KD):
                        j = f.UP + KD * c + n
                        g.wait_bank(pe, i, j)
                        cut_products(pe, bank[:, j % 6, 0:CH], [(wh[4 + k][:, n * P:(n + 1) * P], wl[4 + k][:, n * P:(n + 1) * P],
                                     hh[:, k, chunk(c)], hl[:, k, chunk(c)]) for k in range(2)], g.full)

        def ffn_act(act, f, before):
            before.wait_all_read(act)
            if f.layer:
                act.wait_ge(misc_out, 16 * STORES)

            def cut(i, u):
                act.wait_ge(raw_in[u % WQ], i * 32 + 16 * (f.units0 // WQ + u // WQ + 1))
                act.activation(wh[u][:, :], raw_w[u % WQ], ACT.Copy).then_inc(wh_done, 1)

            def gates(i, t):
                for c in range(NCH):
                    g.wait_full(act, i, 6 * t + 2 * c)
                    act.wait_ge(hid_cut, i * 6 + (f.hid0 + NCH * t + c + 1))
                    act.activation(tmp[:, c, :], bank[:, 2 * c, 0:CH], ACT.Silu).then_inc(g.free[0], 1)

            g = f.gemm
            before.wait_full(act, before.rounds - 1, before.per - 1)
            cut(0, 0)
            cut(0, 1)
            norm_act(act, f.nn, x, copy=lambda c: stream_high(act, f, c))
            cut(0, 2)
            cut(0, 3)
            act.wait_ge(n_mm, KD * NCH * (f.nn + 1))

            def body(i, last):
                g.wait_full(act, i, -1)
                cut(i, 4)
                cut(i, 5)
                g.wait_read(act, i, -2)
                gates(i, 0)
                if not last:
                    g.wait_full(act, i, 5)
                    cut(i + 1, 0)
                    cut(i + 1, 1)
                gates(i, 1)
                if not last:
                    g.wait_full(act, i, 11)
                    cut(i + 1, 2)
                    cut(i + 1, 3)

            with act.Fori(0, g.rounds - 1) as i:
                body(i, False)
            body(g.rounds - 1, True)

        def stream_high(act, f, c):
            act.wait_ge(n_out, KD * (NCH * f.nn + c + 1))
            act.activation(xh[:, :, chunk(c)], x_scaled[:, :, chunk(c)], ACT.Copy).then_inc(xh_done, 1)

        def ffn_pool(pool, f):
            def cut(i, u):
                pool.wait_ge(wh_done, i * 6 + (f.units0 + u + 1))
                pool.tensor_tensor(wl[u][:, :], raw_w[u % WQ], wh[u][:, :].bitcast(F32), ALU.subtract).then_inc(w_cut, 1)

            with pool.Fori(0, KF // 2) as i:
                for u in range(6):
                    cut(i, u)

        def ffn_dve(dve, f, before, step):
            before.wait_all_read(dve)
            if f.layer:
                dve.wait_ge(misc_out, 16 * STORES)

            def stream_low(c):
                dve.wait_ge(xh_done, NCH * f.layer + c + 1)
                dve.tensor_tensor(xl[:, :, chunk(c)], x_scaled[:, :, chunk(c)], xh[:, :, chunk(c)].bitcast(F32), ALU.subtract).then_inc(x_cut, 1)
            norm_dve(dve, f.nn, x, x_scaled, V_FFN0 + f.layer, after=stream_low)
            g = f.gemm
            if f.layer == 0:
                dve.sem_inc(hid_cut, 3)
            with dve.Fori(0, g.rounds) as i:
                step.enter(i, 6)
                for t in range(2):
                    for c in range(NCH):
                        g.wait_full(dve, i, 6 * t + 2 * c + 1)
                        g.wait_pair(dve, i, 6 * t + 2 * c, 0)
                        dve.tensor_tensor(tmp[:, c, :], bank[:, 2 * c + 1, 0:CH], tmp[:, c, :], ALU.mult).then_inc(g.free[1], 1)
                        g.wait_pair(dve, i, 6 * t + 2 * c, 1)
                        step(dve.tensor_copy(hh[:, t, chunk(c)], tmp[:, c, :]))
                        dve.tensor_tensor(hl[:, t, chunk(c)], tmp[:, c, :], hh[:, t, chunk(c)].bitcast(F32), ALU.subtract).then_inc(hid_cut, 1)
                for c in range(NCH):
                    for n in range(KD):
                        j = f.UP + KD * c + n
                        g.wait_full(dve, i, j)
                        dve.tensor_tensor(x[:, n, chunk(c)], x[:, n, chunk(c)], bank[:, j % 6, 0:CH], ALU.add).then_inc(g.free[j % 2], 1)
            step.leave(g.rounds)

        g_pw1 = Gemm(g_sems, 4, (4, 5, 10, 11))
        g_pw2 = Gemm(g_sems, 2)
        f1 = Ffn(1, 4)
        w_pw1 = a["conv_w_pw1"].rearrange("e k n -> (e k) n")
        w_pw2 = a["conv_w_pw2"].rearrange("e k n -> (e k) n")
        HIST = CW - 1
        glu = flat(0, KD, GL)
        cout = flat(KD * GL, KD, TT)
        coutf = big[:, KD * GL:KD * (GL + TT)]
        C1 = KD * (GL + TT)
        shist = flat(C1, KD, B, HIST)
        ssum8 = flat(C1 + KD * B * HIST, KD, B)
        C2 = C1 + KD * B * HIST + KD * B
        srows2 = flat(C2, 2, D, parts=B * HIST // 2)
        wprod = flat(C2, 2, T)
        wacc = flat(C2 + 2 * T, T)
        NPOOL = 11
        TAPS = CW - NPOOL
        NDIAG, NLAST = 10, 8
        diags = [probs[:].rearrange("p b g x -> p (b g x)")[:, q * P:(q + 1) * P] for q in range(8)]
        diags += [aw[:].rearrange("p b g h -> p (b g h)")[:, q * P:(q + 1) * P] for q in range(NDIAG - 8)]
        diag_set, diag_full = sem("diag_set"), sem("diag_full")
        crow = flat(C2, D, parts=HIST + B)
        hist_zero, hist_in, hist_full, hist_copied = (sem(x) for x in ("hist_zero", "hist_in", "hist_full", "hist_copied"))
        tap_in, tap_added, tile_conv = sem("tap_in"), sem("tap_added"), sem("tile_conv")
        crow_full, crow_copied, samples_conv = sem("crow_full"), sem("crow_copied"), sem("samples_conv")
        mu_full, mu_in, centred, ln_silu = sem("mu_full"), sem("mu_in"), sem("centred"), sem("ln_silu")

        def conf_pool(pool, step):
            f0.down.wait_all_read(pool)
            for u in range(2):
                src = a["state_conv_buf"].rearrange("e b w d -> (e b w) d")[120 * u:120 * (u + 1), :]
                pool.dma_start(srows2[:, u, :], src).then_inc(hist_in, 16)
            pool.wait_ge(hist_full, 1)
            pool.sem_inc(tap_added, 2)
            def add_taps(n, taps):
                for q in range(taps - 1):
                    pool.wait_ge(tap_in, n * NPOOL + q + 2)
                    step(pool.tensor_tensor(wacc, wacc, wprod[:, q % 2, :], ALU.add))
                    pool.sem_inc(tap_added, 1)
            with pool.Fori(0, KD - 1) as n:
                step.enter(n, NPOOL - 1)
                add_taps(n, NPOOL)
            step.leave(KD - 1)
            add_taps(KD - 1, NLAST)
            pool.wait_ge(crow_copied, 2)
            store(pool, o["new_conv_buf_prompt"].rearrange("e b w c -> (e b w) c"), crow[0:HIST, :])
            store(pool, o["new_conv_buf_sample"][0, :, HIST - 1, :], crow[HIST:HIST + B, :])

        def conf_pe(pe):
            norm_pe(pe, 2)
            pe.wait_ge(hist_in, 32)
            for u in range(2):
                for k in range(KD):
                    mm = pe.transpose(bank[:, 2 * u + k // 4, k % 4 * 120:(k % 4 + 1) * 120], srows2[:, u, k * P:(k + 1) * P], ident[0:120, 0:120])
            mm.then_inc(hist_full, 1)
            pe.wait_ge(hist_copied, 4)
            pair_pe(pe, g_pw1, xn, lambda c: pe.wait_ge(n_out, KD * (NCH * 2 + c + 1)))
            g_pw1.wait_all_read(pe)
            for k in range(KD):
                mm = pe.transpose(bank[0:HIST + B, k // 4, k % 4 * P:(k % 4 + 1) * P], glu[:, k, T:GL], ident[:, :])
            mm.then_inc(crow_full, 1)
            pe.wait_ge(diag_set, NDIAG)
            for q in range(NDIAG):
                for v in range(2):
                    mm = pe.matmul(bank[:, 5 + v, :], diags[q], glu[:, KD - 1, q + 512 * v:q + 512 * (v + 1)], start=(q == 0), stop=(q == NDIAG - 1))
            mm.then_inc(diag_full, 1)
            pe.wait_ge(samples_conv, 1)
            for k in range(KD):
                pe.wait_ge(tile_conv, k + 1)
                for c in range(NCH):
                    mm = pe.matmul(bank[:, 2 + c, 0:CH], ones[:, :], cout[:, k, chunk(c)], start=(k == 0), stop=(k == KD - 1))
                    if k == KD - 1:
                        mm.then_inc(mu_full, 1)
            norm_pe(pe, 3)
            pe.wait_ge(crow_copied, 2)
            project_pe(pe, g_pw2, cout, lambda c: pe.wait_ge(ln_silu, KD * (c + 1)))

        def conf_act(act):
            f0.down.wait_all_read(act)
            norm_act(act, 2, x)
            act.wait_ge(hist_full, 1)
            for u in range(2):
                for v in range(2):
                    d = shist[:, 4 * v:4 * v + 4, :, :].rearrange("p k b w -> p k (b w)")[:, :, 120 * u:120 * u + 120]
                    act.activation(d, bank[:, 2 * u + v, 0:480].rearrange("p (k r) -> p k r", k=4), ACT.Copy).then_inc(hist_copied, 1)
            for q in range(NDIAG):
                act.activation(diags[q], ident[:, :], ACT.Copy, scale=vec[:, KD - 1, V_WDW + q:V_WDW + q + 1]).then_inc(diag_set, 1)
            g = g_pw1
            g.grant(act, [0])
            act.wait_ge(n_mm, KD * NCH * 3)

            def taps(n, q0, q1):
                for q in range(q0, q1):
                    src = big[:, ds(n * GL + (TAPS + q), T)]
                    w = vecf[:, ds(n * NV + (V_WDW + TAPS + q), 1)]
                    if q == 0:
                        act.wait_ge(tile_conv, n)
                        act.sem_inc(wait_carrier, 1)
                        act.activation(wacc, src, ACT.Copy, scale=w).then_inc(tap_in, 1)
                    else:
                        act.wait_ge(tap_added, n * (NPOOL - 1) + q)
                        act.sem_inc(wait_carrier, 1)
                        act.activation(wprod[:, (q - 1) % 2, :], src, ACT.Copy, scale=w).then_inc(tap_in, 1)

            def gate(i, t, c):
                g.wait_full(act, i, 6 * t + 2 * c)
                g.wait_pair(act, i, 6 * t + 2 * c - 6, 1)
                act.sem_inc(wait_carrier, 1)
                act.activation(tmp[:, c, :], bank[:, 2 * c, 0:CH], ACT.Sigmoid, bias=vecf[:, ds(i * (2 * NV) + (t * NV + V_BG), 1)]).then_inc(g.free[0], 1)

            for t in range(2):
                for c in range(NCH):
                    gate(0, t, c)
                    if t == 1:
                        g.wait_pair(act, 0, 4, 1)
                        act.wait_ge(hist_zero, 1)
                        taps_first(act, *SPLIT[c])
            with act.Fori(1, g.rounds) as i:
                for t in range(2):
                    for c in range(NCH):
                        gate(i, t, c)
                        g.wait_pair(act, i, 6 * t - 2, 1)
                        taps(i * 2 + (t - 1), *SPLIT[c])
            g.wait_all_read(act)
            n = KD - 1
            for r in range(NLAST):
                q = CW - NLAST + r
                src, w = glu[:, n, q:q + T], vec[:, n, V_WDW + q:V_WDW + q + 1]
                if r == 0:
                    act.wait_ge(tile_conv, n)
                    act.activation(wacc, src, ACT.Copy, scale=w).then_inc(tap_in, 1)
                else:
                    act.wait_ge(tap_added, n * (NPOOL - 1) + r)
                    act.activation(wprod[:, (r - 1) % 2, :], src, ACT.Copy, scale=w).then_inc(tap_in, 1)
            act.wait_ge(crow_full, 1)
            act.wait_ge(tap_added, 2 + (KD - 1) * (NPOOL - 1) + NLAST - 1)
            act.wait_ge(tile_conv, KD)
            for u in range(2):
                act.activation(crow[:, 512 * u:512 * (u + 1)], bank[0:HIST + B, u, :], ACT.Copy).then_inc(crow_copied, 1)
            for c in range(NCH):
                act.wait_ge(mu_full, c + 1)
                act.activation(rstd[:, c, :], bank[:, 2 + c, 0:CH], ACT.Copy, scale=1.0 / D).then_inc(mu_in, 1)
            act.wait_ge(centred, NCH * KD)
            norm_act(act, 3, cout, LN_EPS)
            for c in range(NCH):
                for k in range(KD):
                    act.wait_ge(n_out, KD * (3 * 3 + c) + k + 1)
                    act.activation(cout[:, k, chunk(c)], cout[:, k, chunk(c)], ACT.Silu, bias=vcol(V_LB, k)).then_inc(ln_silu, 1)

        SPLIT = [(0, 4), (4, 8), (8, NPOOL)]

        def taps_first(act, q0, q1):
            for q in range(q0, q1):
                src, w = glu[:, 0, TAPS + q:TAPS + q + T], vec[:, 0, V_WDW + TAPS + q:V_WDW + TAPS + q + 1]
                if q == 0:
                    act.activation(wacc, src, ACT.Copy, scale=w).then_inc(tap_in, 1)
                else:
                    act.wait_ge(tap_added, q)
                    act.activation(wprod[:, (q - 1) % 2, :], src, ACT.Copy, scale=w).then_inc(tap_in, 1)

        def conf_dve(dve, step):
            f0.down.wait_all_read(dve)
            norm_dve(dve, 2, x, xn, V_MIX1)
            dve.memset(glu[:, :, 0:HIST], 0.0).then_inc(hist_zero, 1)
            dve.wait_ge(hist_copied, 4)
            wd = vec[:, :, V_WDW:V_WDW + HIST].unsqueeze(2).to_broadcast([P, KD, B, HIST])
            step(dve.tensor_tensor(shist, shist, wd, ALU.mult))
            step(dve.tensor_reduce(ssum8, shist, AX.X, ALU.add))
            g = g_pw1
            g.grant(dve, [1])

            def glu_job(i, t, c):
                g.wait_full(dve, i, 6 * t + 2 * c + 1)
                g.wait_pair(dve, i, 6 * t + 2 * c, 0)
                dve.scalar_tensor_tensor(big[:, ds(i * (2 * GL) + (t * GL + HIST + c * CH), CH)], bank[:, 2 * c + 1, 0:CH],
                                         vecf[:, ds(i * (2 * NV) + (t * NV + V_BA), 1)], tmp[:, c, :], ALU.add, ALU.mult).then_inc(g.free[1], 1)

            def conv(n, q0, q1):
                for q in range(q0, min(q1, TAPS)):
                    w = vecf[:, ds(n * NV + (V_WDW + q), 1)]
                    for v in range(2):
                        d = big[:, ds(n * TT + (KD * GL + v * T // 2), T // 2)]
                        src = big[:, ds(n * GL + (q + v * T // 2), T // 2)]
                        if q == 0:
                            step.lagged(dve.tensor_scalar(d, src, w, vecf[:, ds(n * NV + V_BDW, 1)], ALU.mult, ALU.add))
                        else:
                            step.lagged(dve.scalar_tensor_tensor(d, src, w, d, ALU.mult, ALU.add))
                if q1 > TAPS:
                    d = big[:, ds(n * TT + KD * GL, T)]
                    step.settle()
                    dve.wait_ge(tap_added, n * (NPOOL - 1) + (NPOOL - 1 + 2))
                    dve.tensor_tensor(d, d, wacc, ALU.add).then_inc(tile_conv, 1)

            PARTS = [(0, TAPS // 3), (TAPS // 3, 2 * TAPS // 3), (2 * TAPS // 3, TAPS + 1)]
            dve.wait_ge(hist_zero, 1)
            for t in range(2):
                for c in range(NCH):
                    glu_job(0, t, c)
                    if t == 1:
                        if c == 0:
                            g.wait_pair(dve, 0, 4, 1)
                        conv(0, *PARTS[c])
            with dve.Fori(1, g.rounds) as i:
                step.enter(i - 1, 4 * TAPS)
                for t in range(2):
                    for c in range(NCH):
                        glu_job(i, t, c)
                        if c == 0:
                            g.wait_pair(dve, i, 6 * t - 2, 1)
                        conv(i * 2 + (t - 1), *PARTS[c])
            step.leave(g.rounds - 1)
            g.wait_all_read(dve)
            snew_ = glu[:, :, HIST + T:GL]
            wl = vec[:, :, V_WDW + HIST].unsqueeze(2).to_broadcast([P, KD, B])
            cs = cout[:, :, T:TT]
            step(dve.tensor_tensor(cs, snew_, wl, ALU.mult))
            step(dve.tensor_tensor(cs, cs, ssum8, ALU.add))
            dve.tensor_tensor(cs, cs, vec[:, :, V_BDW].unsqueeze(2).to_broadcast([P, KD, B]), ALU.add).then_inc(samples_conv, 1)
            n = KD - 1
            d = cout[:, n, 0:T]
            for q in range(NDIAG, CW - NLAST):
                w = vec[:, n, V_WDW + q:V_WDW + q + 1]
                for v in range(2):
                    dv, src = cout[:, n, v * T // 2:(v + 1) * T // 2], glu[:, n, q + v * T // 2:q + (v + 1) * T // 2]
                    if q == NDIAG:
                        step.lagged(dve.tensor_scalar(dv, src, w, vec[:, n, V_BDW:V_BDW + 1], ALU.mult, ALU.add))
                    else:
                        step.lagged(dve.scalar_tensor_tensor(dv, src, w, dv, ALU.mult, ALU.add))
            step.settle()
            dve.wait_ge(diag_full, 1)
            step(dve.tensor_tensor(d.rearrange("p (v t) -> p v t", v=2), d.rearrange("p (v t) -> p v t", v=2), bank[:, 5:7, :], ALU.add))
            dve.wait_ge(tap_added, n * (NPOOL - 1) + (NLAST - 1 + 2))
            dve.tensor_tensor(d, d, wacc, ALU.add).then_inc(tile_conv, 1)
            for c in range(NCH):
                dve.wait_ge(mu_in, c + 1)
                for k in range(KD):
                    dve.tensor_tensor(cout[:, k, chunk(c)], cout[:, k, chunk(c)], rstd[:, c, :], ALU.subtract).then_inc(centred, 1)
            dve.wait_ge(centred, NCH * KD)
            norm_dve(dve, 3, cout, cout, V_LG)
            add_out(dve, g_pw2, four_tiles, V_BPW2)

        y_full, y_copied = sem("y_full"), [sem("y_copied0"), sem("y_copied1")]
        y_out = [sem("y_out0"), sem("y_out1")]
        yrow = flat(0, 2, D)

        def final_pe(pe):
            norm_pe(pe, 5)
            for n in range(NB + 1):
                pe.wait_ge(n_out, KD * (3 * 5) + KD * min(NCH, 1 + min(TT - 1, (n + 1) * P - 1) // CH))
                if n >= 2:
                    for e in range(2):
                        pe.wait_ge(y_copied[e], n - 1)
                w = P if n < NB else B
                for k in range(KD):
                    mm = pe.transpose(bank[0:w, 2 * (n % 2) + k // 4, k % 4 * P:(k % 4 + 1) * P], xn[:, k, n * P:n * P + w], ident[:, :])
                mm.then_inc(y_full, 1)

        def final_copy(eng, e):
            for n in range(NB + 1):
                w = P if n < NB else B
                eng.wait_ge(y_full, n + 1)
                if n >= 2:
                    eng.wait_ge(y_out[n % 2], 16 * (n // 2))
                s, d = bank[0:w, 2 * (n % 2) + e, :], yrow[0:w, n % 2, 512 * e:512 * (e + 1)]
                if e == 0:
                    eng.activation(d, s, ACT.Copy).then_inc(y_copied[e], 1)
                else:
                    eng.tensor_copy(d, s).then_inc(y_copied[e], 1)

        def final_sp(sp):
            yp = o["y_prompt"].rearrange("o (n p) d -> (o n) p d", p=P)
            for n in range(NB + 1):
                for e in range(2):
                    sp.wait_ge(y_copied[e], n + 1)
                if n < NB:
                    sp.dma_start(yp[n], yrow[:, n % 2, :]).then_inc(y_out[n % 2], 16)
                else:
                    sp.dma_start(o["y_sample"].rearrange("b o d -> (b o) d"), yrow[0:B, n % 2, :]).then_inc(y_out[n % 2], 16)
            sp.wait_ge(y_out[0], 16 * (NB // 2 + 1))
            sp.wait_ge(y_out[1], 16 * (NB // 2))

        def pe_rest(pe):
            kv_pe(pe)
            att_pe(pe)
            gdn_in_pe(pe)
            sm_pe(pe)
            l2_pe(pe)
            gate_pe(pe)
            chunk_pe(pe)
            sample_pe(pe)
            onorm_pe(pe)
            out_pe(pe)
            ffn_pe(pe, f0)
            conf_pe(pe)
            ffn_pe(pe, f1)
            final_pe(pe)

        def act_rest(act):
            kv_act(act)
            att_act(act)
            gdn_in_act(act)
            l2_squares(act)
            sm_act(act)
            l2_act(act)
            gate_act_fn(act)
            chunk_act(act)
            sample_act(act)
            onorm_act(act)
            ffn_act(act, f0, g_out)
            conf_act(act)
            ffn_act(act, f1, g_pw2)
            f1.down.wait_all_read(act)
            norm_act(act, 5, x)
            final_copy(act, 0)

        def dve_rest(dve, step):
            kv_dve(dve)
            att_dve(dve, step)
            gdn_in_dve(dve, step)
            sm_dve(dve, step)
            l2_dve(dve)
            gate_dve(dve, step)
            chunk_dve(dve, step)
            sample_dve(dve, step)
            onorm_dve(dve)
            out_dve(dve)
            ffn_dve(dve, f0, g_out, step)
            conf_dve(dve, step)
            ffn_dve(dve, f1, g_pw2, step)
            f1.down.wait_all_read(dve)
            norm_dve(dve, 5, x, xn, V_FIN)
            final_copy(dve, 1)

        def sp_rest(sp):
            kv_sp(sp)
            gdn_in_sp(sp)
            chunk_sp(sp)
            stream(sp, g_out, lambda i, s: cols(w_out0, i * 4 + s), g_gdn)
            ffn_sp(sp, f0, g_out)
            stream(sp, g_pw1, lambda i, s: cols(w_pw1, i * 2 + (s // 2 + KD * (1 - s % 2))), f0.down)
            stream(sp, g_pw2, lambda i, s: cols(w_pw2, i * 4 + s), g_pw1)
            ffn_sp(sp, f1, g_pw2)
            final_sp(sp)

        def pool_rest(pool, step):
            att_pool(pool)
            pool.wait_ge(v_out, 16 * NB)
            gdn_in_pool(pool)
            pool.sem_inc(qdec_done, 1)
            chunk_pool(pool)
            sample_pool(pool)
            ffn_pool(pool, f0)
            conf_pool(pool, step)
            ffn_pool(pool, f1)
            pool.wait_ge(misc_out, 16 * STORES)

        @blk.sync
        def _(sp):
            sp_part1(sp)
            sp_rest(sp)

        @blk.tensor
        def _(pe):
            pe_part1(pe)
            pe_rest(pe)

        @blk.scalar
        def _(act):
            act_part1(act)
            act_rest(act)

        @blk.vector
        def _(dve):
            step = Chain(dve, dve_step)
            dve_part1(dve, step)
            dve_rest(dve, step)

        @blk.gpsimd
        def _(pool):
            step = Chain(pool, pool_step)
            pool_part1(pool, step)
            pool_rest(pool, step)


INS = ["x_prompt", "x_sample", "cache_attn_k", "cache_attn_v", "page_table", "state_gdn_conv", "state_gdn_s",
       "state_conv_buf", "norm_mix", "norm_ffn", "norm_final", "w_in", "w_out", "gdn_conv_w", "gdn_A_log",
       "gdn_dt_bias", "gdn_norm_w", "lam_q1", "lam_k1", "lam_q2", "lam_k2", "diff_subln_w", "rel_bias",
       "conv_w_pw1", "conv_b_pw1", "conv_w_dw", "conv_b_dw", "conv_ln_g", "conv_ln_b", "conv_w_pw2",
       "conv_b_pw2", "ffn_w_gate", "ffn_w_up", "ffn_w_down"]
OUTS = [("y_prompt", (1, T, D)), ("y_sample", (B, 1, D)), ("new_k_prompt", (1, 1, T, H, P)), ("new_v_prompt", (1, 1, T, H, P)),
        ("new_k_sample", (1, B, 1, H, P)), ("new_v_sample", (1, B, 1, H, P)), ("new_gdn_conv_prompt", (1, 1, GW - 1, CQ)),
        ("new_gdn_conv_sample", (1, B, GW - 1, CQ)), ("new_gdn_s_prompt", (1, 1, H, P, P)), ("new_gdn_s_sample", (1, B, H, P, P)),
        ("new_conv_buf_prompt", (1, 1, CW - 1, D)), ("new_conv_buf_sample", (1, B, CW - 1, D))]


def kernel(**inputs):
    import concourse.bacc as bacc
    from concourse.bass_utils import run_bass_kernel_spmd
    nc = bacc.Bacc("TRN2", target_bir_lowering=False, num_devices=1)
    arrays, a = {}, {}
    for name, v in {**{n: inputs[n] for n in INS}, **shape_constants()}.items():
        v = np.ascontiguousarray(v)
        arrays[f"in_{name}"] = v
        a[name] = nc.dram_tensor(f"in_{name}", v.shape, mybir.dt.from_np(v.dtype), kind="ExternalInput").ap()
    o = {name: nc.dram_tensor(f"out_{name}", shape, F32, kind="ExternalOutput").ap() for name, shape in OUTS}
    build(nc, a, o)
    r = run_bass_kernel_spmd(nc, [arrays], core_ids=[0])
    return tuple(r.results[0][f"out_{name}"] for name, _ in OUTS)
```
